# Optimizing a Trainium2 kernel written in Bass

```python
import jax, jax.numpy as jnp
from jax import lax
import numpy as np
import math

D_MODEL = 1024
BATCH = 1
SEQ = 256
DEPTH = 1

HG_HEADS = 8
HG_KEY_DIM = 128
HG_VAL_DIM = D_MODEL // HG_HEADS
HG_KEY = HG_HEADS * HG_KEY_DIM
HG_VAL = HG_HEADS * HG_VAL_DIM
HG_CHUNK = 64
SG_GROUPS = 8
SG_GROUP_DIM = 64
SG_WIDTH = SG_GROUPS * SG_GROUP_DIM
SG_CHUNK = 128
FFN_HIDDEN = ((8 * D_MODEL // 3 + 255) // 256) * 256
PLE_DIM = 256
EPS = 1e-6
IN_SPLITS = (HG_KEY, HG_KEY, HG_KEY, HG_VAL, HG_VAL, SG_WIDTH, SG_WIDTH, D_MODEL, D_MODEL)
N_IN = HG_KEY * 3 + HG_VAL * 2 + SG_WIDTH * 2 + D_MODEL * 2


def rms_norm(x, g):
    xf = x.astype(jnp.float32)
    y = xf * lax.rsqrt(jnp.mean(xf * xf, axis=-1, keepdims=True) + EPS)
    return (y * g.astype(jnp.float32)).astype(x.dtype)

def layer_norm(x, g, b):
    xf = x.astype(jnp.float32)
    mu = jnp.mean(xf, axis=-1, keepdims=True)
    xc = xf - mu
    y = xc * lax.rsqrt(jnp.mean(xc * xc, axis=-1, keepdims=True) + EPS)
    return (y * g.astype(jnp.float32) + b.astype(jnp.float32)).astype(x.dtype)

def layer_lower_bounds(gamma):
    sm = jax.nn.softmax(gamma.astype(jnp.float32), axis=0)
    return jnp.cumsum(sm, axis=0) - sm[0:1]

def _to_chunks(t):
    b, s, h, d = t.shape
    return t.reshape(b, s // HG_CHUNK, HG_CHUNK, h, d).transpose(1, 0, 3, 2, 4)

def hgrn2_direction(q, k, v, logf):
    bsz, s, h, dk = q.shape
    dv = v.shape[-1]
    mask = jnp.tril(jnp.ones((HG_CHUNK, HG_CHUNK), dtype=jnp.float32))

    def step(state, inp):
        qc, kc, vc, gc = inp
        b = jnp.cumsum(gc, axis=2)
        o_inter = jnp.einsum('bhtk,bhkv->bhtv', qc * jnp.exp(b), state)
        diff = b[:, :, :, None, :] - b[:, :, None, :, :]
        decay = jnp.exp(jnp.minimum(diff, 0.0)) * mask[:, :, None]
        scores = jnp.einsum('bhtk,bhsk,bhtsk->bhts', qc, kc, decay)
        o_intra = jnp.einsum('bhts,bhsv->bhtv', scores, vc)
        b_last = b[:, :, -1:, :]
        new_state = (jnp.exp(b_last[:, :, 0, :])[..., None] * state
                     + jnp.einsum('bhsk,bhsv->bhkv', kc * jnp.exp(b_last - b), vc))
        return new_state, o_inter + o_intra

    init = jnp.zeros((bsz, h, dk, dv), jnp.float32)
    _, o = lax.scan(step, init, (_to_chunks(q), _to_chunks(k), _to_chunks(v), _to_chunks(logf)))
    return o.transpose(1, 0, 3, 2, 4).reshape(bsz, s, h, dv)

def hgrn2_mixer(zq, zf_fwd, zf_bwd, zi, zg, lb_f, lb_b, norm_g):
    bsz, s, _ = zq.shape
    f32 = jnp.float32
    tiny = jnp.finfo(f32).tiny
    q = jax.nn.silu(zq.astype(f32)).reshape(bsz, s, HG_HEADS, HG_KEY_DIM)
    v = zi.astype(f32).reshape(bsz, s, HG_HEADS, HG_VAL_DIM)

    def gates(zf, lb):
        zf = zf.astype(f32)
        f = lb + (1.0 - lb) * jax.nn.sigmoid(zf)
        logf = jnp.log(jnp.maximum(f, tiny))
        k = (1.0 - lb) * jax.nn.sigmoid(-zf)
        return (k.reshape(bsz, s, HG_HEADS, HG_KEY_DIM), logf.reshape(bsz, s, HG_HEADS, HG_KEY_DIM))

    k_f, logf_f = gates(zf_fwd, lb_f)
    k_b, logf_b = gates(zf_bwd, lb_b)
    o_fwd = hgrn2_direction(q, k_f, v, logf_f)
    o_bwd = hgrn2_direction(q[:, ::-1], k_b[:, ::-1], v[:, ::-1], logf_b[:, ::-1])[:, ::-1]
    o = o_fwd + o_bwd
    o = rms_norm(o, norm_g.reshape(HG_HEADS, HG_VAL_DIM)).reshape(bsz, s, HG_VAL)
    return (o * jax.nn.silu(zg.astype(f32))).astype(zq.dtype)

def spatial_gating(zu, zv, w_s, b_s, ln_g, ln_b):
    bsz, s, _ = zu.shape
    u = jax.nn.gelu(zu, approximate=False)
    v = layer_norm(jax.nn.gelu(zv, approximate=False), ln_g, ln_b)
    vr = v.reshape(bsz, s // SG_CHUNK, SG_CHUNK, SG_GROUPS, SG_GROUP_DIM)
    sg = jnp.einsum('gts,bcsge->bctge', w_s, vr) + b_s.T[None, None, :, :, None]
    return u * sg.reshape(bsz, s, SG_WIDTH)

def first_inputs(seed: int = 0) -> dict:
    key = jax.random.key(seed)
    ks = jax.random.split(key, 24)
    f32 = jnp.float32

    def nrm(k, shape, scale):
        return jax.random.normal(k, shape, f32) * scale

    def gain(k, shape):
        return 1.0 + 0.05 * jax.random.normal(k, shape, f32)

    return {
        "x": nrm(ks[0], (BATCH, SEQ, D_MODEL), 1.0),
        "p": nrm(ks[1], (DEPTH, BATCH, SEQ, PLE_DIM), 1.0),
        "norm_mix_pre": gain(ks[2], (DEPTH, D_MODEL)),
        "w_in": nrm(ks[3], (DEPTH, D_MODEL, N_IN), D_MODEL ** -0.5),
        "lb_gamma_fwd": nrm(ks[4], (DEPTH, HG_KEY), 0.1),
        "lb_gamma_bwd": nrm(ks[5], (DEPTH, HG_KEY), 0.1),
        "hg_norm": gain(ks[6], (DEPTH, HG_VAL)),
        "sg_w": nrm(ks[7], (DEPTH, SG_GROUPS, SG_CHUNK, SG_CHUNK), SG_CHUNK ** -0.5),
        "sg_b": gain(ks[8], (DEPTH, SG_GROUPS, SG_CHUNK)),
        "sg_ln_g": gain(ks[9], (DEPTH, SG_WIDTH)),
        "sg_ln_b": nrm(ks[10], (DEPTH, SG_WIDTH), 0.02),
        "w_a": nrm(ks[11], (DEPTH, HG_VAL, D_MODEL), HG_VAL ** -0.5),
        "w_b": nrm(ks[12], (DEPTH, SG_WIDTH, D_MODEL), SG_WIDTH ** -0.5),
        "w_out": nrm(ks[13], (DEPTH, D_MODEL, D_MODEL), D_MODEL ** -0.5),
        "norm_mix_post": gain(ks[14], (DEPTH, D_MODEL)),
        "norm_ffn_pre": gain(ks[15], (DEPTH, D_MODEL)),
        "w_gate": nrm(ks[16], (DEPTH, D_MODEL, FFN_HIDDEN), D_MODEL ** -0.5),
        "w_up": nrm(ks[17], (DEPTH, D_MODEL, FFN_HIDDEN), D_MODEL ** -0.5),
        "w_down": nrm(ks[18], (DEPTH, FFN_HIDDEN, D_MODEL), FFN_HIDDEN ** -0.5),
        "norm_ffn_post": gain(ks[19], (DEPTH, D_MODEL)),
        "w_ple": nrm(ks[20], (DEPTH, PLE_DIM, D_MODEL), PLE_DIM ** -0.5),
        "w_ple_gate": nrm(ks[21], (DEPTH, D_MODEL, D_MODEL), D_MODEL ** -0.5),
    }

def first_block(x, p, norm_mix_pre, w_in, lb_gamma_fwd, lb_gamma_bwd, hg_norm, sg_w, sg_b,
              sg_ln_g, sg_ln_b, w_a, w_b, w_out, norm_mix_post, norm_ffn_pre, w_gate, w_up,
              w_down, norm_ffn_post, w_ple, w_ple_gate):
    lb_fwd_all = layer_lower_bounds(lb_gamma_fwd)
    lb_bwd_all = layer_lower_bounds(lb_gamma_bwd)
    offsets = [int(o) for o in np.cumsum(IN_SPLITS)[:-1]]
    for l in range(DEPTH):
        h = rms_norm(x, norm_mix_pre[l])
        z = jnp.einsum('bsd,dn->bsn', h, w_in[l])
        zq, zf_f, zf_b, zi, zg, zu, zv, ga, gb = jnp.split(z, offsets, axis=-1)
        a_out = hgrn2_mixer(zq, zf_f, zf_b, zi, zg, lb_fwd_all[l], lb_bwd_all[l], hg_norm[l])
        b_out = spatial_gating(zu, zv, sg_w[l], sg_b[l], sg_ln_g[l], sg_ln_b[l])
        merged = (jax.nn.sigmoid(ga) * jnp.einsum('bsv,vd->bsd', a_out, w_a[l])
                  + jax.nn.sigmoid(gb) * jnp.einsum('bsw,wd->bsd', b_out, w_b[l]))
        mix = jnp.einsum('bsd,de->bse', merged, w_out[l])
        x = x + rms_norm(mix, norm_mix_post[l])
        h2 = rms_norm(x, norm_ffn_pre[l])
        ff = jnp.einsum('bsf,fd->bsd',
                        jax.nn.silu(jnp.einsum('bsd,df->bsf', h2, w_gate[l]))
                        * jnp.einsum('bsd,df->bsf', h2, w_up[l]), w_down[l])
        x = x + rms_norm(ff, norm_ffn_post[l])
        x = x + (jnp.einsum('bse,ed->bsd', p[l], w_ple[l])
                 * jax.nn.sigmoid(jnp.einsum('bsd,de->bse', x, w_ple_gate[l])))
    return x


HEAD_DIM_A = 64
N_HEADS_A = 8
WIDTH_A = N_HEADS_A * HEAD_DIM_A
DILATED_BRANCHES = ((128, 1), (512, 4), (2048, 16))

N_HEADS_B = 8
QK_NOPE_DIM = 64
QK_ROPE_DIM = 32
V_HEAD_DIM = 64
QK_HEAD_DIM_B = QK_NOPE_DIM + QK_ROPE_DIM
Q_LORA_RANK = 768
KV_LORA_RANK = 256
WIDTH_B = N_HEADS_B * V_HEAD_DIM
ROPE_THETA = 10000.0

MIX_WIDTH = WIDTH_A + WIDTH_B
D_FF = 4 * D_MODEL

REL_BUCKETS = 32
REL_MAX_DIST = 2048
Q_BLOCK = 128

IN_SPLITS_2 = (WIDTH_A, WIDTH_A, WIDTH_A, Q_LORA_RANK, KV_LORA_RANK, QK_ROPE_DIM)
IN_WIDTH = sum(IN_SPLITS_2)


def rms_norm_2(x, g):
    xf = x.astype(jnp.float32)
    y = xf * lax.rsqrt(jnp.mean(xf * xf, axis=-1, keepdims=True) + EPS)
    return (y * g.astype(jnp.float32)).astype(x.dtype)

def t5_causal_bucket(dist):
    dist = np.asarray(dist, dtype=np.int64)
    max_exact = REL_BUCKETS // 2
    safe = np.maximum(dist, 1).astype(np.float32)
    large = max_exact + (np.log(safe / max_exact) / math.log(REL_MAX_DIST / max_exact)
                         * (REL_BUCKETS - max_exact)).astype(np.int64)
    large = np.minimum(large, REL_BUCKETS - 1)
    return np.where(dist < max_exact, dist, large).astype(np.int32)

def apply_rope(x, positions):
    r = x.shape[-1]
    inv_freq = 1.0 / (ROPE_THETA ** (jnp.arange(0, r, 2, dtype=jnp.float32) / r))
    ang = positions.astype(jnp.float32)[..., None] * inv_freq
    cos = jnp.cos(ang)[:, :, None, :]
    sin = jnp.sin(ang)[:, :, None, :]
    xf = x.astype(jnp.float32)
    x1, x2 = xf[..., : r // 2], xf[..., r // 2:]
    out = jnp.concatenate([x1 * cos - x2 * sin, x2 * cos + x1 * sin], axis=-1)
    return out.astype(x.dtype)

def to_query_blocks(t):
    b, s = t.shape[:2]
    nblk = s // Q_BLOCK
    return jnp.moveaxis(t.reshape((b, nblk, Q_BLOCK) + t.shape[2:]), 1, 0)

def from_query_blocks(t):
    t = jnp.moveaxis(t, 0, 1)
    return t.reshape((t.shape[0], t.shape[1] * t.shape[2]) + t.shape[3:])

def dilated_attention(q, k, v, rel_bias):
    b, s, h, dh = q.shape
    scale = 1.0 / math.sqrt(dh)
    branches = []
    for window, dil in DILATED_BRANCHES:
        offs_np = dil * np.arange(window // dil + 1, dtype=np.int32)
        bias = rel_bias[jnp.asarray(t5_causal_bucket(offs_np))].T.astype(jnp.float32)
        branches.append((jnp.asarray(offs_np), bias))
    nblk = s // Q_BLOCK

    def block_fn(args):
        i, qi = args
        tq = i * Q_BLOCK + jnp.arange(Q_BLOCK, dtype=jnp.int32)
        ms, ss, os_ = [], [], []
        for offs, bias in branches:
            idx = tq[:, None] - offs[None, :]
            valid = idx >= 0
            idxc = jnp.maximum(idx, 0)
            kg = k[:, idxc]
            vg = v[:, idxc]
            logits = jnp.einsum('bqhd,bqkhd->bhqk', qi, kg).astype(jnp.float32) * scale
            logits = logits + bias[None, :, None, :]
            logits = jnp.where(valid[None, None], logits, -jnp.inf)
            m = jnp.max(logits, axis=-1, keepdims=True)
            p = jnp.exp(logits - m)
            den = jnp.sum(p, axis=-1, keepdims=True)
            o = jnp.einsum('bhqk,bqkhd->bhqd', p, vg.astype(jnp.float32)) / den
            ms.append(m); ss.append(den); os_.append(o)
        m_all = jnp.stack(ms)
        w = jnp.stack(ss) * jnp.exp(m_all - jnp.max(m_all, axis=0, keepdims=True))
        out = jnp.sum(w * jnp.stack(os_), axis=0) / jnp.sum(w, axis=0)
        return jnp.transpose(out, (0, 2, 1, 3)).astype(q.dtype)

    out = lax.map(block_fn, (jnp.arange(nblk, dtype=jnp.int32), to_query_blocks(q)))
    return from_query_blocks(out)

def causal_block_attention(q, k, v):
    b, s, h, dqk = q.shape
    scale = 1.0 / math.sqrt(dqk)
    kpos = jnp.arange(s, dtype=jnp.int32)
    nblk = s // Q_BLOCK

    def block_fn(args):
        i, qi = args
        tq = i * Q_BLOCK + jnp.arange(Q_BLOCK, dtype=jnp.int32)
        logits = jnp.einsum('bqhd,bkhd->bhqk', qi, k).astype(jnp.float32) * scale
        logits = jnp.where((kpos[None, :] <= tq[:, None])[None, None], logits, -jnp.inf)
        p = jax.nn.softmax(logits, axis=-1)
        out = jnp.einsum('bhqk,bkhd->bqhd', p, v.astype(jnp.float32))
        return out.astype(q.dtype)

    out = lax.map(block_fn, (jnp.arange(nblk, dtype=jnp.int32), to_query_blocks(q)))
    return from_query_blocks(out)

def second_inputs(seed: int = 0) -> dict:
    key = jax.random.key(seed)
    ks = jax.random.split(key, 20)
    f32 = jnp.float32

    def nrm(k, shape, fan_in):
        return jax.random.normal(k, shape, f32) * (fan_in ** -0.5)

    def gain(k, n):
        return 1.0 + 0.05 * jax.random.normal(k, (n,), f32)

    x = jax.random.normal(ks[0], (BATCH, SEQ, D_MODEL), f32)
    offset = jax.random.randint(ks[1], (BATCH, 1), 0, 1024, dtype=jnp.int32)
    positions = jnp.arange(SEQ, dtype=jnp.int32)[None, :] + offset
    return {
        "x": x,
        "positions": positions,
        "norm_mix_g": gain(ks[2], D_MODEL),
        "w_in": nrm(ks[3], (D_MODEL, IN_WIDTH), D_MODEL),
        "qnorm_a_g": gain(ks[4], HEAD_DIM_A),
        "knorm_a_g": gain(ks[5], HEAD_DIM_A),
        "rel_bias": 0.5 * jax.random.normal(ks[6], (REL_BUCKETS, N_HEADS_A), f32),
        "cq_norm_g": gain(ks[7], Q_LORA_RANK),
        "ckv_norm_g": gain(ks[8], KV_LORA_RANK),
        "w_uq": nrm(ks[9], (Q_LORA_RANK, N_HEADS_B * QK_HEAD_DIM_B), Q_LORA_RANK),
        "w_ukv": nrm(ks[10], (KV_LORA_RANK, N_HEADS_B * (QK_NOPE_DIM + V_HEAD_DIM)), KV_LORA_RANK),
        "qnorm_b_g": gain(ks[11], QK_HEAD_DIM_B),
        "knorm_b_g": gain(ks[12], QK_HEAD_DIM_B),
        "w_o": nrm(ks[13], (MIX_WIDTH, D_MODEL), MIX_WIDTH),
        "norm_ffn_g": gain(ks[14], D_MODEL),
        "w_ff1": nrm(ks[15], (D_MODEL, D_FF), D_MODEL),
        "w_ff2": nrm(ks[16], (D_FF, D_MODEL), D_FF),
    }

def second_block(x, positions, norm_mix_g, w_in, qnorm_a_g, knorm_a_g, rel_bias,
              cq_norm_g, ckv_norm_g, w_uq, w_ukv, qnorm_b_g, knorm_b_g, w_o,
              norm_ffn_g, w_ff1, w_ff2):
    b, s, _ = x.shape
    h = x
    for _layer in range(DEPTH):
        xn = rms_norm_2(h, norm_mix_g)
        proj = jnp.einsum('bsd,de->bse', xn, w_in)
        cuts = list(np.cumsum(IN_SPLITS_2)[:-1])
        qa, ka, va, c_q, c_kv, k_rope = jnp.split(proj, cuts, axis=-1)

        qa = rms_norm_2(qa.reshape(b, s, N_HEADS_A, HEAD_DIM_A), qnorm_a_g)
        ka = rms_norm_2(ka.reshape(b, s, N_HEADS_A, HEAD_DIM_A), knorm_a_g)
        va = va.reshape(b, s, N_HEADS_A, HEAD_DIM_A)
        out_a = dilated_attention(qa, ka, va, rel_bias).reshape(b, s, WIDTH_A)

        qb = jnp.einsum('bsr,re->bse', rms_norm_2(c_q, cq_norm_g), w_uq)
        qb = qb.reshape(b, s, N_HEADS_B, QK_HEAD_DIM_B)
        kv = jnp.einsum('bsr,re->bse', rms_norm_2(c_kv, ckv_norm_g), w_ukv)
        kv = kv.reshape(b, s, N_HEADS_B, QK_NOPE_DIM + V_HEAD_DIM)
        k_nope, vb = kv[..., :QK_NOPE_DIM], kv[..., QK_NOPE_DIM:]
        k_rope_h = jnp.broadcast_to(k_rope[:, :, None, :], (b, s, N_HEADS_B, QK_ROPE_DIM))
        kb = jnp.concatenate([k_nope, k_rope_h], axis=-1)
        qb = rms_norm_2(qb, qnorm_b_g)
        kb = rms_norm_2(kb, knorm_b_g)
        qb = jnp.concatenate([qb[..., :QK_NOPE_DIM],
                              apply_rope(qb[..., QK_NOPE_DIM:], positions)], axis=-1)
        kb = jnp.concatenate([kb[..., :QK_NOPE_DIM],
                              apply_rope(kb[..., QK_NOPE_DIM:], positions)], axis=-1)
        out_b = causal_block_attention(qb, kb, vb).reshape(b, s, WIDTH_B)

        mixed = jnp.concatenate([out_a, out_b], axis=-1)
        h = h + jnp.einsum('bse,ed->bsd', mixed, w_o)

        hn = rms_norm_2(h, norm_ffn_g)
        hid = jnp.square(jax.nn.relu(jnp.einsum('bsd,df->bsf', hn, w_ff1)))
        h = h + jnp.einsum('bsf,fd->bsd', hid, w_ff2)
    return h


def setup_inputs(seed=0):
    out = dict(first_inputs(seed))
    for name, value in second_inputs(seed + 1).items():
        if name != "x":
            out[name + "_2"] = value
    return out


def reference(
    x, p, norm_mix_pre, w_in, lb_gamma_fwd, lb_gamma_bwd, hg_norm, sg_w, sg_b, sg_ln_g, sg_ln_b,
    w_a, w_b, w_out, norm_mix_post, norm_ffn_pre, w_gate, w_up, w_down, norm_ffn_post, w_ple,
    w_ple_gate, positions_2, norm_mix_g_2, w_in_2, qnorm_a_g_2, knorm_a_g_2, rel_bias_2,
    cq_norm_g_2, ckv_norm_g_2, w_uq_2, w_ukv_2, qnorm_b_g_2, knorm_b_g_2, w_o_2, norm_ffn_g_2,
    w_ff1_2, w_ff2_2,
):
    x = first_block(
        x, p, norm_mix_pre, w_in, lb_gamma_fwd, lb_gamma_bwd, hg_norm, sg_w, sg_b, sg_ln_g,
        sg_ln_b, w_a, w_b, w_out, norm_mix_post, norm_ffn_pre, w_gate, w_up, w_down,
        norm_ffn_post, w_ple, w_ple_gate,
    )
    return second_block(
        x, positions_2, norm_mix_g_2, w_in_2, qnorm_a_g_2, knorm_a_g_2, rel_bias_2, cq_norm_g_2,
        ckv_norm_g_2, w_uq_2, w_ukv_2, qnorm_b_g_2, knorm_b_g_2, w_o_2, norm_ffn_g_2, w_ff1_2,
        w_ff2_2,
    )


_drawn_inputs = setup_inputs


def setup_inputs(seed=0):
    import zlib

    import numpy as np

    out = dict(_drawn_inputs(seed))
    spreads = {}
    factors = {'sg_ln_b': 5.306,
     'norm_mix_g_2': 5.322,
     'qnorm_a_g_2': 8.0,
     'knorm_a_g_2': 8.0,
     'cq_norm_g_2': 8.0,
     'ckv_norm_g_2': 8.0,
     'qnorm_b_g_2': 8.0,
     'knorm_b_g_2': 8.0,
     'norm_ffn_g_2': 5.669}
    for name, (base, spread) in spreads.items():
        noise = np.random.default_rng([zlib.crc32(name.encode()), seed]).standard_normal(out[name].shape)
        drawn = base * np.exp(spread * noise) if base else spread * noise
        out[name] = __import__('jax').numpy.asarray(drawn.astype(out[name].dtype))
    for name, factor in factors.items():
        out[name] = (out[name] * factor).astype(out[name].dtype)
    return out
```

```python
from contextlib import ExitStack

import numpy as np

import concourse.bass as bass
from concourse import mybir

F32 = mybir.dt.float32
F32R = mybir.dt.float32r
I32 = mybir.dt.int32
ALU = mybir.AluOpType
ACT = mybir.ActivationFunctionType
AX = mybir.AxisListType.X

P = 128
T = 256
D = 1024
DT = D // P
UNIT = 2048
RING = 3
HEADS = 8
FFN = 2816
FFN2 = 4096
EPS = 1e-6
TINY = float(np.finfo(np.float32).tiny)
NEG = -1e30

U_ZV, U_ZU = 0, 2
U_Q = (4, 10)
U_F = ((6, 8), (12, 14))
U_ZI, U_GA, U_ZG, U_GB = 16, 20, 24, 28
U_WA, U_WB, U_WOUT, U_PLE = 32, 36, 38, 42
U_F1 = 43
PAIRS1 = FFN // 256
U_PG = U_F1 + 3 * PAIRS1
U_CQ = U_PG + 4
U_CKV, U_QA, U_KA, U_VA = U_CQ + 3, U_CQ + 4, U_CQ + 6, U_CQ + 8
U_KR, U_UK, U_UQ = U_CQ + 10, U_CQ + 11, U_CQ + 12
U_WO = U_UQ + 3
U_F2 = U_WO + 4
PAIRS2 = FFN2 // 256
UNITS = U_F2 + 2 * PAIRS2

PAR = {}
_at = 0
for _name, _n in (("mix_pre", 8), ("gamma", 16), ("hg_norm", 8), ("mix_post", 8), ("ffn_pre", 8),
                  ("ffn_post", 8), ("mix2", 8), ("cq", 6), ("ckv", 2), ("ffn2", 8), ("qa", 1), ("ka", 1),
                  ("qb", 1), ("kb", 1), ("qb_swap", 1), ("kb_swap", 1)):
    PAR[_name] = _at
    _at += _n
NPAR = _at
C_ID, C_Z64, C_Z96, C_MEAN, C_INVF, C_SIGN = 0, 128, 160, 192, 196, 197
NCST = 198
MEAN_D, MEAN_CQ, MEAN_CKV, MEAN_HEAD = range(4)


def banks_of(u):
    if u in (U_WB, U_WB + 1, U_PLE) or U_UK <= u:
        return ()
    if U_F1 <= u < U_PG:
        r = u - U_F1
        gate = r == 0 or ((r - 2) % 3 == 0 and u != U_PG - 1)
        return (u % RING,) if gate else ()
    if u == U_KR:
        return (0, 1, 2)
    return (u % RING,)


def fill_counts():
    before, count = [], [0] * RING
    for u in range(UNITS):
        before.append(tuple(count))
        for b in banks_of(u):
            count[b] += 1
    return before


FILLS = fill_counts()

SIGNALS = {
    "sq": dict(n1=2, n3=2, n4=4, n5=2, n6=2),
    "st": dict(n1=1, o=1, n2=1, n3=1, n4=1, n5=1, c=2, sa=1, sb=1, n6=1),
    "rx": dict(n1=1, o=1, n2=1, n3=1, n4=1, n5=1, c=2, sa=1, sb=1, n6=1),
    "bc": dict(n1=1, o=4, n2=1, n3=1, n4=1, n5=1, c=2, sa=2, sb=4, n6=1),
    "bcs": dict(n1=1, n2=1, n3=1, n4=1, n5=1, c=2, n6=1),
    "y": dict(n1=8, a=2, m=4, n2=8, n3=8, n4=8, ff=2, n5=8, c=2, n6=8),
    "hi": dict(n1=2, a=2, b=2, m=4, p=1, n3=2, ff=2, n5=2, c=2, n6=2),
    "lo": dict(n1=2, a=2, b=2, m=4, p=1, n3=2, ff=2, n5=2, c=2, n6=2),
}


def before(kind, stage):
    stages = list(SIGNALS[kind])
    return sum(SIGNALS[kind][s] for s in stages[:stages.index(stage)])


def hgrn_schedule():
    steps = {}
    for g, first in enumerate((10, 16)):
        for lv in range(9):
            steps.setdefault(first + lv, []).append(("level", g, lv))
    for g, u in enumerate((20, 25)):
        steps.setdefault(u, []).append(("pv", g, 0))
    return steps


_C1 = np.float32(6.28125)
_C2 = np.float32(int((2 * np.pi - float(_C1)) * 2 ** 21) / 2 ** 21)
TWO_PI = (float(_C1), float(_C2), float(np.float32(2 * np.pi - float(_C1) - float(_C2))))


def build_blocks(nc, w, xT, pT, par, cst, lvl, sgw, sgb, lnr, rel, oneh, maskb, pos, out):
    scratch = nc.dram_tensor("bias_scratch", [HEADS, 512], F32, kind="Internal").ap()
    ctx = ExitStack()
    with ctx:
        def sb(name, shape, dt=F32):
            return ctx.enter_context(nc.sbuf_tensor(name, shape, dt))

        sems = {}

        def sem(name):
            if name not in sems:
                sems[name] = ctx.enter_context(nc.semaphore(name))
            return sems[name]

        raw = sb("raw", [P, RING, UNIT])
        whi = sb("whi", [P, RING, UNIT], F32R)
        wlo = sb("wlo", [P, RING, UNIT], F32R)
        xh = sb("xh", [P, 16, T], F32R)
        xl = sb("xl", [P, 16, T], F32R)
        x = sb("x", [P, DT, T])
        work = sb("work", [P, 88 * T])
        par_s = sb("par_s", [P, NPAR])
        cst_s = sb("cst_s", [P, NCST])
        lvl_s = sb("lvl_s", [P, 7, P], I32)
        lb = sb("lb", [P, 3, 16])
        rx = sb("rx", [P, 2, P])
        bcs = sb("bcs", [P, T])
        nt = sb("nt", [P, 4, 32])
        nti = sb("nti", [P, 32], I32)
        rs = sb("rs", [P, 32])
        smx = sb("smx", [P, 4, 4])
        ps = [ctx.enter_context(nc.psum_tensor(f"ps{b}", [P, 512], F32)) for b in range(8)]

        def view(at, tiles, inner=T):
            return work[:, at * T:(at + tiles) * T].rearrange("p (n t) -> p n t", t=inner)

        def col(name, k=0, a=0, b=P):
            return par_s[a:b, PAR[name] + k:PAR[name] + k + 1]

        def two(ap):
            return ap.rearrange("p (a t) -> p a t", a=2)

        ident = cst_s[:, C_ID:C_ID + P]

        def mean_col(which):
            return cst_s[:, C_MEAN + which:C_MEAN + which + 1]

        sq1, y1 = view(28, 8), view(36, 8)
        zv, zu = view(52, 4, 512), view(48, 4)
        lnr_s = view(44, 4, 512)
        sgw_s, sgb_s = view(64, 4, P), view(68, 2, P)
        vn = view(28, 4, 512)
        bout = view(84, 4)
        G = []
        for g in range(2):
            a = 28 * g
            G.append(dict(q=view(a, 4), Q=(view(a + 4, 4), view(a + 8, 4)),
                          K=(view(a + 12, 4), view(a + 16, 4)), F=(view(a + 20, 4), view(a + 24, 4)),
                          S=work[:, (56 + 8 * g) * T:(64 + 8 * g) * T].rearrange("p (s h t) -> p s h t", s=2, t=T)))
        zi = view(72, 8, D)
        t1 = view(80, 4, 512)
        ga, zg, gb = view(4, 8), view(12, 8), view(20, 8)
        sqo = [view(80, 4), view(52, 4)]
        rxo = view(32, 8, P)
        afull = view(40, 8)
        merged, mtmp = view(48, 8), view(56, 8)
        mix, sq2, tmp2 = view(0, 8), view(8, 8), view(16, 8)
        sq3, y3 = view(24, 8), view(32, 8)
        plx = view(56, 8)
        pT_s = view(80, 2)
        silu = work[:, 72 * T:74 * T]
        hid = [view(74, 2), view(76, 2), view(78, 2)]
        sgate = view(74, 4, 512)
        gtmp = work[:, 78 * T:80 * T]
        bias = view(0, 8)
        qa, ka = view(8, 4), view(12, 4)
        sqA, kxA = view(16, 8), view(16, 4, 512)
        va, vb = view(24, 4, 512), view(28, 4, 512)
        c8, sqc, yc = view(32, 8), view(40, 8), view(64, 8)
        qb, kb, qsw, sqq, sqk = view(48, 8), view(56, 8), view(64, 8), view(72, 8), view(32, 8)
        kxB = view(72, 6, 96)
        probs = work[:, 16 * T:22 * T].rearrange("p (n t) -> p n t", t=384)
        probsT = work[:, 40 * T:46 * T].rearrange("p (n t) -> p n t", t=384)
        cosk, sink, cosq, sinq = (view(80 + i, 1) for i in range(4))
        kr, krs = view(84, 1), view(85, 1)
        ang, red = view(86, 1), view(87, 1)
        maskb_s = view(46, 1)
        oneh_s = view(86, 2, 512)
        bvec = view(80, 2, 512)
        rel_s = view(82, 1)

        block = ctx.enter_context(nc.Block())

        @block.sync
        def _(sp):
            sp.dma_start(x[:, 0:4, :], xT[:, 0:4, :]).then_inc(sem("x_in"), 16)
            sp.dma_start(x[:, 4:8, :], xT[:, 4:8, :]).then_inc(sem("x_in2"), 16)

            def load(u, slot):
                sp.dma_start(raw[:, slot, :], w[u]).then_inc(sem(f"raw_in{slot}"), 16)

            for u in range(RING):
                load(u, u)
            with sp.Fori(1, UNITS // RING) as i:
                for s in range(RING):
                    sp.wait_ge(sem("lo_ready"), i * RING + (s + 1 - RING))
                    sp.dma_start(raw[:, s, :], w[bass.ds(i * RING + s, 1)].rearrange("a p n -> (a p) n")).then_inc(sem(f"raw_in{s}"), 16)
            for u in range(UNITS // RING * RING, UNITS):
                sp.wait_ge(sem("lo_ready"), u + 1 - RING)
                load(u, u % RING)
            for b in range(4):
                sp.wait_ge(sem("out_ready"), b + 1)
                sp.dma_start(out[:, 2 * b:2 * b + 2, :], x[:, 2 * b:2 * b + 2, :]).then_inc(sem("out_sent"), 16)
            sp.wait_ge(sem("out_sent"), 64)

        @block.gpsimd
        def _(pool):
            pool.dma_start(par_s[:, :], par).then_inc(sem("par_in"), 16)
            pool.dma_start(cst_s[:, :], cst).then_inc(sem("cst_in"), 16)
            pool.dma_start(lnr_s, lnr).then_inc(sem("sg_in"), 16)
            pool.dma_start(sgw_s, sgw).then_inc(sem("sgw_in"), 16)
            pool.dma_start(sgb_s, sgb).then_inc(sem("sgb_in"), 16)
            pool.dma_start(lvl_s[:, :, :], lvl).then_inc(sem("lvl_in"), 16)
            pool.wait_ge(sem("act_lo"), before("lo", "b") + 2)
            pool.wait_ge(sem("norm_stats"), before("st", "o") + 1)
            pool.dma_start(pT_s, pT).then_inc(sem("p_in"), 16)
            pool.wait_ge(sem("act_lo"), before("lo", "p") + 1)
            pool.wait_ge(sem("act_y"), before("y", "ff") + 2)
            pool.dma_start(oneh_s[0:33, 0, :], oneh).then_inc(sem("oneh_in"), 16)
            pool.wait_ge(sem("rel_one"), 1)
            pool.dma_start(rel_s[0:32, 0, 0:HEADS], rel).then_inc(sem("rel_in"), 16)
            pool.wait_ge(sem("bvec"), 1)
            pool.dma_start(scratch, bvec[0:HEADS, 0, :]).then_inc(sem("scr_out"), 16)
            pool.wait_ge(sem("scr_out"), 16)
            pool.dma_start(bias[:, :, :], bass.AP(scratch.tensor, 0, [[1, P], [512, HEADS], [1, T]])).then_inc(sem("bias_in"), 16)
            pool.dma_start(ang[64:96, 0, :].bitcast(I32), pos[0:1, :].broadcast_to([32, T])).then_inc(sem("pos_in"), 16)
            pool.wait_ge(sem("act_lo"), before("lo", "c") + 2)
            pool.dma_start(maskb_s[:, 0, :], maskb).then_inc(sem("maskb_in"), 16)
            for s in ("bias_in", "pos_in", "maskb_in"):
                pool.wait_ge(sem(s), 16)

        @block.scalar
        def _(act):
            A = nc.scalar.activation

            def split_hi(u, slot=None, rounds=None):
                if slot is None:
                    slot, rounds = u % RING, u // RING
                act.wait_ge(sem(f"raw_in{slot}"), rounds * 16 + 16)
                if not isinstance(u, int) or u >= RING:
                    act.wait_ge(sem("unit_used"), u + 1 - RING)
                A(whi[:, slot, :], raw[:, slot, :], ACT.Copy).then_inc(sem("hi_ready"), 1)

            def ahead(u):
                if u + RING < UNITS:
                    split_hi(u + RING)

            def filled(u):
                act.wait_ge(sem("unit_used"), u + 1)

            def evac(u, outs, func, b=None, **kw):
                b = u % RING if b is None else b
                src = two(ps[b][:, :]) if len(outs.shape) == 3 else ps[b][:, :]
                return A(outs, src, func, **kw).then_inc(sem(f"evac{b}"), 1)

            def split_x(name, y, dst, groups, n):
                for k in range(groups):
                    act.wait_ge(sem("act_y"), before("y", name) + n * (k + 1))
                    t = y.shape[1] // groups
                    A(xh[:, dst + k * t:dst + (k + 1) * t, :], y[:, k * t:(k + 1) * t, :], ACT.Copy)\
                        .then_inc(sem("act_hi"), 1)

            def bc_copy(name):
                act.wait_ge(sem("norm_bc"), before("bc", name) + 1)
                A(bcs[:, :], ps[7][:, T:2 * T], ACT.Copy).then_inc(sem("norm_bcs"), 1)

            for k in range(2):
                act.wait_ge(sem(("x_in", "x_in2")[k]), 16)
                A(sq1[:, 4 * k:4 * k + 4, :], x[:, 4 * k:4 * k + 4, :], ACT.Square).then_inc(sem("norm_sq"), 1)
            split_hi(0)
            bc_copy("n1")
            split_x("n1", y1, 0, 2, 4)
            split_hi(1)
            split_hi(2)
            act.wait_ge(sem("gam_sub"), 1)
            A(lb[:, 1, :], lb[:, 0, :], ACT.Exp).then_inc(sem("gam_exp"), 1)

            ahead(U_ZV)
            ahead(U_ZV + 1)
            filled(U_ZV + 1)
            for s in range(2):
                evac(U_ZV + s, zv[:, s, :], ACT.Gelu)
            for m in range(2):
                u = U_ZU + m
                ahead(u)
                filled(u)
                evac(u, zu[:, 2 * m:2 * m + 2, :], ACT.Gelu)
            steps = hgrn_schedule()

            def hgrn_act(kind, g, lv):
                H = G[g]
                if kind == "level" and lv in (0, 8):
                    act.wait_ge(sem(f"lv_mm{g}"), lv + 1)
                    for s in range(2):
                        cols = (s if lv == 0 else 1 - s) * P
                        A(H["S"][:, s, :, cols:cols + P], ps[3 + 2 * g + s][:, :].rearrange("p (h t) -> p h t", h=4),
                          ACT.Copy).then_inc(sem(f"lv_copy{g}"), 1)
                if kind == "pv":
                    act.wait_ge(sem(f"pv_mm{g}"), 1)
                    for s in range(2):
                        src = ps[3 + 2 * g + s][:, :].rearrange("p (h t) -> p h t", h=2)
                        A(H["q"][:, 2 * s:2 * s + 2, :], src, ACT.Copy)
                        A(sqo[g][:, 2 * s:2 * s + 2, :], src, ACT.Square).then_inc(sem(f"o_sq{g}"), 1)

            for u in range(4, 32):
                ahead(u)
                if u < U_ZI:
                    g, r = divmod(u - 4, 6)
                    part, m = divmod(r, 2)
                    H = G[g]
                    if g == 1 and part == 0 and m == 0:
                        act.wait_ge(sem("b_out"), 1)
                    filled(u)
                    if part == 0:
                        evac(u, H["q"][:, 2 * m:2 * m + 2, :], ACT.Silu)
                    else:
                        A(H["F"][part - 1][:, 2 * m:2 * m + 2, :], two(ps[u % RING][:, :]), ACT.Sigmoid)
                        evac(u, H["K"][part - 1][:, 2 * m:2 * m + 2, :], ACT.Sigmoid, scale=-1.0)
                elif u < U_GA:
                    if (u - U_ZI) % 2 == 1:
                        filled(u)
                        half = (u - U_ZI) // 2
                        for s in range(2):
                            evac(u - 1 + s, zi[:, s, half * 512:half * 512 + 512], ACT.Copy)
                else:
                    dst, func, m = ((ga, ACT.Sigmoid, u - U_GA) if u < U_ZG else
                                    (zg, ACT.Silu, u - U_ZG) if u < U_GB else (gb, ACT.Sigmoid, u - U_GB))
                    if u == U_GA:
                        act.wait_ge(sem("lv_mm0"), 9)
                    if u == U_GB:
                        act.wait_ge(sem("tree0"), 7)
                    filled(u)
                    evac(u, dst[:, 2 * m:2 * m + 2, :], func)
                for step in steps.get(u, ()):
                    hgrn_act(*step)
            split_x("a", afull, 8, 2, 1)
            filled(U_GB + 3)
            for k in range(2):
                A(xh[:, 2 * k:2 * k + 2, :], bout[:, 2 * k:2 * k + 2, :], ACT.Copy).then_inc(sem("act_hi"), 1)
            for u in range(U_WA, U_WOUT):
                ahead(u)
            split_x("m", merged, 8, 4, 1)
            for m in range(4):
                u = U_WOUT + m
                ahead(u)
                filled(u)
                A(sq2[:, 2 * m:2 * m + 2, :], two(ps[u % RING][:, :]), ACT.Square)
                evac(u, mix[:, 2 * m:2 * m + 2, :], ACT.Copy)
                if m == 1:
                    act.wait_ge(sem("p_in"), 16)
                    A(xh[:, 6:8, :], pT_s, ACT.Copy).then_inc(sem("act_hi"), 1)
            bc_copy("n2")
            ahead(U_PLE)
            filled(U_PLE)
            for b in range(4):
                A(plx[:, 2 * b:2 * b + 2, :], two(ps[3 + b][:, :]), ACT.Copy).then_inc(sem("ple_copy"), 1)
            for k in range(2):
                act.wait_ge(sem("n2_x"), k + 1)
                A(sq3[:, 4 * k:4 * k + 4, :], x[:, 4 * k:4 * k + 4, :], ACT.Square).then_inc(sem("norm_sq"), 1)
            bc_copy("n3")
            split_x("n3", y3, 8, 2, 4)

            def silu_pair(j, u, bank):
                act.wait_ge(sem("unit_used"), u + 1)
                if not isinstance(j, int) or j >= 1:
                    act.wait_ge(sem("hid_y"), j)
                A(silu, ps[bank][:, :], ACT.Silu).then_inc(sem(f"evac{bank}"), 1)

            def hidden_hi(j, hidden_name, tile, slot_h):
                act.wait_ge(sem(hidden_name + "_y"), j + 1)
                A(xh[:, tile:tile + 2, :], hid[slot_h], ACT.Copy).then_inc(sem(hidden_name + "_hi"), 1)

            def split_at(i, k):
                split_hi(6 * i + k, k % RING, 2 * i + k // RING)

            split_hi(U_F1 + RING)
            silu_pair(0, U_F1, U_F1 % RING)
            split_hi(U_F1 + 1 + RING)
            hidden_hi(0, "hid", 0, 0)
            with act.Fori(0, (PAIRS1 - 1) // 2) as i:
                for c in range(2):
                    k = U_F1 + 2 + 3 * c
                    split_at(i, k + RING)
                    silu_pair(2 * i + (1 + c), 6 * i + k, k % RING)
                    split_at(i, k + 1 + RING)
                    hidden_hi(2 * i + (1 + c), "hid", 2 * ((1 + c) % 2), (1 + c) % 2)
                    split_at(i, k + 2 + RING)
            ahead(U_PG - 1)
            filled(U_PG - 1)
            for b in range(4):
                A(sq2[:, 2 * b:2 * b + 2, :], two(ps[3 + b][:, :]), ACT.Square).then_inc(sem("norm_sq"), 1)
            bc_copy("n4")

            split_x("ff", x, 0, 2, 1)
            for m in range(4):
                u = U_PG + m
                ahead(u)
                filled(u)
                if m >= 2:
                    act.wait_ge(sem("pg_x"), m - 1)
                evac(u, sgate[:, m % 2, :], ACT.Sigmoid)
            act.wait_ge(sem("pg_x"), 4)
            for k in range(2):
                A(sq3[:, 4 * k:4 * k + 4, :], x[:, 4 * k:4 * k + 4, :], ACT.Square).then_inc(sem("norm_sq"), 1)
            bc_copy("n5")
            split_x("n5", y3, 8, 2, 4)

            act.wait_ge(sem("ang"), 1)
            A(sink[64:96, 0, :], red[64:96, 0, :], ACT.Sin).then_inc(sem("sin"), 1)
            act.wait_ge(sem("ang"), 2)
            A(cosk[64:96, 0, :], ang[64:96, 0, :], ACT.Sin).then_inc(sem("sin"), 1)

            for m in range(4):
                u = U_CQ + m
                ahead(u)
                filled(u)
                A(sqc[:, 2 * m:2 * m + 2, :], two(ps[u % RING][:, :]), ACT.Square)
                evac(u, c8[:, 2 * m:2 * m + 2, :], ACT.Copy)
            for m in range(4):
                u = U_QA + m
                ahead(u)
                filled(u)
                dst, name = (qa, "qa") if m < 2 else (ka, "ka")
                A(sqA[:, 2 * m:2 * m + 2, :], two(ps[u % RING][:, :]), ACT.Square)
                evac(u, dst[:, 2 * (m % 2):2 * (m % 2) + 2, :], ACT.Copy, scale=col(name))
                if m in (1, 2):
                    n = m - 1
                    act.wait_ge(sem("norm_bc"), before("bc", "c") + n + 1)
                    A(bcs[:, :], ps[7][:, T:2 * T], ACT.Copy).then_inc(sem("norm_bcs"), 1)
            split_x("c", yc, 0, 2, 1)
            ahead(U_VA)
            ahead(U_VA + 1)
            filled(U_VA + 1)
            for s in range(2):
                evac(U_VA + s, va[:, s, :], ACT.Copy)

            def head_pair_filled(name, half, u):
                if half == 3:
                    filled(u)
                else:
                    act.wait_ge(sem(name + "_mm"), half + 1)

            def softmax_exp(p):
                act.wait_ge(sem("head_max"), p + 1)
                for hh in range(2):
                    for s in range(2):
                        sl = slice(0, P) if s == 0 else slice(P, 384)
                        k = 2 * hh + s
                        A(probs[:, 2 * (p % 2) + hh, sl], probs[:, 2 * (p % 2) + hh, sl], ACT.Exp,
                          bias=smx[:, 1, k:k + 1], accum_out=smx[:, 2, k:k + 1]).then_inc(sem("head_exp"), 1)

            def probs_copy(p):
                act.wait_ge(sem("head_tr"), p + 1)
                for hh in range(2):
                    A(probsT[:, 2 * (p % 2) + hh, :], ps[5 + hh][:, 0:384], ACT.Copy).then_inc(sem("head_trc"), 1)

            def heads_hi(p):
                act.wait_ge(sem("head_pv"), p + 1)
                A(xh[:, 8 + p, :], ps[7][:, 0:T], ACT.Copy).then_inc(sem("head_mh"), 1)

            u = U_KR
            ahead(u)
            filled(u)
            A(kr[64:96, 0, :], ps[0][64:96, 0:T], ACT.Copy, scale=col("kb", 0, 64, 96))
            A(krs[64:96, 0, :], ps[0][96:128, 0:T], ACT.Copy)
            act.wait_ge(sem("act_lo"), before("lo", "c") + 2)
            for h in range(HEADS):
                last = A(sqk[64:96, h, :], ps[0][64:96, 0:T], ACT.Square)
            last.then_inc(sem("evac0"), 1)
            evac(u, vb[:, 0, :], ACT.Copy, b=1)
            evac(u, vb[:, 1, :], ACT.Copy, b=2)
            softmax_exp(0)
            for n in range(4):
                u = U_UK + n
                if n:
                    ahead(u)
                else:
                    for half in range(4):
                        if half == 3:
                            ahead(u)
                        head_pair_filled("uk", half, U_UK)
                        b = (U_UK + half) % RING
                        src = ps[b][0:64, :].rearrange("p (h t) -> p h t", h=2)
                        hs = slice(2 * half, 2 * half + 2)
                        A(sqk[0:64, hs, :], src, ACT.Square)
                        A(kb[0:64, hs, :], src, ACT.Copy, scale=col("kb", 0, 0, 64)).then_inc(sem("uk_ev"), 1)
                    probs_copy(0)
                    softmax_exp(1)
                    continue
                for half in ((0,), (1,), (2, 3))[n - 1]:
                    head_pair_filled("uq", half, U_UQ + 2)
                    b = half % RING
                    src = ps[b][0:96, :].rearrange("p (h t) -> p h t", h=2)
                    hs = slice(2 * half, 2 * half + 2)
                    if half == 0:
                        act.wait_ge(sem("act_lo"), before("lo", "c") + 2)
                    A(sqq[0:96, hs, :], src, ACT.Square)
                    A(qsw[64:96, hs, :], ps[b][96:128, :].rearrange("p (h t) -> p h t", h=2), ACT.Copy)
                    A(qb[0:96, hs, :], src, ACT.Copy, scale=col("qb", 0, 0, 96)).then_inc(sem("uq_ev"), 1)
                if n == 1:
                    heads_hi(0)
                    probs_copy(1)
                    softmax_exp(2)
                elif n == 2:
                    heads_hi(1)
                    probs_copy(2)
                    softmax_exp(3)
                else:
                    heads_hi(2)
                    probs_copy(3)
                    heads_hi(3)
            for p in range(6):
                if 1 <= p < 5:
                    probs_copy(p + 3)
                if p < 4:
                    softmax_exp(4 + p)
                if p >= 2:
                    heads_hi(p + 2)
            for m in range(4):
                ahead(U_WO + m)
            for k in range(2):
                act.wait_ge(sem("wo_x"), 2 * k + 2)
                A(sq3[:, 4 * k:4 * k + 4, :], x[:, 4 * k:4 * k + 4, :], ACT.Square).then_inc(sem("norm_sq"), 1)
            bc_copy("n6")
            split_x("n6", y3, 0, 2, 4)

            def relu_pair(j, u, bank):
                act.wait_ge(sem("unit_used"), u + 1)
                if not isinstance(j, int) or j >= 1:
                    act.wait_ge(sem("hid2_y"), j)
                A(silu, ps[bank][:, :], ACT.Relu).then_inc(sem("relu"), 1)

            split_hi(U_F2 + RING)
            relu_pair(0, U_F2, U_F2 % RING)
            hidden_hi(0, "hid2", 8, 0)
            with act.Fori(0, (PAIRS2 - 1) // 3 - 1) as i:
                for c in range(3):
                    k = U_F2 + 1 + 2 * c
                    split_at(i, k + RING)
                    relu_pair(3 * i + (1 + c), 6 * i + k, k % RING)
                    hidden_hi(3 * i + (1 + c), "hid2", 8 + 2 * ((1 + c) % 3), (1 + c) % 3)
                    split_at(i, k + 1 + RING)
            for j in range(PAIRS2 - 3, PAIRS2):
                u = U_F2 + 2 * j - 1
                ahead(u)
                relu_pair(j, u, u % RING)
                hidden_hi(j, "hid2", 8 + 2 * (j % 3), j % 3)
                ahead(u + 1)

        @block.vector
        def _(dve):
            V = nc.vector
            chained = [0]

            def count(ins):
                chained[0] += 1
                ins.then_inc(sem("dve_chain"), 1)

            def link(ins):
                count(ins)
                dve.wait_ge(sem("dve_chain"), chained[0])

            def split_lo(u, slot=None):
                slot = u % RING if slot is None else slot
                dve.wait_ge(sem("hi_ready"), u + 1)
                V.tensor_tensor(wlo[:, slot, :], raw[:, slot, :], whi[:, slot, :].bitcast(F32), ALU.subtract)\
                    .then_inc(sem("lo_ready"), 1)

            def ahead(u):
                if u + RING < UNITS:
                    split_lo(u + RING)

            def evacuated(u):
                b = u % RING
                dve.wait_ge(sem(f"evac{b}"), FILLS[u][b] + 1)

            def rsqrt(src, dst, n):
                v, y, a, b2 = (nt[:, i, 0:n] for i in range(4))
                link(V.tensor_scalar(v, src, EPS, None, ALU.add))
                link(V.tensor_scalar(nti[:, 0:n], v.bitcast(I32), 1, None, ALU.logical_shift_right))
                link(V.tensor_scalar(y.bitcast(I32), nti[:, 0:n], -1.0, 1597463007.0, ALU.mult, ALU.add))
                for it in range(4):
                    link(V.tensor_tensor(a, y, y, ALU.mult))
                    link(V.scalar_tensor_tensor(b2, a, -0.5, v, ALU.mult, ALU.mult))
                    o = dst if it == 3 else y
                    link(V.scalar_tensor_tensor(o, b2, 1.5, y, ALU.add, ALU.mult))

            def norm_factors(name):
                dve.wait_ge(sem("norm_stats"), before("st", name) + 1)
                rsqrt(ps[7][:, 0:2], rs[:, 0:2], 2)
                V.tensor_copy(rx[:, :, :], rs[:, 0:2].unsqueeze(2).broadcast_to([P, 2, P])).then_inc(sem("norm_factors"), 1)

            def norm_apply(name, src, gain, y):
                dve.wait_ge(sem("norm_bcs"), before("bcs", name) + 1)
                for k in range(DT):
                    V.scalar_tensor_tensor(y[:, k, :], src[:, k, :], col(gain, k), bcs[:, :], ALU.mult, ALU.mult)\
                        .then_inc(sem("act_y"), 1)

            def split_x(name, y, dst, groups):
                for k in range(groups):
                    t = y.shape[1] // groups
                    dve.wait_ge(sem("act_hi"), before("hi", name) + k + 1)
                    V.tensor_tensor(xl[:, dst + k * t:dst + (k + 1) * t, :], y[:, k * t:(k + 1) * t, :],
                                    xh[:, dst + k * t:dst + (k + 1) * t, :].bitcast(F32), ALU.subtract)\
                        .then_inc(sem("act_lo"), 1)

            dve.wait_ge(sem("par_in"), 16)
            dve.wait_ge(sem("x_in"), 16)
            dve.wait_ge(sem("x_in2"), 16)
            norm_factors("n1")
            split_lo(0)
            norm_apply("n1", x, "mix_pre", y1)
            split_x("n1", y1, 0, 2)
            split_lo(1)
            gam = par_s[:, PAR["gamma"]:PAR["gamma"] + 16]
            V.tensor_tensor(lb[:, 0, :], gam, gam, ALU.subtract).then_inc(sem("gam_sub"), 1)
            split_lo(2)
            dve.wait_ge(sem("gam_exp"), 1)
            link(V.reciprocal(lb[:, 0, :], lb[:, 1, :]))
            link(V.tensor_tensor(lb[:, 1, :], lb[:, 1, :], lb[:, 0, :], ALU.mult))
            link(V.tensor_tensor(lb[:, 0, :], lb[:, 1, :], lb[:, 1, :], ALU.subtract))
            link(V.tensor_scalar(lb[:, 2, :], lb[:, 0, :], -1.0, 1.0, ALU.mult, ALU.add))

            ahead(0)
            ahead(1)
            dve.wait_ge(sem("sg_in"), 16)
            bn = nt[:, 0, 0:12].rearrange("p (s n) -> p s n", s=2)
            mv = rs[:, 0:4].rearrange("p (s n) -> p s n", s=2)
            for s in range(2):
                evacuated(U_ZV + s)
                link(V.bn_stats(bn[:, s, :], zv[:, s, :]))
            for s in range(2):
                link(V.bn_aggr(mv[:, s, :], bn[:, s, :]))
            rsqrt(mv[:, :, 1], rs[:, 8:10], 2)
            for s in range(2):
                link(V.tensor_scalar(zv[:, s, :], zv[:, s, :], mv[:, s, 0:1], rs[:, 8 + s:9 + s], ALU.subtract, ALU.mult))
                link(V.tensor_tensor(zv[:, s, :], zv[:, s, :], lnr_s[:, 0, :], ALU.mult))
                V.tensor_tensor(vn[:, s, :], zv[:, s, :], lnr_s[:, 1, :], ALU.add).then_inc(sem("vn"), 1)

            steps = hgrn_schedule()

            def gates(g, part, m):
                H = G[g]
                for h in (2 * m, 2 * m + 1):
                    c = 8 * part + 4 * g + h
                    link(V.tensor_scalar(H["F"][part][:, h, :], H["F"][part][:, h, :], lb[:, 2, c:c + 1],
                                         lb[:, 0, c:c + 1], ALU.mult, ALU.add))
                    link(V.tensor_scalar(H["K"][part][:, h, :], H["K"][part][:, h, :], lb[:, 2, c:c + 1], None, ALU.mult))
                fm = H["F"][part][:, 2 * m:2 * m + 2, :]
                link(V.tensor_scalar(fm, fm, TINY, 1.0, ALU.max, ALU.min))

            def decay(g, d, level):
                if level == 0:
                    return G[g]["F"][d].rearrange("p h t -> p (h t)")
                if level == 1:
                    return t1[:, d, :]
                at = sum(4 * T >> i for i in range(2, level))
                return G[g]["F"][d].rearrange("p h t -> p (h t)")[:, at:at + (4 * T >> level)]

            def tree_update(g, lv):
                H = G[g]
                half = 1 << (lv - 1)
                for d in range(2):
                    pair = decay(g, d, lv - 1).rearrange("p (n two) -> p n two", two=2)
                    if lv < 7:
                        count(V.tensor_tensor(decay(g, d, lv), pair[:, :, 0], pair[:, :, 1], ALU.mult))
                    n = 4 * T // (2 * half)
                    for X, side in ((H["Q"][d], 1 - d), (H["K"][d], d)):
                        v = X.rearrange("p h (n two w) -> p (h n) two w", two=2, w=half)[:, :, side, :]
                        dec = pair[:, :, 1 - side:2 - side].broadcast_to([P, n, half])
                        last = V.tensor_tensor(v, v, dec, ALU.mult)
                        if d == 0 or X is H["Q"][d]:
                            count(last)
                last.then_inc(sem(f"tree{g}"), 1)
                dve.wait_ge(sem(f"tree{g}"), lv)

            def hgrn_dve(kind, g, lv):
                H = G[g]
                if kind == "prep":
                    for d in range(2):
                        V.tensor_tensor(H["Q"][d], H["q"], H["F"][d], ALU.mult).then_inc(sem(f"q_init{g}"), 1)
                if kind == "level" and 1 <= lv <= 7:
                    dve.wait_ge(sem(f"lv_mm{g}"), lv + 1)
                    dve.wait_ge(sem("lvl_in"), 16)
                    if lv == 1:
                        dve.wait_ge(sem(f"lv_copy{g}"), 2)
                        dve.wait_ge(sem(f"q_init{g}"), 2)
                    for s in range(2):
                        V.copy_predicated(H["S"][:, s, :, s * P:(s + 1) * P],
                                          lvl_s[:, lv - 1, :].unsqueeze(1).broadcast_to([P, 4, P]),
                                          ps[3 + 2 * g + s][:, :].rearrange("p (h t) -> p h t", h=4))\
                            .then_inc(sem(f"lv_pred{g}"), 1)
                    dve.wait_ge(sem(f"lv_pred{g}"), 2 * lv)
                    tree_update(g, lv)

            for u in range(2, 32):
                ahead(u)
                if u == U_ZU + 1:
                    evacuated(U_ZU)
                    evacuated(U_ZU + 1)
                    dve.wait_ge(sem("sgb_in"), 16)
                if u == 5:
                    for b in range(2):
                        dve.wait_ge(sem("sg_mm"), b + 1)
                        s2 = sgb_s[:, 2 * b:2 * b + 2, :].unsqueeze(2).broadcast_to([P, 2, 2, P])
                        o4 = bout[:, 2 * b:2 * b + 2, :].rearrange("p j (s t) -> p j s t", s=2)
                        link(V.tensor_tensor(o4, ps[3 + b][:, :].rearrange("p (j s t) -> p j s t", j=2, s=2), s2, ALU.add))
                    V.tensor_tensor(bout, bout, zu, ALU.mult).then_inc(sem("b_out"), 1)
                if 4 <= u < U_ZI:
                    g, r = divmod(u - 4, 6)
                    part, m = divmod(r, 2)
                    if part:
                        evacuated(u)
                        gates(g, part - 1, m)
                    if r == 5:
                        hgrn_dve("prep", g, 0)
                for step in steps.get(u, ()):
                    hgrn_dve(*step)
                if u == U_GB - 2:
                    dve.wait_ge(sem("norm_stats"), before("st", "o") + 1)
                    rsqrt(ps[7][:, 0:16], rs[:, 0:16], 16)
                    V.tensor_copy(rxo, rs[:, 0:16].unsqueeze(2).broadcast_to([P, 16, P])).then_inc(sem("norm_factors"), 1)
                if u == U_GB:
                    for h in range(HEADS):
                        if h % 2 == 0:
                            dve.wait_ge(sem("norm_bc"), before("bc", "o") + h // 2 + 1)
                        link(V.scalar_tensor_tensor(afull[:, h, :], G[h // 4]["q"][:, h % 4, :], col("hg_norm", h),
                                                    ps[3 + h // 2][:, (h % 2) * T:(h % 2 + 1) * T], ALU.mult, ALU.mult))
                    evacuated(U_ZG + 3)
                    for k in range(2):
                        V.tensor_tensor(afull[:, 4 * k:4 * k + 4, :], afull[:, 4 * k:4 * k + 4, :],
                                        zg[:, 4 * k:4 * k + 4, :], ALU.mult).then_inc(sem("act_y"), 1)
            split_x("a", afull, 8, 2)
            for k in range(2):
                dve.wait_ge(sem("act_hi"), before("hi", "b") + k + 1)
                V.tensor_tensor(xl[:, 2 * k:2 * k + 2, :], bout[:, 2 * k:2 * k + 2, :],
                                xh[:, 2 * k:2 * k + 2, :].bitcast(F32), ALU.subtract).then_inc(sem("act_lo"), 1)
            evacuated(U_GB + 3)
            for m in range(4):
                u = U_WA + m
                ahead(u)
                dve.wait_ge(sem("unit_used"), u + 1)
                V.tensor_tensor(ga[:, 2 * m:2 * m + 2, :], ga[:, 2 * m:2 * m + 2, :], two(ps[u % RING][:, :]),
                                ALU.mult).then_inc(sem(f"evac{u % RING}"), 1)
            for n in range(2):
                u = U_WB + n
                ahead(u)
                dve.wait_ge(sem("unit_used"), u + 1)
                if n == 0:
                    for m in range(4):
                        evacuated(U_WA + m)
                for b in range(2):
                    t = slice(4 * n + 2 * b, 4 * n + 2 * b + 2)
                    link(V.tensor_tensor(mtmp[:, t, :], gb[:, t, :], two(ps[3 + 2 * n + b][:, :]), ALU.mult))
                    V.tensor_tensor(merged[:, t, :], mtmp[:, t, :], ga[:, t, :], ALU.add).then_inc(sem("act_y"), 1)
            split_x("m", merged, 8, 4)
            for m in range(4):
                ahead(U_WOUT + m)
                if m == 2:
                    dve.wait_ge(sem("act_hi"), before("hi", "p") + 1)
                    V.tensor_tensor(xl[:, 6:8, :], pT_s, xh[:, 6:8, :].bitcast(F32), ALU.subtract).then_inc(sem("act_lo"), 1)
            norm_factors("n2")
            norm_apply("n2", mix, "mix_post", tmp2)
            for k in range(2):
                dve.wait_ge(sem("act_y"), before("y", "n2") + 4 * k + 4)
                V.tensor_tensor(x[:, 4 * k:4 * k + 4, :], x[:, 4 * k:4 * k + 4, :], tmp2[:, 4 * k:4 * k + 4, :], ALU.add)\
                    .then_inc(sem("n2_x"), 1)
            ahead(U_PLE)
            norm_factors("n3")
            dve.wait_ge(sem("n2_x"), 2)
            norm_apply("n3", x, "ffn_pre", y3)
            split_x("n3", y3, 8, 2)

            def hidden(j, slot_h, u_up, bank, silus):
                dve.wait_ge(sem("unit_used"), u_up + 1)
                dve.wait_ge(sem(f"evac{(bank - 1) % RING}"), silus)
                if not isinstance(j, int) or j >= 1:
                    dve.wait_ge(sem("hid_lo"), j)
                V.tensor_tensor(hid[slot_h], two(silu), two(ps[bank][:, :]), ALU.mult).then_inc(sem("hid_y"), 1)

            def hidden_lo(j, slot_h, hidden_name, base):
                dve.wait_ge(sem(hidden_name + "_hi"), j + 1)
                V.tensor_tensor(xl[:, base + 2 * slot_h:base + 2 * slot_h + 2, :], hid[slot_h],
                                xh[:, base + 2 * slot_h:base + 2 * slot_h + 2, :].bitcast(F32), ALU.subtract)\
                    .then_inc(sem(hidden_name + "_lo"), 1)

            split_lo(U_F1 + RING)
            split_lo(U_F1 + 1 + RING)
            hidden(0, 0, U_F1 + 1, (U_F1 + 1) % RING, FILLS[U_F1][U_F1 % RING] + 1)
            hidden_lo(0, 0, "hid", 0)
            with dve.Fori(0, (PAIRS1 - 1) // 2) as i:
                for c in range(2):
                    j = 2 * i + (1 + c)
                    u = 6 * i + (U_F1 + 2 + 3 * c)
                    s0 = (U_F1 + 2) % RING
                    split_lo(u + RING, s0)
                    split_lo(u + 1 + RING, (s0 + 1) % RING)
                    hidden(j, (1 + c) % 2, u + 1, (s0 + 1) % RING, FILLS[U_F1 + 2][s0] + j)
                    hidden_lo(j, (1 + c) % 2, "hid", 0)
                    split_lo(u + 2 + RING, (s0 + 2) % RING)
            ahead(U_PG - 1)
            norm_factors("n4")
            dve.wait_ge(sem("norm_bcs"), before("bcs", "n4") + 1)
            for k in range(DT):
                V.scalar_tensor_tensor(tmp2[:, k, :], ps[3 + k // 2][:, (k % 2) * T:(k % 2 + 1) * T], col("ffn_post", k),
                                       bcs[:, :], ALU.mult, ALU.mult).then_inc(sem("act_y"), 1)
            for k in range(2):
                dve.wait_ge(sem("act_y"), before("y", "n4") + 4 * k + 4)
                V.tensor_tensor(x[:, 4 * k:4 * k + 4, :], x[:, 4 * k:4 * k + 4, :], tmp2[:, 4 * k:4 * k + 4, :], ALU.add)\
                    .then_inc(sem("act_y"), 1)
            split_x("ff", x, 0, 2)
            dve.wait_ge(sem("ple_copy"), 4)
            for m in range(4):
                u = U_PG + m
                ahead(u)
                evacuated(u)
                if m == 0:
                    dve.wait_ge(sem("act_y"), before("y", "ff") + 2)
                    dve.wait_ge(sem("act_lo"), before("lo", "ff") + 2)
                else:
                    dve.wait_ge(sem("pg_x"), m)
                link(V.tensor_tensor(two(gtmp),
                                     two(sgate[:, m % 2, :]), plx[:, 2 * m:2 * m + 2, :], ALU.mult))
                V.tensor_tensor(x[:, 2 * m:2 * m + 2, :], x[:, 2 * m:2 * m + 2, :],
                                two(gtmp), ALU.add).then_inc(sem("pg_x"), 1)
                if m == 0:
                    dve.wait_ge(sem("oneh_in"), 16)
                    V.memset(rel_s[0:33, 0, 0:HEADS], 1.0).then_inc(sem("rel_one"), 1)
                if m == 3:
                    dve.wait_ge(sem("bv_mm"), 1)
                    V.tensor_copy(bvec[0:HEADS, 0, :], ps[3][0:HEADS, :]).then_inc(sem("bvec"), 1)
            norm_factors("n5")
            dve.wait_ge(sem("pg_x"), 4)
            norm_apply("n5", x, "mix2", y3)
            split_x("n5", y3, 8, 2)
            dve.wait_ge(sem("pos_in"), 16)
            a_, r_, c_ = ang[64:96, 0, :], red[64:96, 0, :], cosk[64:96, 0, :]
            link(V.tensor_copy(r_, a_.bitcast(I32)))
            link(V.tensor_scalar(a_, r_, cst_s[64:96, C_INVF:C_INVF + 1], None, ALU.mult))
            link(V.tensor_scalar(c_, a_, 1.0 / (2 * np.pi), 12582912.0, ALU.mult, ALU.add))
            link(V.tensor_scalar(c_, c_, 12582912.0, None, ALU.subtract))
            for part in TWO_PI:
                link(V.scalar_tensor_tensor(a_, c_, -part, a_, ALU.mult, ALU.add))
            lim = 3.1415925
            V.tensor_scalar(r_, a_, lim, -lim, ALU.min, ALU.max).then_inc(sem("ang"), 1)
            link(V.tensor_scalar(a_, a_, float(np.pi / 2), None, ALU.add))
            link(V.tensor_scalar(c_, a_, float(np.pi), -2 * float(np.pi), ALU.is_gt, ALU.mult))
            link(V.tensor_tensor(a_, a_, c_, ALU.add))
            V.tensor_scalar(a_, a_, lim, -lim, ALU.min, ALU.max).then_inc(sem("ang"), 1)
            dve.wait_ge(sem("sin"), 2)
            sgn = cst_s[64:96, C_SIGN:C_SIGN + 1]
            link(V.tensor_copy(cosq[64:96, 0, :], cosk[64:96, 0, :]))
            link(V.tensor_scalar(sinq[64:96, 0, :], sink[64:96, 0, :], col("qb_swap", 0, 64, 96), sgn, ALU.mult, ALU.mult))
            link(V.tensor_scalar(sink[64:96, 0, :], sink[64:96, 0, :], col("kb_swap", 0, 64, 96), sgn, ALU.mult, ALU.mult))

            for m in range(4):
                ahead(U_CQ + m)
            for n, (which, gain, tiles, at) in enumerate(((MEAN_CQ, "cq", 6, 0), (MEAN_CKV, "ckv", 2, 6))):
                ahead(U_QA + 2 * n)
                dve.wait_ge(sem("norm_stats"), before("st", "c") + n + 1)
                rsqrt(ps[7][:, 0:2], rs[:, 0:2], 2)
                V.tensor_copy(rx[:, :, :], rs[:, 0:2].unsqueeze(2).broadcast_to([P, 2, P])).then_inc(sem("norm_factors"), 1)
                dve.wait_ge(sem("norm_bcs"), before("bcs", "c") + n + 1)
                for k in range(tiles):
                    ins = V.scalar_tensor_tensor(yc[:, at + k, :], c8[:, at + k, :], col(gain, k), bcs[:, :], ALU.mult, ALU.mult)
                    if (at + k) % 4 == 3:
                        ins.then_inc(sem("act_y"), 1)
                    else:
                        count(ins)
                ahead(U_QA + 2 * n + 1)
            split_x("c", yc, 0, 2)

            def head_factors(name, width, kx):
                dve.wait_ge(sem("norm_stats"), before("st", name) + 1)
                rsqrt(ps[7][:, 0:32], rs[:, 0:32], 32)
                r3 = rs[:, 0:32].rearrange("p (s h) -> p s h", s=2)
                link(V.tensor_copy(kx, r3[:, :, 8:16].unsqueeze(3).broadcast_to([P, 2, HEADS, width])))
                V.tensor_scalar(r3[:, :, 0:8], r3[:, :, 0:8], float(np.float32(1.0 / np.sqrt(width))), None, ALU.mult)\
                    .then_inc(sem("norm_factors"), 1)

            def logits_row(p):
                dve.wait_ge(sem("head_qk"), p + 1)
                if p >= 2:
                    dve.wait_ge(sem("head_tr"), p - 1)
                for hh in range(2):
                    h = 2 * (p % 4) + hh
                    L = probs[:, 2 * (p % 2) + hh, :]
                    tab = bias_table(h) if p < 4 else mask_table()
                    V.scalar_tensor_tensor(L[:, 0:P], ps[3 + hh][:, 0:P], rs[:, h:h + 1], tab[0], ALU.mult, ALU.add)\
                        .then_inc(sem("head_l"), 1)
                    V.scalar_tensor_tensor(L[:, P:384], ps[3 + hh][:, P:384], rs[:, 16 + h:17 + h], tab[1], ALU.mult, ALU.add)\
                        .then_inc(sem("head_l"), 1)
                dve.wait_ge(sem("head_l"), 4 * p + 4)
                L2 = probs[:, 2 * (p % 2):2 * (p % 2) + 2, :]
                m4 = smx[:, 0, :].rearrange("p (h s) -> p h s", s=2)
                V.reduce_max(m4[:, :, 0], L2[:, :, 0:P], AX).then_inc(sem("red"), 1)
                V.reduce_max(m4[:, :, 1], L2[:, :, P:384], AX).then_inc(sem("red"), 1)
                redn[0] += 2
                dve.wait_ge(sem("red"), redn[0])
                V.tensor_scalar(smx[:, 1, :], smx[:, 0, :], -1.0, None, ALU.mult).then_inc(sem("head_max"), 1)

            def normalise(p):
                dve.wait_ge(sem("head_exp"), 4 * p + 4)
                link(V.reciprocal(smx[:, 0, :], smx[:, 2, :]))
                for hh in range(2):
                    L = probs[:, 2 * (p % 2) + hh, :]
                    V.tensor_scalar(L[:, 0:P], L[:, 0:P], smx[:, 0, 2 * hh:2 * hh + 1], None, ALU.mult).then_inc(sem("head_p"), 1)
                    V.tensor_scalar(L[:, P:384], L[:, P:384], smx[:, 0, 2 * hh + 1:2 * hh + 2], None, ALU.mult).then_inc(sem("head_p"), 1)

            def heads_lo(p):
                dve.wait_ge(sem("head_mh"), p + 1)
                V.tensor_tensor(xl[:, 8 + p, :], ps[7][:, 0:T], xh[:, 8 + p, :].bitcast(F32), ALU.subtract)\
                    .then_inc(sem("head_ml"), 1)

            redn = [0]

            def bias_table(h):
                return bias[:, h, 127::-1], bias[:, h, ::-1]

            def mask_table():
                return maskb_s[:, 0, P:T], maskb_s[:, 0, :]

            ahead(U_VA)
            head_factors("sa", 64, kxA.rearrange("p s (h w) -> p s h w", h=HEADS))
            ahead(U_VA + 1)
            evacuated(U_KA)
            evacuated(U_KA + 1)
            for b in range(2):
                dve.wait_ge(sem("norm_bc"), before("bc", "sa") + b + 1)
                V.tensor_tensor(ka[:, 2 * b:2 * b + 2, :], ka[:, 2 * b:2 * b + 2, :],
                                two(ps[3 + b][:, :]), ALU.mult).then_inc(sem("ka_n"), 1)
            dve.wait_ge(sem("bias_in"), 16)
            ahead(U_KR)
            logits_row(0)
            ahead(U_UK)
            dve.wait_ge(sem("evac0"), FILLS[U_KR][0] + 1)
            k_, s_ = kr[64:96, 0, :], krs[64:96, 0, :]
            link(V.tensor_tensor(k_, k_, cosk[64:96, 0, :], ALU.mult))
            link(V.tensor_tensor(s_, s_, sink[64:96, 0, :], ALU.mult))
            link(V.tensor_tensor(k_, k_, s_, ALU.add))
            normalise(0)
            logits_row(1)
            ahead(U_UQ)
            normalise(1)
            logits_row(2)
            heads_lo(0)
            ahead(U_UQ + 1)
            normalise(2)
            logits_row(3)
            heads_lo(1)
            ahead(U_UQ + 2)
            normalise(3)
            heads_lo(2)
            for half in range(4):
                dve.wait_ge(sem("uq_ev"), half + 1)
                hs = slice(2 * half, 2 * half + 2)
                q_, w_ = qb[64:96, hs, :], qsw[64:96, hs, :]
                V.tensor_tensor(q_, q_, cosq[64:96, 0:1, :].broadcast_to([32, 2, T]), ALU.mult).then_inc(sem("rot"), 1)
                V.tensor_tensor(w_, w_, sinq[64:96, 0:1, :].broadcast_to([32, 2, T]), ALU.mult).then_inc(sem("rot"), 1)
                dve.wait_ge(sem("rot"), 2 * half + 2)
                V.tensor_tensor(q_, q_, w_, ALU.add).then_inc(sem("q_rot"), 1)
            heads_lo(3)
            head_factors("sb", 96, kxB.rearrange("p (s h) w -> p s h w", s=2))
            dve.wait_ge(sem("uk_ev"), 4)
            for b in range(4):
                dve.wait_ge(sem("norm_bc"), before("bc", "sb") + b + 1)
                src = two(ps[b % RING][:, :])
                hs = slice(2 * b, 2 * b + 2)
                V.tensor_tensor(kb[0:64, hs, :], kb[0:64, hs, :], src[0:64], ALU.mult).then_inc(sem("kb_n"), 1)
                V.tensor_tensor(kb[64:96, hs, :], kr[64:96, 0:1, :].broadcast_to([32, 2, T]), src[64:96], ALU.mult)\
                    .then_inc(sem("kb_n"), 1)
            dve.wait_ge(sem("maskb_in"), 16)
            for p in range(6):
                if 1 <= p < 5:
                    normalise(p + 3)
                if p < 4:
                    logits_row(4 + p)
                if p >= 2:
                    heads_lo(p + 2)
            for m in range(4):
                u = U_WO + m
                ahead(u)
                dve.wait_ge(sem("unit_used"), u + 1)
                V.tensor_tensor(x[:, 2 * m:2 * m + 2, :], x[:, 2 * m:2 * m + 2, :],
                                two(ps[u % RING][:, :]), ALU.add).then_inc(sem("wo_x"), 1)
            norm_factors("n6")
            dve.wait_ge(sem("wo_x"), 4)
            norm_apply("n6", x, "ffn2", y3)
            split_x("n6", y3, 0, 2)

            def relu_square(j, slot_h, slot):
                dve.wait_ge(sem("relu"), j + 1)
                if not isinstance(j, int) or j >= 1:
                    dve.wait_ge(sem("hid2_lo"), j)
                V.tensor_tensor(hid[slot_h], two(silu),
                                two(ps[slot][:, :]), ALU.mult).then_inc(sem("hid2_y"), 1)

            split_lo(U_F2 + RING)
            relu_square(0, 0, U_F2 % RING)
            hidden_lo(0, 0, "hid2", 8)
            with dve.Fori(0, (PAIRS2 - 1) // 3 - 1) as i:
                for c in range(3):
                    u0 = 6 * i + (U_F2 + 1 + 2 * c)
                    s0 = (U_F2 + 1 + 2 * c) % RING
                    j = 3 * i + (1 + c)
                    split_lo(u0 + RING, s0)
                    relu_square(j, (1 + c) % 3, s0)
                    hidden_lo(j, (1 + c) % 3, "hid2", 8)
                    split_lo(u0 + 1 + RING, (s0 + 1) % RING)
            for j in range(PAIRS2 - 3, PAIRS2):
                u0 = U_F2 + 2 * j - 1
                ahead(u0)
                relu_square(j, j % 3, u0 % RING)
                hidden_lo(j, j % 3, "hid2", 8)
                ahead(u0 + 1)
            dve.wait_ge(sem("unit_used"), UNITS)
            for b in range(4):
                V.tensor_tensor(x[:, 2 * b:2 * b + 2, :], x[:, 2 * b:2 * b + 2, :],
                                two(ps[3 + b][:, :]), ALU.add).then_inc(sem("out_ready"), 1)

        @block.tensor
        def _(pe):
            mm = nc.tensor.matmul

            def mm3(out, slot, at, tile, start, stop, width=P, skip=False):
                hi = whi[:, slot, at:at + width]
                mm(out, hi, xh[:, tile, :], start=start, stop=False, skip_group_check=skip)
                mm(out, hi, xl[:, tile, :], start=False, stop=False, skip_group_check=skip)
                return mm(out, wlo[:, slot, at:at + width], xh[:, tile, :], start=False, stop=stop, skip_group_check=skip)

            def arrived(u):
                pe.wait_ge(sem("lo_ready"), u + 1)

            def bank_free(u, b):
                if FILLS[u][b]:
                    pe.wait_ge(sem(f"evac{b}"), FILLS[u][b])

            def used(ins):
                ins.then_inc(sem("unit_used"), 1)

            def two_tiles(u, base, x_name=None):
                arrived(u)
                bank_free(u, u % RING)
                for m in range(2):
                    for k in range(8):
                        if x_name and m == 0 and k % 4 == 0:
                            pe.wait_ge(sem("act_lo"), before("lo", x_name) + k // 4 + 1)
                        last = mm3(ps[u % RING][:, m * T:(m + 1) * T], u % RING, (8 * m + k) * P, base + k, k == 0, k == 7)
                used(last)

            def token_major(u0, base, x_name=None):
                for n in range(2):
                    u = u0 + n
                    arrived(u)
                    if n == 0:
                        for s in range(2):
                            bank_free(u0 + s, (u0 + s) % RING)
                    for s in range(2):
                        o = ps[(u0 + s) % RING][:, :]
                        for k in range(4):
                            t = base + 4 * n + k
                            if x_name and s == 0 and k == 0:
                                pe.wait_ge(sem("act_lo"), before("lo", x_name) + n + 1)
                            xs = slice(s * P, (s + 1) * P)
                            wc = slice(512 * k, 512 * k + 512)
                            first, end = n == 0 and k == 0, n == 1 and k == 3
                            mm(o, xh[:, t, xs], whi[:, u % RING, wc], start=first, stop=False)
                            mm(o, xl[:, t, xs], whi[:, u % RING, wc], start=False, stop=False)
                            last = mm(o, xh[:, t, xs], wlo[:, u % RING, wc], start=False, stop=end)
                    used(last)

            def norm_stats(name, sq, waits):
                for s_name, value in waits:
                    pe.wait_ge(sem(s_name), value)
                for s in range(2):
                    for k in range(8):
                        last = mm(ps[7][:, s:s + 1], sq[:, k, s * P:(s + 1) * P], mean_col(MEAN_D), start=k == 0, stop=k == 7)
                last.then_inc(sem("norm_stats"), 1)

            def norm_bc(name):
                pe.wait_ge(sem("norm_factors"), before("rx", name) + 1)
                for s in range(2):
                    last = mm(ps[7][:, T + s * P:T + (s + 1) * P], rx[:, s, :], ident, start=True, stop=True)
                last.then_inc(sem("norm_bc"), 1)

            pe.wait_ge(sem("cst_in"), 16)
            norm_stats("n1", sq1, [("norm_sq", before("sq", "n1") + 2)])
            norm_bc("n1")
            token_major(U_ZV, 0, "n1")
            steps = hgrn_schedule()

            def spatial_mix(b):
                pe.wait_ge(sem("sgw_in"), 16)
                pe.wait_ge(sem("vn"), 2)
                for j in (2 * b, 2 * b + 1):
                    for s in range(2):
                        for e in range(2):
                            g = 2 * j + e
                            c = (j % 2) * T + s * P
                            last = mm(ps[3 + b][64 * e:64 * e + 64, c:c + P], vn[:, s, g * 64:g * 64 + 64],
                                      sgw_s[:, g, :], start=True, stop=True)
                last.then_inc(sem("sg_mm"), 1)

            def hgrn_pe(kind, g, lv):
                H = G[g]
                if kind == "level":
                    banks = (ps[3 + 2 * g], ps[4 + 2 * g])
                    if lv == 0:
                        pe.wait_ge(sem(f"q_init{g}"), 2)
                        pe.wait_ge(sem("b_out"), 1)
                        for s in range(2):
                            for h in range(4):
                                for d in range(2):
                                    ts = slice(s * P, (s + 1) * P)
                                    last = mm(banks[s][:, h * P:(h + 1) * P], H["K"][d][:, h, ts], H["q"][:, h, ts],
                                              start=d == 0, stop=d == 1)
                    elif lv <= 7:
                        if lv == 1:
                            pe.wait_ge(sem(f"lv_copy{g}"), 2)
                        else:
                            pe.wait_ge(sem(f"tree{g}"), lv - 1)
                        w = 1 << (lv - 1)
                        for s in range(2):
                            for h in range(4):
                                o = banks[s][:, h * P:(h + 1) * P].rearrange("p (n two w) -> p n two w", two=2, w=w)
                                for d in range(2):
                                    qv = H["Q"][d][:, h, s * P:(s + 1) * P].rearrange("p (n two w) -> p n two w", two=2, w=w)
                                    last = mm(o[:, :, 1 - d, :], H["K"][d][:, h, s * P:(s + 1) * P], qv[:, :, 1 - d, :],
                                              start=True, stop=True)
                    else:
                        pe.wait_ge(sem(f"tree{g}"), 7)
                        for s in range(2):
                            for h in range(4):
                                last = mm(banks[s][:, h * P:(h + 1) * P], H["K"][s][:, h, s * P:(s + 1) * P],
                                          H["Q"][s][:, h, (1 - s) * P:(2 - s) * P], start=True, stop=True)
                    last.then_inc(sem(f"lv_mm{g}"), 1)
                if kind == "pv":
                    pe.wait_ge(sem(f"lv_copy{g}"), 4)
                    for h in range(4):
                        for s in range(2):
                            hh = 4 * g + h
                            if h == 0 and s == 0:
                                for uu in (U_ZI + 1, U_ZI + 3):
                                    for v in (uu - 1, uu):
                                        pe.wait_ge(sem(f"evac{v % RING}"), FILLS[v][v % RING] + 1)
                            last = mm(ps[3 + 2 * g + h // 2][:, (h % 2) * T:(h % 2 + 1) * T],
                                      zi[:, s, hh * P:(hh + 1) * P], H["S"][:, s, h, :], start=s == 0, stop=s == 1)
                    last.then_inc(sem(f"pv_mm{g}"), 1)

            for u in range(U_ZU, U_WA):
                if U_ZI <= u < U_GA:
                    if (u - U_ZI) % 2 == 0:
                        token_major(u, 0)
                else:
                    two_tiles(u, 0)
                if u == U_Q[0]:
                    spatial_mix(0)
                    spatial_mix(1)
                for step in steps.get(u, ()):
                    hgrn_pe(*step)
                if u == U_GB - 2:
                    for g in range(2):
                        pe.wait_ge(sem(f"o_sq{g}"), 2)
                    for h in range(HEADS):
                        for s in range(2):
                            last = mm(ps[7][:, 2 * h + s:2 * h + s + 1], sqo[h // 4][:, h % 4, s * P:(s + 1) * P],
                                      mean_col(MEAN_HEAD), start=True, stop=True)
                    last.then_inc(sem("norm_stats"), 1)
                if u == U_GB - 1:
                    pe.wait_ge(sem("norm_factors"), before("rx", "o") + 1)
                    for h in range(HEADS):
                        for s in range(2):
                            last = mm(ps[3 + h // 2][:, (h % 2) * T + s * P:(h % 2) * T + (s + 1) * P], rxo[:, 2 * h + s, :],
                                      ident, start=True, stop=True)
                        if h % 2:
                            last.then_inc(sem("norm_bc"), 1)
            for m in range(4):
                two_tiles(U_WA + m, 8, "a" if m == 0 else None)
            for n in range(2):
                u = U_WB + n
                arrived(u)
                if n == 0:
                    pe.wait_ge(sem("act_lo"), before("lo", "b") + 2)
                for m in range(4):
                    for k in range(4):
                        last = mm3(ps[3 + 2 * n + m // 2][:, (m % 2) * T:(m % 2 + 1) * T], u % RING, (4 * m + k) * P, k,
                                   k == 0, k == 3)
                used(last)
            pe.wait_ge(sem("act_lo"), before("lo", "m") + 4)
            for m in range(4):
                two_tiles(U_WOUT + m, 8)
            last_mix = U_WOUT + 3
            norm_stats("n2", sq2, [(f"evac{u % RING}", FILLS[u][u % RING] + 1) for u in range(U_WOUT, U_WOUT + 4)])
            arrived(U_PLE)
            pe.wait_ge(sem("act_lo"), before("lo", "p") + 1)
            for m in range(DT):
                for k in range(2):
                    last = mm3(ps[3 + m // 2][:, (m % 2) * T:(m % 2 + 1) * T], U_PLE % RING, (2 * m + k) * P, 6 + k, k == 0, k == 1)
                if m == 0:
                    norm_bc("n2")
            used(last)
            norm_stats("n3", sq3, [("norm_sq", before("sq", "n3") + 2)])
            norm_bc("n3")

            def down(slot, base, first):
                for kk in range(2):
                    for m in range(DT):
                        start = first and kk == 0 and m % 2 == 0
                        last = mm3(ps[3 + m // 2][:, (m % 2) * T:(m % 2 + 1) * T], slot, (8 * kk + m) * P, base + kk,
                                   start, False, skip=True)
                return last

            def pair_tiles(u, slot, base):
                for m in range(2):
                    for k in range(8):
                        last = mm3(ps[slot][:, m * T:(m + 1) * T], slot, (8 * m + k) * P, base + k, k == 0, k == 7)
                return last

            two_tiles(U_F1, 8, "n3")
            two_tiles(U_F1 + 1, 8)
            pe.wait_ge(sem("ple_copy"), 4)
            s0 = (U_F1 + 2) % RING

            def ffn1_step(j, u, c, first):
                pe.wait_ge(sem("lo_ready"), u + 1)
                pe.wait_ge(sem("hid_y"), j)
                used(pair_tiles(u, s0, 8))
                pe.wait_ge(sem("lo_ready"), u + 2)
                used(pair_tiles(u + 1, (s0 + 1) % RING, 8))
                pe.wait_ge(sem("lo_ready"), u + 3)
                pe.wait_ge(sem("hid_lo"), j)
                used(down((s0 + 2) % RING, 2 * c, first))

            for c in range(2):
                ffn1_step(1 + c, U_F1 + 2 + 3 * c, c, c == 0)
            with pe.Fori(1, (PAIRS1 - 1) // 2) as i:
                for c in range(2):
                    ffn1_step(2 * i + (1 + c), 6 * i + (U_F1 + 2 + 3 * c), c, False)
            arrived(U_PG - 1)
            pe.wait_ge(sem("hid_lo"), PAIRS1)
            used(down((U_PG - 1) % RING, 2 * ((PAIRS1 - 1) % 2), False))
            norm_stats("n4", sq2, [("norm_sq", before("sq", "n4") + 4)])
            norm_bc("n4")
            for m in range(4):
                two_tiles(U_PG + m, 0, "ff" if m == 0 else None)
                if m == 2:
                    pe.wait_ge(sem("rel_in"), 16)
                    pe.wait_ge(sem("oneh_in"), 16)
                    mm(ps[3][0:HEADS, :], rel_s[0:33, 0, 0:HEADS], oneh_s[0:33, 0, :], start=True, stop=True)\
                        .then_inc(sem("bv_mm"), 1)
            norm_stats("n5", sq3, [("norm_sq", before("sq", "n5") + 2)])
            norm_bc("n5")

            def latent_stats(n):
                which, tiles, at = ((MEAN_CQ, 6, 0), (MEAN_CKV, 2, 6))[n]
                for u in range(U_CQ, U_CKV + 1):
                    pe.wait_ge(sem(f"evac{u % RING}"), FILLS[u][u % RING] + 1)
                if n:
                    pe.wait_ge(sem("norm_bcs"), before("bcs", "c") + n)
                for s in range(2):
                    for k in range(tiles):
                        last = mm(ps[7][:, s:s + 1], sqc[:, at + k, s * P:(s + 1) * P], mean_col(which), start=k == 0, stop=k == tiles - 1)
                last.then_inc(sem("norm_stats"), 1)

            def latent_bc(n):
                pe.wait_ge(sem("norm_factors"), before("rx", "c") + n + 1)
                for s in range(2):
                    last = mm(ps[7][:, T + s * P:T + (s + 1) * P], rx[:, s, :], ident, start=True, stop=True)
                last.then_inc(sem("norm_bc"), 1)

            for m in range(4):
                two_tiles(U_CQ + m, 8, "n5" if m == 0 else None)
            two_tiles(U_QA, 8)
            latent_stats(0)
            two_tiles(U_QA + 1, 8)
            latent_bc(0)
            latent_stats(1)
            two_tiles(U_KA, 8)
            latent_bc(1)
            two_tiles(U_KA + 1, 8)
            token_major(U_VA, 8)
            for u in range(U_QA, U_VA):
                pe.wait_ge(sem(f"evac{u % RING}"), FILLS[u][u % RING] + 1)
            for s in range(2):
                for j in range(8):
                    c = 2 * j
                    last = mm(ps[7][:, 16 * s:16 * s + 16], sqA[:, j, s * P:(s + 1) * P],
                              cst_s[:, C_Z64 + 16 - c:C_Z64 + 32 - c], start=j == 0, stop=j == 7)
            last.then_inc(sem("norm_stats"), 1)
            u = U_KR
            arrived(u)
            for b in range(RING):
                bank_free(u, b)
            for k in range(8):
                mm3(ps[0][:, 0:T], u % RING, k * P, 8 + k, k == 0, k == 7)
            pe.wait_ge(sem("act_lo"), before("lo", "c") + 2)
            for s in range(2):
                for k in range(2):
                    xs = slice(s * P, (s + 1) * P)
                    wc = slice(1024 + 512 * k, 1536 + 512 * k)
                    mm(ps[1 + s][:, :], xh[:, 6 + k, xs], whi[:, u % RING, wc], start=k == 0, stop=False)
                    mm(ps[1 + s][:, :], xl[:, 6 + k, xs], whi[:, u % RING, wc], start=False, stop=False)
                    last = mm(ps[1 + s][:, :], xh[:, 6 + k, xs], wlo[:, u % RING, wc], start=False, stop=k == 1)
            used(last)
            pe.wait_ge(sem("norm_factors"), before("rx", "sa") + 1)
            for j in range(4):
                for s in range(2):
                    last = mm(ps[3 + j // 2][:, (j % 2) * T + s * P:(j % 2) * T + (s + 1) * P], kxA[:, s, j * P:(j + 1) * P],
                              ident, start=True, stop=True)
                if j % 2:
                    last.then_inc(sem("norm_bc"), 1)

            def qk(p):
                if p:
                    pe.wait_ge(sem("head_l"), 4 * p)
                else:
                    pe.wait_ge(sem("ka_n"), 2)
                if p == 4:
                    pe.wait_ge(sem("kb_n"), 8)
                    pe.wait_ge(sem("q_rot"), 4)
                for hh in range(2):
                    h = 2 * (p % 4) + hh
                    if p < 4:
                        a = 64 * hh
                        q_, k_ = qa[a:a + 64, h // 2, :], ka[a:a + 64, h // 2, :]
                    else:
                        q_, k_ = qb[0:96, h, :], kb[0:96, h, :]
                    mm(ps[3 + hh][:, 0:P], q_[:, 0:P], k_[:, 0:P], start=True, stop=True)
                    last = mm(ps[3 + hh][:, P:384], q_[:, P:T], k_, start=True, stop=True)
                last.then_inc(sem("head_qk"), 1)

            def turn(p):
                pe.wait_ge(sem("head_p"), 4 * p + 4)
                if p:
                    pe.wait_ge(sem("head_trc"), 2 * p)
                for hh in range(2):
                    for c in range(3):
                        last = nc.tensor.transpose(ps[5 + hh][:, c * P:(c + 1) * P],
                                                   probs[:, 2 * (p % 2) + hh, c * P:(c + 1) * P], ident)
                last.then_inc(sem("head_tr"), 1)

            def pv(p):
                v = va if p < 4 else vb
                pe.wait_ge(sem("head_trc"), 2 * p + 2)
                if p:
                    pe.wait_ge(sem("head_ml"), p)
                for hh in range(2):
                    h = 2 * (p % 4) + hh
                    o = ps[7][64 * hh:64 * hh + 64, :]
                    PT = probsT[:, 2 * (p % 2) + hh, :]
                    hv = slice(64 * h, 64 * h + 64)
                    mm(o[:, 0:P], v[:, 0, hv], PT[:, 0:P], start=True, stop=True)
                    mm(o[:, P:T], v[:, 0, hv], PT[:, P:T], start=True, stop=False)
                    last = mm(o[:, P:T], v[:, 1, hv], PT[:, T:384], start=False, stop=True)
                last.then_inc(sem("head_pv"), 1)

            qk(0)
            arrived(U_UK)
            for h in range(HEADS):
                b = (U_UK + h // 2) % RING
                if h % 2 == 0 and h // 2 < 3:
                    pe.wait_ge(sem(f"evac{b}"), FILLS[U_UK][b])
                if h == 6:
                    pe.wait_ge(sem("uk_ev"), 1)
                for k in range(2):
                    last = mm3(ps[b][:, (h % 2) * T:(h % 2 + 1) * T], U_UK % RING, (2 * h + k) * P, 6 + k, k == 0, k == 1)
                if h % 2 and h < 7:
                    last.then_inc(sem("uk_mm"), 1)
            used(last)
            turn(0)
            qk(1)
            pe.wait_ge(sem("uk_ev"), 4)
            for n in range(3):
                u = U_UQ + n
                arrived(u)
                for blk in range(16):
                    i = 16 * n + blk
                    h, k = divmod(i, 6)
                    b = (h // 2) % RING
                    if h == 6 and k == 0:
                        pe.wait_ge(sem("uq_ev"), 1)
                    last = mm3(ps[b][:, (h % 2) * T:(h % 2 + 1) * T], u % RING, blk * P, k, k == 0, k == 5)
                    if k == 5 and h % 2 and blk < 15:
                        last.then_inc(sem("uq_mm"), 1)
                used(last)
                pv(n)
                turn(n + 1)
                if n < 2:
                    qk(n + 2)
            pe.wait_ge(sem("uq_ev"), 4)
            pe.wait_ge(sem("uk_ev"), 4)
            pv(3)
            pe.wait_ge(sem("head_ml"), 4)
            for s in range(2):
                for h in range(16):
                    sq = (sqq if h < 8 else sqk)[0:96, h % 8, s * P:(s + 1) * P]
                    last = mm(ps[7][:, 16 * s:16 * s + 16], sq, cst_s[0:96, C_Z96 + 16 - h:C_Z96 + 32 - h], start=h == 0, stop=h == 15)
            last.then_inc(sem("norm_stats"), 1)
            pe.wait_ge(sem("norm_factors"), before("rx", "sb") + 1)
            for h in range(HEADS):
                b = (h // 2) % RING
                if h == 6:
                    pe.wait_ge(sem("kb_n"), 2)
                for s in range(2):
                    last = mm(ps[b][0:96, (h % 2) * T + s * P:(h % 2) * T + (s + 1) * P], kxB[:, 8 * s + h, :], ident, start=True, stop=True)
                if h % 2:
                    last.then_inc(sem("norm_bc"), 1)
            for p in range(6):
                if p < 4:
                    qk(4 + p)
                if p >= 2:
                    pv(4 + p - 2)
                if 1 <= p < 5:
                    turn(p + 3)
            pe.wait_ge(sem("head_ml"), 8)
            for m in range(4):
                u = U_WO + m
                arrived(u)
                if m == 3:
                    pe.wait_ge(sem("wo_x"), 1)
                last = pair_tiles(u, u % RING, 8)
                used(last)
            norm_stats("n6", sq3, [("norm_sq", before("sq", "n6") + 2)])
            norm_bc("n6")

            pe.wait_ge(sem("wo_x"), 4)
            arrived(U_F2)
            pe.wait_ge(sem("act_lo"), before("lo", "n6") + 2)
            used(pair_tiles(U_F2, U_F2 % RING, 0))

            def ffn2_step(j, u, s, base, first):
                pe.wait_ge(sem("lo_ready"), u + 1)
                used(pair_tiles(u, s, 0))
                pe.wait_ge(sem("lo_ready"), u + 2)
                pe.wait_ge(sem("hid2_lo"), j)
                used(down((s + 1) % RING, base, first))

            for j in range(1, 4):
                ffn2_step(j, U_F2 + 2 * j - 1, (U_F2 + 2 * j - 1) % RING, 8 + 2 * ((j - 1) % 3), j == 1)
            with pe.Fori(1, (PAIRS2 - 1) // 3) as i:
                for c in range(3):
                    ffn2_step(3 * i + (1 + c), 6 * i + (U_F2 + 1 + 2 * c), (U_F2 + 1 + 2 * c) % RING, 8 + 2 * c, False)
            arrived(UNITS - 1)
            pe.wait_ge(sem("hid2_lo"), PAIRS2)
            used(down((UNITS - 1) % RING, 8 + 2 * ((PAIRS2 - 1) % 3), False))


def _tiles(v):
    return v.reshape(-1, P).T


def _channel_blocks(m):
    k, n = m.shape[0] // P, m.shape[1] // P
    return m.reshape(k, P, n, P).transpose(1, 2, 0, 3).reshape(P, n * k, P)


def _row_blocks(m):
    k, n = m.shape[0] // P, m.shape[1] // P
    return m.reshape(k, P, n, P).transpose(1, 0, 2, 3).reshape(P, n * k, P)


def _wide(m):
    k = m.shape[0] // P
    return m.reshape(k, P, 512).transpose(1, 0, 2).reshape(P, k * 4, P)


def _weights(a):
    f = lambda n: np.asarray(a[n], np.float32) if a[n].ndim == 2 else np.asarray(a[n][0], np.float32)
    w = f("w_in")
    q, ff, fb, zi, zg, zu, zv, ga, gb = np.split(w, np.cumsum([1024] * 5 + [512] * 2 + [1024]), axis=1)
    parts = [_wide(zv), _channel_blocks(zu)]
    for g in range(2):
        parts += [_channel_blocks(m[:, 512 * g:512 * g + 512]) for m in (q, ff, fb)]
    parts += [_wide(zi[:, 0:512]), _wide(zi[:, 512:])]
    parts += [_channel_blocks(m) for m in (ga, zg, gb, f("w_a"), f("w_b"), f("w_out"), f("w_ple"))]
    gate, up, down = f("w_gate"), f("w_up"), f("w_down")
    pair = lambda m, j: m[:, 256 * j:256 * j + 256]
    for j in range(PAIRS1):
        parts += [_channel_blocks(pair(gate, j)), _channel_blocks(pair(up, j))]
        if j:
            parts.append(_row_blocks(down[256 * (j - 1):256 * j]))
    parts += [_row_blocks(down[256 * (PAIRS1 - 1):]), _channel_blocks(f("w_ple_gate"))]
    w2, uq, ukv = f("w_in_2"), f("w_uq_2"), f("w_ukv_2")
    qa, ka, va, cq, ckv, kr = np.split(w2, np.cumsum([512, 512, 512, 768, 256]), axis=1)
    parts += [_channel_blocks(m) for m in (cq, ckv, qa, ka)] + [_wide(va)]
    swap = np.r_[16:32, 0:16]
    ukv = ukv.reshape(256, HEADS, 128)
    uq = uq.reshape(768, HEADS, 96)
    parts += [_channel_blocks(np.concatenate([kr, kr, kr, kr[:, swap]], axis=1)),
              _wide(ukv[:, :, 64:].reshape(256, 512)), _channel_blocks(ukv.reshape(256, 1024)),
              _channel_blocks(np.concatenate([uq, uq[:, :, 64 + swap]], axis=2).reshape(768, 1024)),
              _channel_blocks(f("w_o_2"))]
    ff1, ff2 = f("w_ff1_2"), f("w_ff2_2")
    for j in range(PAIRS2):
        parts.append(_channel_blocks(pair(ff1, j)))
        if j:
            parts.append(_row_blocks(ff2[256 * (j - 1):256 * j]))
    parts.append(_row_blocks(ff2[256 * (PAIRS2 - 1):]))
    full = np.concatenate(parts, axis=1).reshape(P, UNITS, UNIT)
    return np.ascontiguousarray(full.transpose(1, 0, 2))


def _params(a):
    v = lambda n: np.asarray(a[n], np.float32).reshape(-1)
    pad = lambda x, at=0: np.concatenate([np.zeros(at, np.float32), x, np.zeros(P - at - len(x), np.float32)])[:, None]
    swap = lambda g: pad(np.concatenate([g[80:96], g[64:80]]), 64)
    qb, kb = v("qnorm_b_g_2"), v("knorm_b_g_2")
    return np.concatenate([
        _tiles(v("norm_mix_pre")), _tiles(v("lb_gamma_fwd")), _tiles(v("lb_gamma_bwd")), _tiles(v("hg_norm")),
        _tiles(v("norm_mix_post")), _tiles(v("norm_ffn_pre")), _tiles(v("norm_ffn_post")), _tiles(v("norm_mix_g_2")),
        _tiles(v("cq_norm_g_2")), _tiles(v("ckv_norm_g_2")), _tiles(v("norm_ffn_g_2")),
        np.tile(v("qnorm_a_g_2"), 2)[:, None], np.tile(v("knorm_a_g_2"), 2)[:, None],
        pad(qb), pad(kb), swap(qb), swap(kb)], axis=1)


def _constants():
    c = np.zeros((P, NCST), np.float32)
    c[:, C_ID:C_ID + P] = np.eye(P)
    c[:64, C_Z64 + 16] = c[64:, C_Z64 + 17] = 1 / 64
    c[:, C_Z96 + 16] = 1 / 96
    for k, n in enumerate((1024, 768, 256, 128)):
        c[:, C_MEAN + k] = 1 / n
    freq = 1.0 / (np.float32(10000.0) ** (np.arange(0, 32, 2, dtype=np.float32) / np.float32(32)))
    c[64:96, C_INVF] = np.tile(freq, 2)
    c[64:80, C_SIGN], c[80:96, C_SIGN] = -1, 1
    return c


def _level_masks():
    i = np.arange(P)
    return np.stack([(i[:, None] >> lv == i[None] >> lv) & (i[:, None] >> lv - 1 != i[None] >> lv - 1)
                     for lv in range(1, 8)], axis=1).astype(np.int32)


def _distances():
    d = np.arange(512) - 127
    safe = np.maximum(d, 1).astype(np.float32)
    large = 16 + (np.log(safe / 16) / np.log(2048 / 16) * 16).astype(np.int64)
    bucket = np.where(d < 16, d, np.minimum(large, 31))
    n = (d <= 128).astype(int) + (d % 4 == 0) + (d % 16 == 0)
    seen = (d >= 0) & (n > 0)
    t = np.zeros((33, 512), np.float32)
    t[bucket[seen], np.flatnonzero(seen)] = 1
    t[32] = np.where(seen, np.log(np.maximum(n, 1)), NEG)
    return t


def kernel(**a):
    import concourse.bacc as bacc
    from concourse.bass_utils import run_bass_kernel_spmd

    f = lambda n: np.asarray(a[n], np.float32)
    causal = np.zeros((P, T), np.float32)
    causal[:, P:] = np.where(np.arange(P)[None] <= np.arange(P)[:, None], 0, NEG)
    arrays = {
        "w": _weights(a),
        "xT": f("x")[0].T.reshape(DT, P, T).transpose(1, 0, 2),
        "pT": f("p")[0, 0].T.reshape(2, P, T).transpose(1, 0, 2),
        "par": _params(a), "cst": _constants(), "lvl": _level_masks(),
        "sgw": f("sg_w")[0].transpose(2, 0, 1),
        "sgb": np.repeat(f("sg_b")[0].reshape(4, 2, P), 64, axis=1).transpose(1, 0, 2),
        "lnr": np.broadcast_to(np.stack([f("sg_ln_g")[0], f("sg_ln_b")[0]])[None], (P, 2, 512)),
        "rel": f("rel_bias_2"), "oneh": _distances(), "maskb": causal,
        "pos": np.asarray(a["positions_2"], np.int32).reshape(1, T),
    }
    arrays = {k: np.ascontiguousarray(v) for k, v in arrays.items()}
    nc = bacc.Bacc("TRN2", target_bir_lowering=False, num_devices=1)
    args = [nc.dram_tensor(k, v.shape, mybir.dt.from_np(v.dtype), kind="ExternalInput").ap() for k, v in arrays.items()]
    out = nc.dram_tensor("out", (P, DT, T), F32, kind="ExternalOutput").ap()
    build_blocks(nc, *args, out)
    r = run_bass_kernel_spmd(nc, [arrays], core_ids=[0]).results[0]["out"]
    return np.ascontiguousarray(r.transpose(2, 1, 0).reshape(1, T, D))
```

```python
from contextlib import ExitStack

import numpy as np

import concourse.bass as bass
from concourse import mybir

F32 = mybir.dt.float32
F32R = mybir.dt.float32r
I32 = mybir.dt.int32
ALU = mybir.AluOpType
ACT = mybir.ActivationFunctionType
AX = mybir.AxisListType.X

P = 128
T = 256
D = 1024
DT = D // P
UNIT = 2048
RING = 3
HEADS = 8
FFN = 2816
FFN2 = 4096
EPS = 1e-6
TINY = float(np.finfo(np.float32).tiny)
NEG = -1e30

U_ZV, U_ZU = 0, 2
U_Q = (4, 10)
U_F = ((6, 8), (12, 14))
U_ZI, U_GA, U_ZG, U_GB = 16, 20, 24, 28
U_WA, U_WB, U_WOUT, U_PLE = 32, 36, 38, 42
U_F1 = 43
PAIRS1 = FFN // 256
U_PG = U_F1 + 3 * PAIRS1
U_CQ = U_PG + 4
U_CKV, U_QA, U_KA, U_VA = U_CQ + 3, U_CQ + 4, U_CQ + 6, U_CQ + 8
U_KR, U_UK, U_UQ = U_CQ + 10, U_CQ + 11, U_CQ + 12
U_WO = U_UQ + 3
U_F2 = U_WO + 4
PAIRS2 = FFN2 // 256
UNITS = U_F2 + 2 * PAIRS2

PAR = {}
_at = 0
for _name, _n in (("mix_pre", 8), ("gamma", 16), ("hg_norm", 8), ("mix_post", 8), ("ffn_pre", 8),
                  ("ffn_post", 8), ("mix2", 8), ("cq", 6), ("ckv", 2), ("ffn2", 8), ("qa", 1), ("ka", 1),
                  ("qb", 1), ("kb", 1), ("qb_swap", 1), ("kb_swap", 1)):
    PAR[_name] = _at
    _at += _n
NPAR = _at
C_ID, C_Z64, C_Z96, C_MEAN, C_INVF, C_SIGN = 0, 128, 160, 192, 196, 197
NCST = 198
MEAN_D, MEAN_CQ, MEAN_CKV, MEAN_HEAD = range(4)


def banks_of(u):
    if u in (U_WB, U_WB + 1, U_PLE) or U_UK <= u:
        return ()
    if U_F1 <= u < U_PG:
        return ()
    if u == U_KR:
        return (0, 1, 2)
    return (u % RING,)


def fill_counts():
    before, count = [], [0] * RING
    for u in range(UNITS):
        before.append(tuple(count))
        for b in banks_of(u):
            count[b] += 1
    return before


FILLS = fill_counts()

SIGNALS = {
    "sq": dict(n1=2, n3=4, n4=4, n5=4, n6=4),
    "st": dict(n1=1, o=1, n2=1, n3=1, n4=1, n5=1, c=2, sa=1, sb=1, n6=1),
    "rx": dict(n1=1, o=1, n2=1, n3=1, n4=1, n5=1, c=2, sa=1, sb=1, n6=1),
    "bc": dict(n1=1, o=4, n2=1, n3=1, n4=1, n5=1, c=2, sa=2, sb=4, n6=1),
    "bcs": dict(n1=1, n3=1, n4=1, n5=1, c=2, n6=1),
    "y": dict(a=2, m=4, n2=4, n4=4, c=2),
    "hi": dict(n1=4, a=2, b=2, m=4, p=1, n3=4, ff=4, n5=4, c=2, n6=4),
    "lo": dict(n1=4, a=2, b=2, m=4, p=1, n3=4, ff=4, n5=4, c=2, n6=4),
}


NORMS = ("n1", "n2", "n3", "n4", "n5", "cq", "ckv", "n6")


def z_index(u):
    return u - U_ZU if u < U_ZI else u - U_ZU - 4


def k_index(u):
    return (u - U_Q[0]) // 6 * 4 + (u - U_Q[0]) % 6 - 2


def before(kind, stage):
    stages = list(SIGNALS[kind])
    return sum(SIGNALS[kind][s] for s in stages[:stages.index(stage)])


def hgrn_schedule():
    steps = {}
    for g, first in enumerate((10, 18)):
        for lv in range(9):
            steps.setdefault(first + lv, []).append(("level", g, lv))
    for g, u in enumerate((20, 27)):
        steps.setdefault(u, []).append(("pv", g, 0))
    return steps


_C1 = np.float32(6.28125)
_C2 = np.float32(int((2 * np.pi - float(_C1)) * 2 ** 21) / 2 ** 21)
TWO_PI = (float(_C1), float(_C2), float(np.float32(2 * np.pi - float(_C1) - float(_C2))))


def build_blocks(nc, w, xT, pT, par, cst, lvl, sgw, sgb, lnr, rel, oneh, maskb, pos, out):
    scratch = nc.dram_tensor("bias_scratch", [HEADS, 512], F32, kind="Internal").ap()
    ctx = ExitStack()
    with ctx:
        def sb(name, shape, dt=F32):
            return ctx.enter_context(nc.sbuf_tensor(name, shape, dt))

        sems = {}

        def sem(name):
            if name not in sems:
                sems[name] = ctx.enter_context(nc.semaphore(name))
            return sems[name]

        raw = sb("raw", [P, RING, UNIT])
        whi = sb("whi", [P, RING, UNIT], F32R)
        wlo = sb("wlo", [P, RING, UNIT], F32R)
        xh = sb("xh", [P, 16, T], F32R)
        xl = sb("xl", [P, 16, T], F32R)
        x = sb("x", [P, DT, T])
        work = sb("work", [P, 88 * T])
        par_s = sb("par_s", [P, NPAR])
        cst_s = sb("cst_s", [P, NCST])
        lvl_s = sb("lvl_s", [P, 7, P], I32)
        lb = sb("lb", [P, 3, 16])
        rx = sb("rx", [P, 2, P])
        bcs = sb("bcs", [P, T])
        nt = sb("nt", [P, 4, 32])
        eps_s = sb("eps_s", [P, 2])
        rtok = sb("rtok", [P, len(NORMS), 2])
        gqk = sb("gqk", [P, 1])
        half_s = sb("half_s", [P, 2])
        nti = sb("nti", [P, 32], I32)
        rs = sb("rs", [P, 32])
        smx = sb("smx", [P, 4, 4])
        ps = [ctx.enter_context(nc.psum_tensor(f"ps{b}", [P, 512], F32)) for b in range(8)]

        def view(at, tiles, inner=T):
            return work[:, at * T:(at + tiles) * T].rearrange("p (n t) -> p n t", t=inner)

        def col(name, k=0, a=0, b=P):
            return par_s[a:b, PAR[name] + k:PAR[name] + k + 1]

        def two(ap):
            return ap.rearrange("p (a t) -> p a t", a=2)

        ident = cst_s[:, C_ID:C_ID + P]

        def mean_col(which):
            return cst_s[:, C_MEAN + which:C_MEAN + which + 1]

        sq1 = view(28, 8)
        zv, zu = view(52, 4, 512), view(48, 4)
        lnr_s = view(44, 4, 512)
        sgw_s, sgb_s = view(64, 4, P), view(68, 2, P)
        vn = view(28, 4, 512)
        bout = view(84, 4)
        G = []
        for g in range(2):
            a = 28 * g
            G.append(dict(q=view(a, 4), Q=(view(a + 4, 4), view(a + 8, 4)),
                          K=(view(a + 12, 4), view(a + 16, 4)), F=(view(a + 20, 4), view(a + 24, 4)),
                          S=work[:, (56 + 8 * g) * T:(64 + 8 * g) * T].rearrange("p (s h t) -> p s h t", s=2, t=T)))
        zi = view(72, 8, D)
        t1 = view(80, 4, 512)
        ga, zg, gb = view(4, 8), view(12, 8), view(20, 8)
        sqo = [view(56, 4), view(52, 4)]
        rxo = view(32, 8, P)
        afull = view(40, 8)
        merged, mtmp = view(48, 8), view(56, 8)
        mix, sq2, tmp2 = view(0, 8), view(8, 8), view(16, 8)
        sq3 = view(24, 8)
        plx = view(56, 8)
        pT_s = view(80, 2)
        silu = work[:, 72 * T:74 * T]
        hid = [view(74, 2), view(76, 2), view(78, 2)]
        gated = work[:, 32 * T:34 * T]
        sgate = view(74, 4, 512)
        gtmp = work[:, 78 * T:80 * T]
        bias = view(0, 8)
        qa, ka = view(8, 4), view(12, 4)
        sqA, kxA = view(16, 8), view(16, 4, 512)
        va, vb = view(24, 4, 512), view(28, 4, 512)
        bcs2 = view(56, 1)[:, 0, :]
        c8, sqc, yc = view(32, 8), view(40, 8), view(64, 8)
        qb, kb, qsw, sqq, sqk = view(48, 8), view(56, 8), view(64, 8), view(72, 8), view(32, 8)
        kxB = view(72, 6, 96)
        probs = work[:, 16 * T:22 * T].rearrange("p (n t) -> p n t", t=384)
        probsT = work[:, 40 * T:46 * T].rearrange("p (n t) -> p n t", t=384)
        cosk, sink, cosq, sinq = (view(80 + i, 1) for i in range(4))
        kr, krs = view(84, 1), view(85, 1)
        ang, red = view(86, 1), view(87, 1)
        maskb_s = view(46, 1)
        oneh_s = view(86, 2, 512)
        bvec = view(80, 2, 512)
        rel_s = view(82, 1)

        block = ctx.enter_context(nc.Block())

        @block.sync
        def _(sp):
            sp.dma_start(x[:, 0:4, :], xT[:, 0:4, :]).then_inc(sem("x_in"), 16)
            sp.dma_start(x[:, 4:8, :], xT[:, 4:8, :]).then_inc(sem("x_in2"), 16)

            def load(u, slot):
                sp.dma_start(raw[:, slot, :], w[u]).then_inc(sem(f"raw_in{slot}"), 16)

            for u in range(RING):
                load(u, u)
            with sp.Fori(1, UNITS // RING) as i:
                for s in range(RING):
                    sp.wait_ge(sem("lo_ready"), i * RING + (s + 1 - RING))
                    sp.dma_start(raw[:, s, :], w[bass.ds(i * RING + s, 1)].rearrange("a p n -> (a p) n")).then_inc(sem(f"raw_in{s}"), 16)
            for u in range(UNITS // RING * RING, UNITS):
                sp.wait_ge(sem("lo_ready"), u + 1 - RING)
                load(u, u % RING)
            for b in range(4):
                sp.wait_ge(sem("out_ready"), b + 1)
                sp.dma_start(out[:, 2 * b:2 * b + 2, :], x[:, 2 * b:2 * b + 2, :]).then_inc(sem("out_sent"), 16)
            sp.wait_ge(sem("out_sent"), 64)

        @block.gpsimd
        def _(pool):
            pool.dma_start(par_s[:, :], par).then_inc(sem("par_in"), 16)
            pool.dma_start(cst_s[:, :], cst).then_inc(sem("cst_in"), 16)
            pool.dma_start(lnr_s, lnr).then_inc(sem("sg_in"), 16)
            pool.dma_start(sgw_s, sgw).then_inc(sem("sgw_in"), 16)
            pool.dma_start(sgb_s, sgb).then_inc(sem("sgb_in"), 16)
            pool.dma_start(lvl_s[:, :, :], lvl).then_inc(sem("lvl_in"), 16)
            nc.gpsimd.memset(half_s[:, :], -0.5).then_inc(sem("half"), 1)
            pool.wait_ge(sem("half"), 1)

            def token_factors(n):
                pool.wait_ge(sem("eps_added"), n + 1)
                nc.gpsimd.tensor_tensor(rtok[:, n, :], eps_s[:, :], half_s[:, :], ALU.pow).then_inc(sem("rtok"), 1)

            token_factors(0)
            pool.wait_ge(sem("act_lo"), before("lo", "b") + 2)
            pool.wait_ge(sem("norm_stats"), before("st", "o") + 1)
            pool.dma_start(pT_s, pT).then_inc(sem("p_in"), 16)
            for n in range(1, 4):
                token_factors(n)
            pool.wait_ge(sem("act_lo"), before("lo", "p") + 1)
            pool.wait_ge(sem("ff_x"), 4)
            pool.dma_start(oneh_s[0:33, 0, :], oneh).then_inc(sem("oneh_in"), 16)
            pool.wait_ge(sem("rel_one"), 1)
            pool.dma_start(rel_s[0:32, 0, 0:HEADS], rel).then_inc(sem("rel_in"), 16)
            pool.wait_ge(sem("bvec"), 1)
            pool.dma_start(scratch, bvec[0:HEADS, 0, :]).then_inc(sem("scr_out"), 16)
            pool.wait_ge(sem("scr_out"), 16)
            pool.dma_start(bias[:, :, :], bass.AP(scratch.tensor, 0, [[1, P], [512, HEADS], [1, T]])).then_inc(sem("bias_in"), 16)
            pool.dma_start(ang[64:96, 0, :].bitcast(I32), pos[0:1, :].broadcast_to([32, T])).then_inc(sem("pos_in"), 16)
            for n in range(4, 7):
                token_factors(n)
            pool.wait_ge(sem("act_lo"), before("lo", "c") + 2)
            pool.dma_start(maskb_s[:, 0, :], maskb).then_inc(sem("maskb_in"), 16)
            for s in ("bias_in", "pos_in", "maskb_in"):
                pool.wait_ge(sem(s), 16)
            token_factors(7)

        @block.scalar
        def _(act):
            A = nc.scalar.activation

            def split_hi(u, slot=None, rounds=None):
                if slot is None:
                    slot, rounds = u % RING, u // RING
                act.wait_ge(sem(f"raw_in{slot}"), rounds * 16 + 16)
                if not isinstance(u, int) or u >= RING:
                    act.wait_ge(sem("unit_used"), u + 1 - RING)
                A(whi[:, slot, :], raw[:, slot, :], ACT.Copy).then_inc(sem("hi_ready"), 1)

            def ahead(u):
                if u + RING < UNITS:
                    split_hi(u + RING)

            def filled(u):
                act.wait_ge(sem("unit_used"), u + 1)

            def evac(u, outs, func, b=None, **kw):
                b = u % RING if b is None else b
                src = two(ps[b][:, :]) if len(outs.shape) == 3 else ps[b][:, :]
                return A(outs, src, func, **kw).then_inc(sem(f"evac{b}"), 1)

            def split_x(name, y, dst, groups, n):
                for k in range(groups):
                    act.wait_ge(sem("act_y"), before("y", name) + n * (k + 1))
                    t = y.shape[1] // groups
                    A(xh[:, dst + k * t:dst + (k + 1) * t, :], y[:, k * t:(k + 1) * t, :], ACT.Copy)\
                        .then_inc(sem("act_hi"), 1)

            def gained_hi(name, gain, dst, k):
                for t in (2 * k, 2 * k + 1):
                    ins = A(xh[:, dst + t, :], x[:, t, :], ACT.Copy, scale=col(gain, t))
                ins.then_inc(sem("act_hi"), 1)

            def activated(u, dst, func, source=None, last=True, **kw):
                act.wait_ge(sem(f"evac{u % RING}"), FILLS[u][u % RING] + 1)
                ins = A(dst, dst if source is None else source, func, **kw)
                if last:
                    ins.then_inc(sem("z_act"), 1)

            def bc_copy(name):
                act.wait_ge(sem("norm_bc"), before("bc", name) + 1)
                A(bcs[:, :], ps[7][:, T:2 * T], ACT.Copy).then_inc(sem("norm_bcs"), 1)

            for k in range(2):
                act.wait_ge(sem(("x_in", "x_in2")[k]), 16)
                A(sq1[:, 4 * k:4 * k + 4, :], x[:, 4 * k:4 * k + 4, :], ACT.Square).then_inc(sem("norm_sq"), 1)
            act.wait_ge(sem("par_in"), 16)
            split_hi(0)
            for k in range(4):
                gained_hi("n1", "mix_pre", 0, k)
            split_hi(1)
            split_hi(2)
            bc_copy("n1")
            act.wait_ge(sem("gam_sub"), 1)
            A(lb[:, 1, :], lb[:, 0, :], ACT.Exp).then_inc(sem("gam_exp"), 1)

            ahead(U_ZV)
            ahead(U_ZV + 1)
            filled(U_ZV + 1)
            act.wait_ge(sem("rtok"), 1)
            for s in range(2):
                evac(U_ZV + s, zv[:, s, :], ACT.Gelu, scale=rtok[:, 0, s:s + 1])
            for m in range(2):
                u = U_ZU + m
                ahead(u)
                activated(u, zu[:, 2 * m:2 * m + 2, :], ACT.Gelu)
            steps = hgrn_schedule()

            def hgrn_act(kind, g, lv):
                H = G[g]
                if kind == "level" and lv in (0, 8):
                    act.wait_ge(sem(f"lv_mm{g}"), lv + 1)
                    for s in range(2):
                        cols = (s if lv == 0 else 1 - s) * P
                        A(H["S"][:, s, :, cols:cols + P], ps[3 + 2 * g + s][:, :].rearrange("p (h t) -> p h t", h=4),
                          ACT.Copy).then_inc(sem(f"lv_copy{g}"), 1)
                if kind == "pv":
                    act.wait_ge(sem(f"pv_mm{g}"), 1)
                    for s in range(2):
                        src = ps[3 + 2 * g + s][:, :].rearrange("p (h t) -> p h t", h=2)
                        A(H["q"][:, 2 * s:2 * s + 2, :], src, ACT.Copy)
                        A(sqo[g][:, 2 * s:2 * s + 2, :], src, ACT.Square).then_inc(sem(f"o_sq{g}"), 1)

            for u in range(4, 32):
                ahead(u)
                if u < U_ZI:
                    g, r = divmod(u - 4, 6)
                    part, m = divmod(r, 2)
                    H = G[g]
                    if part == 0:
                        activated(u, H["q"][:, 2 * m:2 * m + 2, :], ACT.Silu)
                    else:
                        F_, K_ = (H[n][part - 1][:, 2 * m:2 * m + 2, :] for n in ("F", "K"))
                        activated(u, F_, ACT.Sigmoid, source=K_)
                        act.wait_ge(sem("z_act"), z_index(u) + 1)
                        A(K_, K_, ACT.Sigmoid, scale=-1.0).then_inc(sem("z_k"), 1)
                        act.wait_ge(sem("lb"), 1)
                        act.wait_ge(sem("z_k"), k_index(u) + 1)
                        for h in (2 * m, 2 * m + 1):
                            c = 8 * (part - 1) + 4 * g + h
                            A(H["F"][part - 1][:, h, :], H["F"][part - 1][:, h, :], ACT.Identity, scale=lb[:, 2, c:c + 1],
                              bias=lb[:, 0, c:c + 1])
                            ins = A(H["K"][part - 1][:, h, :], H["K"][part - 1][:, h, :], ACT.Copy, scale=lb[:, 2, c:c + 1])
                        ins.then_inc(sem("gates"), 1)
                elif u < U_GA:
                    if (u - U_ZI) % 2 == 1:
                        filled(u)
                        half = (u - U_ZI) // 2
                        for s in range(2):
                            evac(u - 1 + s, zi[:, s, half * 512:half * 512 + 512], ACT.Copy, scale=rtok[:, 0, s:s + 1])
                else:
                    dst, func, m = ((ga, ACT.Sigmoid, u - U_GA) if u < U_ZG else
                                    (zg, ACT.Silu, u - U_ZG) if u < U_GB else (gb, ACT.Sigmoid, u - U_GB))
                    activated(u, dst[:, 2 * m:2 * m + 2, :], func)
                for step in steps.get(u, ()):
                    hgrn_act(*step)
                if u == U_GB + 2:
                    split_x("a", afull, 8, 2, 1)
            filled(U_GB + 3)
            for k in range(2):
                A(xh[:, 2 * k:2 * k + 2, :], bout[:, 2 * k:2 * k + 2, :], ACT.Copy).then_inc(sem("act_hi"), 1)
            for u in range(U_WA, U_WOUT):
                ahead(u)
            split_x("m", merged, 8, 4, 1)
            for m in range(4):
                u = U_WOUT + m
                ahead(u)
                filled(u)
                A(sq2[:, 2 * m:2 * m + 2, :], two(ps[u % RING][:, :]), ACT.Square)
                for t in range(2):
                    ins = A(mix[:, 2 * m + t, :], ps[u % RING][:, t * T:(t + 1) * T], ACT.Copy, scale=col("mix_post", 2 * m + t))
                ins.then_inc(sem(f"evac{u % RING}"), 1)
                if m == 1:
                    act.wait_ge(sem("p_in"), 16)
                    A(xh[:, 6:8, :], pT_s, ACT.Copy).then_inc(sem("act_hi"), 1)
            for k in range(4):
                act.wait_ge(sem("n2_x"), k + 1)
                gained_hi("n3", "ffn_pre", 8, k)
                A(sq3[:, 2 * k:2 * k + 2, :], x[:, 2 * k:2 * k + 2, :], ACT.Square).then_inc(sem("norm_sq"), 1)
            ahead(U_PLE)
            filled(U_PLE)
            for b in range(4):
                A(plx[:, 2 * b:2 * b + 2, :], two(ps[3 + b][:, :]), ACT.Copy).then_inc(sem("ple_copy"), 1)

            def silu_pair(j):
                act.wait_ge(sem("gate_r"), j + 1)
                A(silu, silu, ACT.Silu).then_inc(sem("silu"), 1)

            def hidden_hi(j, hidden_name, tile, slot_h):
                act.wait_ge(sem(hidden_name + "_y"), j + 1)
                A(xh[:, tile:tile + 2, :], hid[slot_h], ACT.Copy).then_inc(sem(hidden_name + "_hi"), 1)

            def split_at(i, k):
                split_hi(6 * i + k, k % RING, 2 * i + k // RING)

            split_hi(U_F1 + RING)
            bc_copy("n3")
            split_hi(U_F1 + 1 + RING)
            silu_pair(0)
            hidden_hi(0, "hid", 0, 0)
            with act.Fori(0, (PAIRS1 - 1) // 2) as i:
                for c in range(2):
                    k = U_F1 + 2 + 3 * c
                    split_at(i, k + RING)
                    silu_pair(2 * i + (1 + c))
                    split_at(i, k + 1 + RING)
                    hidden_hi(2 * i + (1 + c), "hid", 2 * ((1 + c) % 2), (1 + c) % 2)
                    split_at(i, k + 2 + RING)
            for b in range(4):
                if b < 3:
                    act.wait_ge(sem("ff_bank"), b + 1)
                else:
                    filled(U_PG - 1)
                A(sq2[:, 2 * b:2 * b + 2, :], two(ps[3 + b][:, :]), ACT.Square).then_inc(sem("norm_sq"), 1)
            ahead(U_PG - 1)
            bc_copy("n4")

            for k in range(4):
                act.wait_ge(sem("ff_x"), k + 1)
                A(xh[:, 2 * k:2 * k + 2, :], x[:, 2 * k:2 * k + 2, :], ACT.Copy).then_inc(sem("act_hi"), 1)
            for m in range(4):
                u = U_PG + m
                ahead(u)
                if m:
                    act.wait_ge(sem("pg_x"), m)
                    gained_hi("n5", "mix2", 8, m - 1)
                    A(sq3[:, 2 * m - 2:2 * m, :], x[:, 2 * m - 2:2 * m, :], ACT.Square).then_inc(sem("norm_sq"), 1)
                filled(u)
                evac(u, sgate[:, m % 2, :], ACT.Sigmoid)
            act.wait_ge(sem("pg_x"), 4)
            gained_hi("n5", "mix2", 8, 3)
            A(sq3[:, 6:8, :], x[:, 6:8, :], ACT.Square).then_inc(sem("norm_sq"), 1)

            for m in range(4):
                u = U_CQ + m
                ahead(u)
                if m == 1:
                    bc_copy("n5")
                if m:
                    act.wait_ge(sem(f"evac{(u - 1) % RING}"), FILLS[u - 1][(u - 1) % RING] + 1)
                    A(sqc[:, 2 * m - 2:2 * m, :], c8[:, 2 * m - 2:2 * m, :], ACT.Square).then_inc(sem("c_sq"), 1)
            u = U_CKV
            act.wait_ge(sem(f"evac{u % RING}"), FILLS[u][u % RING] + 1)
            A(sqc[:, 6:8, :], c8[:, 6:8, :], ACT.Square).then_inc(sem("c_sq"), 1)
            for m in range(4):
                u = U_QA + m
                if m >= 2:
                    act.wait_ge(sem("norm_bc"), before("bc", "c") + m - 1)
                    A(bcs2, ps[7][:, T:2 * T], ACT.Copy).then_inc(sem("norm_bcs"), 1)
                ahead(u)
                act.wait_ge(sem(f"evac{u % RING}"), FILLS[u][u % RING] + 1)
                A(sqA[:, 2 * m:2 * m + 2, :], (qa if m < 2 else ka)[:, 2 * (m % 2):2 * (m % 2) + 2, :], ACT.Square)\
                    .then_inc(sem("qk_sq"), 1)
            act.wait_ge(sem("ang"), 1)
            A(sink[64:96, 0, :], red[64:96, 0, :], ACT.Sin).then_inc(sem("sin"), 1)
            act.wait_ge(sem("ang"), 2)
            A(cosk[64:96, 0, :], ang[64:96, 0, :], ACT.Sin).then_inc(sem("sin"), 1)
            split_x("c", yc, 0, 2, 1)
            ahead(U_VA)
            ahead(U_VA + 1)
            filled(U_VA + 1)
            for s in range(2):
                evac(U_VA + s, va[:, s, :], ACT.Copy, scale=rtok[:, 4, s:s + 1])

            def head_pair_filled(name, half, u):
                if half == 3:
                    filled(u)
                else:
                    act.wait_ge(sem(name + "_mm"), half + 1)

            def softmax_exp(p):
                act.wait_ge(sem("head_max"), p + 1)
                for hh in range(2):
                    for s in range(2):
                        sl = slice(0, P) if s == 0 else slice(P, 384)
                        k = 2 * hh + s
                        A(probs[:, 2 * (p % 2) + hh, sl], probs[:, 2 * (p % 2) + hh, sl], ACT.Exp,
                          bias=smx[:, 1, k:k + 1], accum_out=smx[:, 2, k:k + 1]).then_inc(sem("head_exp"), 1)

            def probs_copy(p):
                act.wait_ge(sem("head_tr"), p + 1)
                for hh in range(2):
                    A(probsT[:, 2 * (p % 2) + hh, :], ps[5 + hh][:, 0:384], ACT.Copy).then_inc(sem("head_trc"), 1)

            def heads_hi(p):
                act.wait_ge(sem("head_pv"), p + 1)
                A(xh[:, 8 + p, :], ps[7][:, 0:T], ACT.Copy).then_inc(sem("head_mh"), 1)

            u = U_KR
            ahead(u)
            act.wait_ge(sem("evac0"), FILLS[u][0] + 1)
            act.wait_ge(sem("act_lo"), before("lo", "c") + 2)
            A(sqk[64:96, :, :], kr[64:96, 0:1, :].broadcast_to([32, HEADS, T]), ACT.Square).then_inc(sem("kr_sq"), 1)
            filled(u)
            evac(u, vb[:, 0, :], ACT.Copy, b=1)
            evac(u, vb[:, 1, :], ACT.Copy, b=2)
            softmax_exp(0)
            for n in range(4):
                u = U_UK + n
                if n:
                    ahead(u)
                else:
                    for half in range(4):
                        if half == 3:
                            ahead(u)
                        head_pair_filled("uk", half, U_UK)
                        b = (U_UK + half) % RING
                        src = ps[b][0:64, :].rearrange("p (h t) -> p h t", h=2)
                        hs = slice(2 * half, 2 * half + 2)
                        A(sqk[0:64, hs, :], src, ACT.Square)
                        A(kb[0:64, hs, :], src, ACT.Copy, scale=col("kb", 0, 0, 64)).then_inc(sem("uk_ev"), 1)
                    probs_copy(0)
                    softmax_exp(1)
                    continue
                for half in ((0,), (1,), (2, 3))[n - 1]:
                    head_pair_filled("uq", half, U_UQ + 2)
                    b = half % RING
                    src = ps[b][0:96, :].rearrange("p (h t) -> p h t", h=2)
                    hs = slice(2 * half, 2 * half + 2)
                    if half == 0:
                        act.wait_ge(sem("act_lo"), before("lo", "c") + 2)
                    A(sqq[0:96, hs, :], src, ACT.Square)
                    A(qsw[64:96, hs, :], ps[b][96:128, :].rearrange("p (h t) -> p h t", h=2), ACT.Copy)
                    A(qb[0:96, hs, :], src, ACT.Copy, scale=col("qb", 0, 0, 96)).then_inc(sem("uq_ev"), 1)
                if n == 1:
                    heads_hi(0)
                    probs_copy(1)
                    softmax_exp(2)
                elif n == 2:
                    heads_hi(1)
                    probs_copy(2)
                    softmax_exp(3)
                else:
                    heads_hi(2)
                    probs_copy(3)
                    heads_hi(3)
            for p in range(6):
                if 1 <= p < 5:
                    probs_copy(p + 3)
                if p < 4:
                    softmax_exp(4 + p)
                if p >= 2:
                    heads_hi(p + 2)
            for m in range(4):
                ahead(U_WO + m)
                act.wait_ge(sem("wo_x"), m + 1)
                gained_hi("n6", "ffn2", 0, m)
                A(sq3[:, 2 * m:2 * m + 2, :], x[:, 2 * m:2 * m + 2, :], ACT.Square).then_inc(sem("norm_sq"), 1)

            def relu_pair(j, u, bank):
                act.wait_ge(sem("unit_used"), u + 1)
                if not isinstance(j, int) or j >= 1:
                    act.wait_ge(sem("hid2_y"), j)
                A(silu, ps[bank][:, :], ACT.Relu).then_inc(sem("relu"), 1)

            split_hi(U_F2 + RING)
            relu_pair(0, U_F2, U_F2 % RING)
            hidden_hi(0, "hid2", 8, 0)
            bc_copy("n6")
            with act.Fori(0, (PAIRS2 - 1) // 3 - 1) as i:
                for c in range(3):
                    k = U_F2 + 1 + 2 * c
                    split_at(i, k + RING)
                    relu_pair(3 * i + (1 + c), 6 * i + k, k % RING)
                    hidden_hi(3 * i + (1 + c), "hid2", 8 + 2 * ((1 + c) % 3), (1 + c) % 3)
                    split_at(i, k + 1 + RING)
            for j in range(PAIRS2 - 3, PAIRS2):
                u = U_F2 + 2 * j - 1
                ahead(u)
                relu_pair(j, u, u % RING)
                hidden_hi(j, "hid2", 8 + 2 * (j % 3), j % 3)
                ahead(u + 1)

        @block.vector
        def _(dve):
            V = nc.vector
            chained = [0]

            def count(ins):
                chained[0] += 1
                ins.then_inc(sem("dve_chain"), 1)

            def link(ins):
                count(ins)
                dve.wait_ge(sem("dve_chain"), chained[0])

            def split_lo(u, slot=None):
                slot = u % RING if slot is None else slot
                dve.wait_ge(sem("hi_ready"), u + 1)
                V.tensor_tensor(wlo[:, slot, :], raw[:, slot, :], whi[:, slot, :].bitcast(F32), ALU.subtract)\
                    .then_inc(sem("lo_ready"), 1)

            def ahead(u):
                if u + RING < UNITS:
                    split_lo(u + RING)

            def evacuated(u):
                b = u % RING
                dve.wait_ge(sem(f"evac{b}"), FILLS[u][b] + 1)

            def rsqrt(src, dst, n):
                v, y, a, b2 = (nt[:, i, 0:n] for i in range(4))
                link(V.tensor_scalar(v, src, EPS, None, ALU.add))
                link(V.tensor_scalar(nti[:, 0:n], v.bitcast(I32), 1, None, ALU.logical_shift_right))
                link(V.tensor_scalar(y.bitcast(I32), nti[:, 0:n], -1.0, 1597463007.0, ALU.mult, ALU.add))
                for it in range(3):
                    link(V.tensor_tensor(a, y, y, ALU.mult))
                    link(V.scalar_tensor_tensor(b2, a, -0.5, v, ALU.mult, ALU.mult))
                    o = dst if it == 2 else y
                    link(V.scalar_tensor_tensor(o, b2, 1.5, y, ALU.add, ALU.mult))

            def norm_factors(name, n, k=0):
                dve.wait_ge(sem("norm_stats"), before("st", name) + k + 1)
                V.tensor_scalar(eps_s[:, :], ps[7][:, 0:2], EPS, None, ALU.add).then_inc(sem("eps_added"), 1)
                dve.wait_ge(sem("rtok"), n + 1)
                V.tensor_copy(rx[:, :, :], rtok[:, n, :].unsqueeze(2).broadcast_to([P, 2, P])).then_inc(sem("norm_factors"), 1)

            def gained_lo(name, gain, dst, k):
                dve.wait_ge(sem("act_hi"), before("hi", name) + k + 1)
                for t in (2 * k, 2 * k + 1):
                    ins = V.scalar_tensor_tensor(xl[:, dst + t, :], x[:, t, :], col(gain, t), xh[:, dst + t, :].bitcast(F32),
                                                 ALU.mult, ALU.subtract)
                ins.then_inc(sem("act_lo"), 1)

            def factors_by_tile(n):
                return bcs[:, :].unsqueeze(1).broadcast_to([P, n, T])

            def scaled(u, dst):
                dve.wait_ge(sem("unit_used"), u + 1)
                V.tensor_tensor(dst, two(ps[u % RING][:, :]), factors_by_tile(2), ALU.mult).then_inc(sem(f"evac{u % RING}"), 1)

            def activated(u):
                dve.wait_ge(sem("z_act"), z_index(u) + 1)

            def split_x(name, y, dst, groups):
                for k in range(groups):
                    t = y.shape[1] // groups
                    dve.wait_ge(sem("act_hi"), before("hi", name) + k + 1)
                    V.tensor_tensor(xl[:, dst + k * t:dst + (k + 1) * t, :], y[:, k * t:(k + 1) * t, :],
                                    xh[:, dst + k * t:dst + (k + 1) * t, :].bitcast(F32), ALU.subtract)\
                        .then_inc(sem("act_lo"), 1)

            dve.wait_ge(sem("par_in"), 16)
            dve.wait_ge(sem("x_in"), 16)
            dve.wait_ge(sem("x_in2"), 16)
            split_lo(0)
            for k in range(4):
                gained_lo("n1", "mix_pre", 0, k)
            norm_factors("n1", 0)
            split_lo(1)
            gam = par_s[:, PAR["gamma"]:PAR["gamma"] + 16]
            V.tensor_tensor(lb[:, 0, :], gam, gam, ALU.subtract).then_inc(sem("gam_sub"), 1)
            split_lo(2)
            dve.wait_ge(sem("gam_exp"), 1)
            link(V.reciprocal(lb[:, 0, :], lb[:, 1, :]))
            link(V.tensor_tensor(lb[:, 1, :], lb[:, 1, :], lb[:, 0, :], ALU.mult))
            link(V.tensor_tensor(lb[:, 0, :], lb[:, 1, :], lb[:, 1, :], ALU.subtract))
            V.tensor_scalar(lb[:, 2, :], lb[:, 0, :], -1.0, 1.0, ALU.mult, ALU.add).then_inc(sem("lb"), 1)

            ahead(0)
            ahead(1)
            dve.wait_ge(sem("sg_in"), 16)
            bn = nt[:, 0, 0:12].rearrange("p (s n) -> p s n", s=2)
            mv = rs[:, 0:4].rearrange("p (s n) -> p s n", s=2)
            for s in range(2):
                evacuated(U_ZV + s)
                link(V.bn_stats(bn[:, s, :], zv[:, s, :]))
            for s in range(2):
                link(V.bn_aggr(mv[:, s, :], bn[:, s, :]))
            rsqrt(mv[:, :, 1], rs[:, 8:10], 2)
            for s in range(2):
                link(V.tensor_scalar(zv[:, s, :], zv[:, s, :], mv[:, s, 0:1], rs[:, 8 + s:9 + s], ALU.subtract, ALU.mult))
                link(V.tensor_tensor(zv[:, s, :], zv[:, s, :], lnr_s[:, 0, :], ALU.mult))
                V.tensor_tensor(vn[:, s, :], zv[:, s, :], lnr_s[:, 1, :], ALU.add).then_inc(sem("vn"), 1)

            steps = hgrn_schedule()

            def gates(g, part, m):
                dve.wait_ge(sem("gates"), k_index(U_Q[g] + 2 + 2 * part + m) + 1)
                fm = G[g]["F"][part][:, 2 * m:2 * m + 2, :]
                link(V.tensor_scalar(fm, fm, TINY, 1.0, ALU.max, ALU.min))

            def decay(g, d, level):
                if level == 0:
                    return G[g]["F"][d].rearrange("p h t -> p (h t)")
                if level == 1:
                    return t1[:, d, :]
                at = sum(4 * T >> i for i in range(2, level))
                return G[g]["F"][d].rearrange("p h t -> p (h t)")[:, at:at + (4 * T >> level)]

            def tree_update(g, lv):
                H = G[g]
                half = 1 << (lv - 1)
                for d in range(2):
                    pair = decay(g, d, lv - 1).rearrange("p (n two) -> p n two", two=2)
                    if lv < 7:
                        count(V.tensor_tensor(decay(g, d, lv), pair[:, :, 0], pair[:, :, 1], ALU.mult))
                    n = 4 * T // (2 * half)
                    for X, side in ((H["Q"][d], 1 - d), (H["K"][d], d)):
                        v = X.rearrange("p h (n two w) -> p (h n) two w", two=2, w=half)[:, :, side, :]
                        dec = pair[:, :, 1 - side:2 - side].broadcast_to([P, n, half])
                        last = V.tensor_tensor(v, v, dec, ALU.mult)
                        if d == 0 or X is H["Q"][d]:
                            count(last)
                last.then_inc(sem(f"tree{g}"), 1)
                dve.wait_ge(sem(f"tree{g}"), lv)

            def hgrn_dve(kind, g, lv):
                H = G[g]
                if kind == "prep":
                    activated(U_Q[g] + 1)
                    for d in range(2):
                        V.tensor_tensor(H["Q"][d], H["q"], H["F"][d], ALU.mult).then_inc(sem(f"q_init{g}"), 1)
                if kind == "level" and 1 <= lv <= 7:
                    dve.wait_ge(sem(f"lv_mm{g}"), lv + 1)
                    dve.wait_ge(sem("lvl_in"), 16)
                    if lv == 1:
                        dve.wait_ge(sem(f"lv_copy{g}"), 2)
                        dve.wait_ge(sem(f"q_init{g}"), 2)
                    for s in range(2):
                        V.copy_predicated(H["S"][:, s, :, s * P:(s + 1) * P],
                                          lvl_s[:, lv - 1, :].unsqueeze(1).broadcast_to([P, 4, P]),
                                          ps[3 + 2 * g + s][:, :].rearrange("p (h t) -> p h t", h=4))\
                            .then_inc(sem(f"lv_pred{g}"), 1)
                    dve.wait_ge(sem(f"lv_pred{g}"), 2 * lv)
                    tree_update(g, lv)

            dve.wait_ge(sem("norm_bcs"), 1)
            for u in range(2, 32):
                if u < U_Q[0]:
                    scaled(u, zu[:, 2 * (u - U_ZU):2 * (u - U_ZU) + 2, :])
                elif u < U_ZI:
                    g, r = divmod(u - 4, 6)
                    part, m = divmod(r, 2)
                    area = G[g]["K"][part - 1] if part else G[g]["q"]
                    scaled(u, area[:, 2 * m:2 * m + 2, :])
                elif u >= U_GA:
                    if u == U_GA:
                        dve.wait_ge(sem("lv_mm0"), 9)
                    area, m = (ga, zg, gb)[(u - U_GA) // 4], (u - U_GA) % 4
                    scaled(u, area[:, 2 * m:2 * m + 2, :])
                if U_Q[0] <= u < U_ZI and (u - 4) % 6 == 5:
                    gates((u - 4) // 6, 1, 1)
                    hgrn_dve("prep", (u - 4) // 6, 0)
                for step in steps.get(u, ()):
                    hgrn_dve(*step)
                ahead(u)
                if u == U_ZU + 1:
                    dve.wait_ge(sem("sgb_in"), 16)
                if u == 5:
                    for b in range(2):
                        dve.wait_ge(sem("sg_mm"), b + 1)
                        s2 = sgb_s[:, 2 * b:2 * b + 2, :].unsqueeze(2).broadcast_to([P, 2, 2, P])
                        o4 = bout[:, 2 * b:2 * b + 2, :].rearrange("p j (s t) -> p j s t", s=2)
                        link(V.tensor_tensor(o4, ps[3 + b][:, :].rearrange("p (j s t) -> p j s t", j=2, s=2), s2, ALU.add))
                    activated(U_ZU + 1)
                    V.tensor_tensor(bout, bout, zu, ALU.mult).then_inc(sem("b_out"), 1)
                if 4 <= u < U_ZI:
                    g, r = divmod(u - 4, 6)
                    part, m = divmod(r, 2)
                    if part and r < 5:
                        gates(g, part - 1, m)
                if u == U_GB:
                    dve.wait_ge(sem("norm_stats"), before("st", "o") + 1)
                    rsqrt(ps[7][:, 0:16], rs[:, 0:16], 16)
                    V.tensor_copy(rxo, rs[:, 0:16].unsqueeze(2).broadcast_to([P, 16, P])).then_inc(sem("norm_factors"), 1)
                if u == U_GB + 2:
                    for h in range(HEADS):
                        if h % 2 == 0:
                            dve.wait_ge(sem("norm_bc"), before("bc", "o") + h // 2 + 1)
                        link(V.scalar_tensor_tensor(afull[:, h, :], G[h // 4]["q"][:, h % 4, :], col("hg_norm", h),
                                                    ps[3 + h // 2][:, (h % 2) * T:(h % 2 + 1) * T], ALU.mult, ALU.mult))
                    activated(U_ZG + 3)
                    for k in range(2):
                        V.tensor_tensor(afull[:, 4 * k:4 * k + 4, :], afull[:, 4 * k:4 * k + 4, :],
                                        zg[:, 4 * k:4 * k + 4, :], ALU.mult).then_inc(sem("act_y"), 1)
                    split_x("a", afull, 8, 2)
            for k in range(2):
                dve.wait_ge(sem("act_hi"), before("hi", "b") + k + 1)
                V.tensor_tensor(xl[:, 2 * k:2 * k + 2, :], bout[:, 2 * k:2 * k + 2, :],
                                xh[:, 2 * k:2 * k + 2, :].bitcast(F32), ALU.subtract).then_inc(sem("act_lo"), 1)
            def merged_lo(k):
                dve.wait_ge(sem("act_hi"), before("hi", "m") + k + 1)
                V.tensor_tensor(xl[:, 8 + 2 * k:10 + 2 * k, :], merged[:, 2 * k:2 * k + 2, :],
                                xh[:, 8 + 2 * k:10 + 2 * k, :].bitcast(F32), ALU.subtract).then_inc(sem("act_lo"), 1)

            activated(U_GB + 3)
            for m in range(4):
                u = U_WA + m
                ahead(u)
                dve.wait_ge(sem("unit_used"), u + 1)
                V.tensor_tensor(ga[:, 2 * m:2 * m + 2, :], ga[:, 2 * m:2 * m + 2, :], two(ps[u % RING][:, :]),
                                ALU.mult).then_inc(sem(f"evac{u % RING}"), 1)
            for n in range(2):
                u = U_WB + n
                ahead(u)
                dve.wait_ge(sem("unit_used"), u + 1)
                if n == 0:
                    for m in range(4):
                        evacuated(U_WA + m)
                for b in range(2):
                    t = slice(4 * n + 2 * b, 4 * n + 2 * b + 2)
                    link(V.tensor_tensor(mtmp[:, t, :], gb[:, t, :], two(ps[3 + 2 * n + b][:, :]), ALU.mult))
                    V.tensor_tensor(merged[:, t, :], mtmp[:, t, :], ga[:, t, :], ALU.add).then_inc(sem("act_y"), 1)
                    if 2 * n + b:
                        merged_lo(2 * n + b - 1)
            merged_lo(3)
            for m in range(4):
                ahead(U_WOUT + m)
                if m == 2:
                    dve.wait_ge(sem("act_hi"), before("hi", "p") + 1)
                    V.tensor_tensor(xl[:, 6:8, :], pT_s, xh[:, 6:8, :].bitcast(F32), ALU.subtract).then_inc(sem("act_lo"), 1)
            norm_factors("n2", 1)
            dve.wait_ge(sem("norm_bc"), before("bc", "n2") + 1)
            fac = ps[7][:, T:2 * T].unsqueeze(1).broadcast_to([P, 2, T])
            for k in range(4):
                t = slice(2 * k, 2 * k + 2)
                V.tensor_tensor(tmp2[:, t, :], mix[:, t, :], fac, ALU.mult).then_inc(sem("act_y"), 1)
                dve.wait_ge(sem("act_y"), before("y", "n2") + k + 1)
                V.tensor_tensor(x[:, t, :], x[:, t, :], tmp2[:, t, :], ALU.add).then_inc(sem("n2_x"), 1)
                if k:
                    gained_lo("n3", "ffn_pre", 8, k - 1)
            gained_lo("n3", "ffn_pre", 8, 3)
            ahead(U_PLE)

            def gate_scaled(j, u, bank):
                dve.wait_ge(sem("unit_used"), u + 1)
                if not isinstance(j, int) or j >= 1:
                    dve.wait_ge(sem("gated"), j)
                V.tensor_tensor(two(silu), two(ps[bank][:, :]), factors_by_tile(2), ALU.mult).then_inc(sem("gate_r"), 1)

            def hidden(j, slot_h, u_up, bank):
                dve.wait_ge(sem("silu"), j + 1)
                if not isinstance(j, int) or j >= 1:
                    dve.wait_ge(sem("hid_y"), j)
                V.tensor_tensor(two(gated), two(silu), factors_by_tile(2), ALU.mult).then_inc(sem("gated"), 1)
                dve.wait_ge(sem("unit_used"), u_up + 1)
                dve.wait_ge(sem("gated"), j + 1)
                if not isinstance(j, int) or j >= 1:
                    dve.wait_ge(sem("hid_lo"), j)
                V.tensor_tensor(hid[slot_h], two(gated), two(ps[bank][:, :]), ALU.mult).then_inc(sem("hid_y"), 1)

            def hidden_lo(j, slot_h, hidden_name, base):
                dve.wait_ge(sem(hidden_name + "_hi"), j + 1)
                V.tensor_tensor(xl[:, base + 2 * slot_h:base + 2 * slot_h + 2, :], hid[slot_h],
                                xh[:, base + 2 * slot_h:base + 2 * slot_h + 2, :].bitcast(F32), ALU.subtract)\
                    .then_inc(sem(hidden_name + "_lo"), 1)

            split_lo(U_F1 + RING)
            norm_factors("n3", 2)
            split_lo(U_F1 + 1 + RING)
            dve.wait_ge(sem("norm_bcs"), before("bcs", "n3") + 1)
            gate_scaled(0, U_F1, U_F1 % RING)
            hidden(0, 0, U_F1 + 1, (U_F1 + 1) % RING)
            hidden_lo(0, 0, "hid", 0)
            with dve.Fori(0, (PAIRS1 - 1) // 2) as i:
                for c in range(2):
                    j = 2 * i + (1 + c)
                    u = 6 * i + (U_F1 + 2 + 3 * c)
                    s0 = (U_F1 + 2) % RING
                    gate_scaled(j, u, s0)
                    split_lo(u + RING, s0)
                    split_lo(u + 1 + RING, (s0 + 1) % RING)
                    hidden(j, (1 + c) % 2, u + 1, (s0 + 1) % RING)
                    hidden_lo(j, (1 + c) % 2, "hid", 0)
                    split_lo(u + 2 + RING, (s0 + 2) % RING)
            def x_lo(k):
                dve.wait_ge(sem("act_hi"), before("hi", "ff") + k + 1)
                V.tensor_tensor(xl[:, 2 * k:2 * k + 2, :], x[:, 2 * k:2 * k + 2, :], xh[:, 2 * k:2 * k + 2, :].bitcast(F32),
                                ALU.subtract).then_inc(sem("act_lo"), 1)

            ahead(U_PG - 1)
            norm_factors("n4", 3)
            dve.wait_ge(sem("norm_bcs"), before("bcs", "n4") + 1)
            for k in range(4):
                for t in range(2):
                    ins = V.scalar_tensor_tensor(tmp2[:, 2 * k + t, :], ps[3 + k][:, t * T:(t + 1) * T], col("ffn_post", 2 * k + t),
                                                 bcs[:, :], ALU.mult, ALU.mult)
                    if t == 0:
                        count(ins)
                ins.then_inc(sem("act_y"), 1)
                dve.wait_ge(sem("act_y"), before("y", "n4") + k + 1)
                V.tensor_tensor(x[:, 2 * k:2 * k + 2, :], x[:, 2 * k:2 * k + 2, :], tmp2[:, 2 * k:2 * k + 2, :], ALU.add)\
                    .then_inc(sem("ff_x"), 1)
                if k:
                    x_lo(k - 1)
            x_lo(3)
            dve.wait_ge(sem("ple_copy"), 4)
            for m in range(4):
                u = U_PG + m
                ahead(u)
                evacuated(u)
                if m == 0:
                    dve.wait_ge(sem("ff_x"), 4)
                    dve.wait_ge(sem("act_lo"), before("lo", "ff") + 4)
                else:
                    dve.wait_ge(sem("pg_x"), m)
                link(V.tensor_tensor(two(gtmp),
                                     two(sgate[:, m % 2, :]), plx[:, 2 * m:2 * m + 2, :], ALU.mult))
                V.tensor_tensor(x[:, 2 * m:2 * m + 2, :], x[:, 2 * m:2 * m + 2, :],
                                two(gtmp), ALU.add).then_inc(sem("pg_x"), 1)
                if m:
                    gained_lo("n5", "mix2", 8, m - 1)
                if m == 0:
                    dve.wait_ge(sem("oneh_in"), 16)
                    V.memset(rel_s[0:33, 0, 0:HEADS], 1.0).then_inc(sem("rel_one"), 1)
                if m == 3:
                    dve.wait_ge(sem("bv_mm"), 1)
                    V.tensor_copy(bvec[0:HEADS, 0, :], ps[3][0:HEADS, :]).then_inc(sem("bvec"), 1)
            gained_lo("n5", "mix2", 8, 3)
            ahead(U_CQ)
            norm_factors("n5", 4)
            ahead(U_CQ + 1)
            dve.wait_ge(sem("norm_bcs"), before("bcs", "n5") + 1)
            for m in range(4):
                scaled(U_CQ + m, c8[:, 2 * m:2 * m + 2, :])
                if m >= 2:
                    ahead(U_CQ + m)
            scaled(U_QA, qa[:, 0:2, :])
            ahead(U_QA)
            norm_factors("c", 5)
            scaled(U_QA + 1, qa[:, 2:4, :])
            ahead(U_QA + 1)
            dve.wait_ge(sem("pos_in"), 16)
            a_, r_, c_ = ang[64:96, 0, :], red[64:96, 0, :], cosk[64:96, 0, :]
            link(V.tensor_copy(r_, a_.bitcast(I32)))
            link(V.tensor_scalar(a_, r_, cst_s[64:96, C_INVF:C_INVF + 1], None, ALU.mult))
            link(V.tensor_scalar(c_, a_, 1.0 / (2 * np.pi), 12582912.0, ALU.mult, ALU.add))
            link(V.tensor_scalar(c_, c_, 12582912.0, None, ALU.subtract))
            for part in TWO_PI:
                link(V.scalar_tensor_tensor(a_, c_, -part, a_, ALU.mult, ALU.add))
            lim = 3.1415925
            V.tensor_scalar(r_, a_, lim, -lim, ALU.min, ALU.max).then_inc(sem("ang"), 1)
            link(V.tensor_scalar(a_, a_, float(np.pi / 2), None, ALU.add))
            link(V.tensor_scalar(c_, a_, float(np.pi), -2 * float(np.pi), ALU.is_gt, ALU.mult))
            link(V.tensor_tensor(a_, a_, c_, ALU.add))
            V.tensor_scalar(a_, a_, lim, -lim, ALU.min, ALU.max).then_inc(sem("ang"), 1)
            for n, (gain, tiles, at) in enumerate((("cq", 6, 0), ("ckv", 2, 6))):
                dve.wait_ge(sem("norm_bcs"), before("bcs", "c") + n + 1)
                for k in range(tiles):
                    ins = V.scalar_tensor_tensor(yc[:, at + k, :], c8[:, at + k, :], col(gain, k), bcs2, ALU.mult, ALU.mult)
                    if (at + k) % 4 == 3:
                        ins.then_inc(sem("act_y"), 1)
                    else:
                        count(ins)
                if n == 0:
                    norm_factors("c", 6, 1)
                scaled(U_KA + n, ka[:, 2 * n:2 * n + 2, :])
                ahead(U_KA + n)
            split_x("c", yc, 0, 2)
            dve.wait_ge(sem("sin"), 2)
            sgn = cst_s[64:96, C_SIGN:C_SIGN + 1]
            link(V.tensor_copy(cosq[64:96, 0, :], cosk[64:96, 0, :]))
            link(V.tensor_scalar(sinq[64:96, 0, :], sink[64:96, 0, :], col("qb_swap", 0, 64, 96), sgn, ALU.mult, ALU.mult))
            link(V.tensor_scalar(sink[64:96, 0, :], sink[64:96, 0, :], col("kb_swap", 0, 64, 96), sgn, ALU.mult, ALU.mult))

            def head_factors(name, width, kx):
                dve.wait_ge(sem("norm_stats"), before("st", name) + 1)
                rsqrt(ps[7][:, 0:32], rs[:, 0:32], 32)
                r3 = rs[:, 0:32].rearrange("p (s h) -> p s h", s=2)
                link(V.tensor_copy(kx, r3[:, :, 8:16].unsqueeze(3).broadcast_to([P, 2, HEADS, width])))
                V.tensor_scalar(r3[:, :, 0:8], r3[:, :, 0:8], float(np.float32(1.0 / np.sqrt(width))), None, ALU.mult)\
                    .then_inc(sem("norm_factors"), 1)

            def logits_row(p):
                dve.wait_ge(sem("head_qk"), p + 1)
                if p >= 2:
                    dve.wait_ge(sem("head_tr"), p - 1)
                for hh in range(2):
                    h = 2 * (p % 4) + hh
                    L = probs[:, 2 * (p % 2) + hh, :]
                    tab = bias_table(h) if p < 4 else mask_table()
                    V.scalar_tensor_tensor(L[:, 0:P], ps[3 + hh][:, 0:P], rs[:, h:h + 1], tab[0], ALU.mult, ALU.add)\
                        .then_inc(sem("head_l"), 1)
                    V.scalar_tensor_tensor(L[:, P:384], ps[3 + hh][:, P:384], rs[:, 16 + h:17 + h], tab[1], ALU.mult, ALU.add)\
                        .then_inc(sem("head_l"), 1)
                dve.wait_ge(sem("head_l"), 4 * p + 4)
                L2 = probs[:, 2 * (p % 2):2 * (p % 2) + 2, :]
                m4 = smx[:, 0, :].rearrange("p (h s) -> p h s", s=2)
                V.reduce_max(m4[:, :, 0], L2[:, :, 0:P], AX).then_inc(sem("red"), 1)
                V.reduce_max(m4[:, :, 1], L2[:, :, P:384], AX).then_inc(sem("red"), 1)
                redn[0] += 2
                dve.wait_ge(sem("red"), redn[0])
                V.tensor_scalar(smx[:, 1, :], smx[:, 0, :], -1.0, None, ALU.mult).then_inc(sem("head_max"), 1)

            def normalise(p):
                dve.wait_ge(sem("head_exp"), 4 * p + 4)
                link(V.reciprocal(smx[:, 0, :], smx[:, 2, :]))
                for hh in range(2):
                    L = probs[:, 2 * (p % 2) + hh, :]
                    V.tensor_scalar(L[:, 0:P], L[:, 0:P], smx[:, 0, 2 * hh:2 * hh + 1], None, ALU.mult).then_inc(sem("head_p"), 1)
                    V.tensor_scalar(L[:, P:384], L[:, P:384], smx[:, 0, 2 * hh + 1:2 * hh + 2], None, ALU.mult).then_inc(sem("head_p"), 1)

            def heads_lo(p):
                dve.wait_ge(sem("head_mh"), p + 1)
                V.tensor_tensor(xl[:, 8 + p, :], ps[7][:, 0:T], xh[:, 8 + p, :].bitcast(F32), ALU.subtract)\
                    .then_inc(sem("head_ml"), 1)

            redn = [0]

            def bias_table(h):
                return bias[:, h, 127::-1], bias[:, h, ::-1]

            def mask_table():
                return maskb_s[:, 0, P:T], maskb_s[:, 0, :]

            ahead(U_VA)
            head_factors("sa", 64, kxA.rearrange("p s (h w) -> p s h w", h=HEADS))
            ahead(U_VA + 1)
            V.tensor_tensor(gqk[:, :], col("qa"), col("ka"), ALU.mult).then_inc(sem("red"), 1)
            redn[0] += 1
            dve.wait_ge(sem("red"), redn[0])
            dve.wait_ge(sem("qk_sq"), 4)
            for b in range(2):
                dve.wait_ge(sem("norm_bc"), before("bc", "sa") + b + 1)
                V.scalar_tensor_tensor(ka[:, 2 * b:2 * b + 2, :], ka[:, 2 * b:2 * b + 2, :], gqk[:, 0:1],
                                       two(ps[3 + b][:, :]), ALU.mult, ALU.mult).then_inc(sem("ka_n"), 1)
            dve.wait_ge(sem("bias_in"), 16)
            ahead(U_KR)
            logits_row(0)
            dve.wait_ge(sem("unit_used"), U_KR + 1)
            k_, s_ = kr[64:96, 0, :], krs[64:96, 0, :]
            link(V.tensor_tensor(s_, ps[0][96:128, 0:T], bcs[96:128, :], ALU.mult))
            V.tensor_tensor(k_, ps[0][64:96, 0:T], bcs[64:96, :], ALU.mult).then_inc(sem("evac0"), 1)
            dve.wait_ge(sem("kr_sq"), 1)
            link(V.scalar_tensor_tensor(k_, k_, col("kb", 0, 64, 96), cosk[64:96, 0, :], ALU.mult, ALU.mult))
            link(V.tensor_tensor(s_, s_, sink[64:96, 0, :], ALU.mult))
            link(V.tensor_tensor(k_, k_, s_, ALU.add))
            ahead(U_UK)
            normalise(0)
            logits_row(1)
            ahead(U_UQ)
            normalise(1)
            logits_row(2)
            heads_lo(0)
            ahead(U_UQ + 1)
            normalise(2)
            logits_row(3)
            heads_lo(1)
            ahead(U_UQ + 2)
            normalise(3)
            heads_lo(2)
            for half in range(4):
                dve.wait_ge(sem("uq_ev"), half + 1)
                hs = slice(2 * half, 2 * half + 2)
                q_, w_ = qb[64:96, hs, :], qsw[64:96, hs, :]
                V.tensor_tensor(q_, q_, cosq[64:96, 0:1, :].broadcast_to([32, 2, T]), ALU.mult).then_inc(sem("rot"), 1)
                V.tensor_tensor(w_, w_, sinq[64:96, 0:1, :].broadcast_to([32, 2, T]), ALU.mult).then_inc(sem("rot"), 1)
                dve.wait_ge(sem("rot"), 2 * half + 2)
                V.tensor_tensor(q_, q_, w_, ALU.add).then_inc(sem("q_rot"), 1)
            heads_lo(3)
            head_factors("sb", 96, kxB.rearrange("p (s h) w -> p s h w", s=2))
            dve.wait_ge(sem("uk_ev"), 4)
            for b in range(4):
                dve.wait_ge(sem("norm_bc"), before("bc", "sb") + b + 1)
                src = two(ps[b % RING][:, :])
                hs = slice(2 * b, 2 * b + 2)
                V.tensor_tensor(kb[0:64, hs, :], kb[0:64, hs, :], src[0:64], ALU.mult).then_inc(sem("kb_n"), 1)
                V.tensor_tensor(kb[64:96, hs, :], kr[64:96, 0:1, :].broadcast_to([32, 2, T]), src[64:96], ALU.mult)\
                    .then_inc(sem("kb_n"), 1)
            dve.wait_ge(sem("maskb_in"), 16)
            for p in range(6):
                if 1 <= p < 5:
                    normalise(p + 3)
                if p < 4:
                    logits_row(4 + p)
                if p >= 2:
                    heads_lo(p + 2)
            for m in range(4):
                u = U_WO + m
                ahead(u)
                dve.wait_ge(sem("unit_used"), u + 1)
                V.tensor_tensor(x[:, 2 * m:2 * m + 2, :], x[:, 2 * m:2 * m + 2, :],
                                two(ps[u % RING][:, :]), ALU.add).then_inc(sem("wo_x"), 1)
                if m:
                    gained_lo("n6", "ffn2", 0, m - 1)
            gained_lo("n6", "ffn2", 0, 3)

            def relu_square(j, slot_h, slot):
                dve.wait_ge(sem("relu"), j + 1)
                if not isinstance(j, int) or j >= 1:
                    dve.wait_ge(sem("hid2_lo"), j)
                V.tensor_tensor(hid[slot_h], two(silu),
                                two(ps[slot][:, :]), ALU.mult).then_inc(sem("hid2_y"), 1)

            split_lo(U_F2 + RING)
            relu_square(0, 0, U_F2 % RING)
            hidden_lo(0, 0, "hid2", 8)
            norm_factors("n6", 7)
            with dve.Fori(0, (PAIRS2 - 1) // 3 - 1) as i:
                for c in range(3):
                    u0 = 6 * i + (U_F2 + 1 + 2 * c)
                    s0 = (U_F2 + 1 + 2 * c) % RING
                    j = 3 * i + (1 + c)
                    split_lo(u0 + RING, s0)
                    relu_square(j, (1 + c) % 3, s0)
                    hidden_lo(j, (1 + c) % 3, "hid2", 8)
                    split_lo(u0 + 1 + RING, (s0 + 1) % RING)
            for j in range(PAIRS2 - 3, PAIRS2):
                u0 = U_F2 + 2 * j - 1
                ahead(u0)
                relu_square(j, j % 3, u0 % RING)
                hidden_lo(j, j % 3, "hid2", 8)
                ahead(u0 + 1)
            dve.wait_ge(sem("norm_bcs"), before("bcs", "n6") + 1)
            link(V.tensor_tensor(bcs[:, :], bcs[:, :], bcs[:, :], ALU.mult))
            dve.wait_ge(sem("wo_x"), 4)
            for b in range(4):
                if b < 3:
                    dve.wait_ge(sem("out_bank"), b + 1)
                else:
                    dve.wait_ge(sem("unit_used"), UNITS)
                link(V.tensor_tensor(tmp2[:, 2 * b:2 * b + 2, :], two(ps[3 + b][:, :]), factors_by_tile(2), ALU.mult))
                V.tensor_tensor(x[:, 2 * b:2 * b + 2, :], x[:, 2 * b:2 * b + 2, :], tmp2[:, 2 * b:2 * b + 2, :],
                                ALU.add).then_inc(sem("out_ready"), 1)

        @block.tensor
        def _(pe):
            mm = nc.tensor.matmul

            def mm3(out, slot, at, tile, start, stop, width=P, skip=False):
                hi = whi[:, slot, at:at + width]
                mm(out, hi, xh[:, tile, :], start=start, stop=False, skip_group_check=skip)
                mm(out, hi, xl[:, tile, :], start=False, stop=False, skip_group_check=skip)
                return mm(out, wlo[:, slot, at:at + width], xh[:, tile, :], start=False, stop=stop, skip_group_check=skip)

            def arrived(u):
                pe.wait_ge(sem("lo_ready"), u + 1)

            def bank_free(u, b):
                if FILLS[u][b]:
                    pe.wait_ge(sem(f"evac{b}"), FILLS[u][b])

            def used(ins):
                ins.then_inc(sem("unit_used"), 1)

            def first_unit(u, base, x_name):
                arrived(u)
                bank_free(u, u % RING)
                for k in range(8):
                    if k % 2 == 0:
                        pe.wait_ge(sem("act_lo"), before("lo", x_name) + k // 2 + 1)
                    for m in range(2):
                        last = mm3(ps[u % RING][:, m * T:(m + 1) * T], u % RING, (8 * m + k) * P, base + k, k == 0 and m == 0,
                                   k == 7, skip=True)
                used(last)

            def two_tiles(u, base, x_name=None):
                arrived(u)
                bank_free(u, u % RING)
                for m in range(2):
                    for k in range(8):
                        if x_name and m == 0 and k % 4 == 0:
                            pe.wait_ge(sem("act_lo"), before("lo", x_name) + k // 4 + 1)
                        last = mm3(ps[u % RING][:, m * T:(m + 1) * T], u % RING, (8 * m + k) * P, base + k, k == 0, k == 7)
                used(last)

            def token_major(u0, base, x_name=None):
                for n in range(2):
                    u = u0 + n
                    arrived(u)
                    if n == 0:
                        for s in range(2):
                            bank_free(u0 + s, (u0 + s) % RING)
                    for s in range(2):
                        o = ps[(u0 + s) % RING][:, :]
                        for k in range(4):
                            t = base + 4 * n + k
                            if x_name and s == 0 and k % 2 == 0:
                                pe.wait_ge(sem("act_lo"), before("lo", x_name) + 2 * n + k // 2 + 1)
                            xs = slice(s * P, (s + 1) * P)
                            wc = slice(512 * k, 512 * k + 512)
                            first, end = n == 0 and k == 0, n == 1 and k == 3
                            mm(o, xh[:, t, xs], whi[:, u % RING, wc], start=first, stop=False)
                            mm(o, xl[:, t, xs], whi[:, u % RING, wc], start=False, stop=False)
                            last = mm(o, xh[:, t, xs], wlo[:, u % RING, wc], start=False, stop=end)
                    used(last)

            def norm_stats(name, sq, waits):
                for s_name, value in waits:
                    pe.wait_ge(sem(s_name), value)
                for s in range(2):
                    for k in range(8):
                        last = mm(ps[7][:, s:s + 1], sq[:, k, s * P:(s + 1) * P], mean_col(MEAN_D), start=k == 0, stop=k == 7)
                last.then_inc(sem("norm_stats"), 1)

            def norm_bc(name):
                pe.wait_ge(sem("norm_factors"), before("rx", name) + 1)
                for s in range(2):
                    last = mm(ps[7][:, T + s * P:T + (s + 1) * P], rx[:, s, :], ident, start=True, stop=True)
                last.then_inc(sem("norm_bc"), 1)

            pe.wait_ge(sem("cst_in"), 16)
            norm_stats("n1", sq1, [("norm_sq", before("sq", "n1") + 2)])
            token_major(U_ZV, 0, "n1")
            norm_bc("n1")
            steps = hgrn_schedule()

            def spatial_mix(b):
                pe.wait_ge(sem("sgw_in"), 16)
                pe.wait_ge(sem("vn"), 2)
                for j in (2 * b, 2 * b + 1):
                    for s in range(2):
                        for e in range(2):
                            g = 2 * j + e
                            c = (j % 2) * T + s * P
                            last = mm(ps[3 + b][64 * e:64 * e + 64, c:c + P], vn[:, s, g * 64:g * 64 + 64],
                                      sgw_s[:, g, :], start=True, stop=True)
                last.then_inc(sem("sg_mm"), 1)

            def hgrn_pe(kind, g, lv):
                H = G[g]
                if kind == "level":
                    banks = (ps[3 + 2 * g], ps[4 + 2 * g])
                    if lv == 0:
                        pe.wait_ge(sem(f"q_init{g}"), 2)
                        pe.wait_ge(sem("b_out"), 1)
                        for s in range(2):
                            for h in range(4):
                                for d in range(2):
                                    ts = slice(s * P, (s + 1) * P)
                                    last = mm(banks[s][:, h * P:(h + 1) * P], H["K"][d][:, h, ts], H["q"][:, h, ts],
                                              start=d == 0, stop=d == 1)
                    elif lv <= 7:
                        if lv == 1:
                            pe.wait_ge(sem(f"lv_copy{g}"), 2)
                        else:
                            pe.wait_ge(sem(f"tree{g}"), lv - 1)
                        w = 1 << (lv - 1)
                        for s in range(2):
                            for h in range(4):
                                o = banks[s][:, h * P:(h + 1) * P].rearrange("p (n two w) -> p n two w", two=2, w=w)
                                for d in range(2):
                                    qv = H["Q"][d][:, h, s * P:(s + 1) * P].rearrange("p (n two w) -> p n two w", two=2, w=w)
                                    last = mm(o[:, :, 1 - d, :], H["K"][d][:, h, s * P:(s + 1) * P], qv[:, :, 1 - d, :],
                                              start=True, stop=True)
                    else:
                        pe.wait_ge(sem(f"tree{g}"), 7)
                        for s in range(2):
                            for h in range(4):
                                last = mm(banks[s][:, h * P:(h + 1) * P], H["K"][s][:, h, s * P:(s + 1) * P],
                                          H["Q"][s][:, h, (1 - s) * P:(2 - s) * P], start=True, stop=True)
                    last.then_inc(sem(f"lv_mm{g}"), 1)
                if kind == "pv":
                    pe.wait_ge(sem(f"lv_copy{g}"), 4)
                    for h in range(4):
                        for s in range(2):
                            hh = 4 * g + h
                            if h == 0 and s == 0:
                                for uu in (U_ZI + 1, U_ZI + 3):
                                    for v in (uu - 1, uu):
                                        pe.wait_ge(sem(f"evac{v % RING}"), FILLS[v][v % RING] + 1)
                            last = mm(ps[3 + 2 * g + h // 2][:, (h % 2) * T:(h % 2 + 1) * T],
                                      zi[:, s, hh * P:(hh + 1) * P], H["S"][:, s, h, :], start=s == 0, stop=s == 1)
                    last.then_inc(sem(f"pv_mm{g}"), 1)

            for u in range(U_ZU, U_WA):
                if U_ZI <= u < U_GA:
                    if (u - U_ZI) % 2 == 0:
                        token_major(u, 0)
                else:
                    two_tiles(u, 0)
                if u == U_Q[0]:
                    spatial_mix(0)
                    spatial_mix(1)
                for step in steps.get(u, ()):
                    hgrn_pe(*step)
                if u == U_GB:
                    for g in range(2):
                        pe.wait_ge(sem(f"o_sq{g}"), 2)
                    for h in range(HEADS):
                        for s in range(2):
                            last = mm(ps[7][:, 2 * h + s:2 * h + s + 1], sqo[h // 4][:, h % 4, s * P:(s + 1) * P],
                                      mean_col(MEAN_HEAD), start=True, stop=True)
                    last.then_inc(sem("norm_stats"), 1)
                if u == U_GB + 1:
                    pe.wait_ge(sem("norm_factors"), before("rx", "o") + 1)
                    for h in range(HEADS):
                        for s in range(2):
                            last = mm(ps[3 + h // 2][:, (h % 2) * T + s * P:(h % 2) * T + (s + 1) * P], rxo[:, 2 * h + s, :],
                                      ident, start=True, stop=True)
                        if h % 2:
                            last.then_inc(sem("norm_bc"), 1)
            for m in range(4):
                two_tiles(U_WA + m, 8, "a" if m == 0 else None)
            for n in range(2):
                u = U_WB + n
                arrived(u)
                if n == 0:
                    pe.wait_ge(sem("act_lo"), before("lo", "b") + 2)
                for m in range(4):
                    for k in range(4):
                        last = mm3(ps[3 + 2 * n + m // 2][:, (m % 2) * T:(m % 2 + 1) * T], u % RING, (4 * m + k) * P, k,
                                   k == 0, k == 3)
                used(last)
            def mix_stats(m):
                pe.wait_ge(sem(f"evac{(U_WOUT + m) % RING}"), FILLS[U_WOUT + m][(U_WOUT + m) % RING] + 1)
                for k in (2 * m, 2 * m + 1):
                    for s in range(2):
                        last = mm(ps[7][:, s:s + 1], sq2[:, k, s * P:(s + 1) * P], mean_col(MEAN_D), start=k == 0 and s == 0,
                                  stop=k == 7, skip_group_check=True)
                return last

            first_unit(U_WOUT, 8, "m")
            for m in range(1, 4):
                two_tiles(U_WOUT + m, 8)
                mix_stats(m - 1)
            mix_stats(3).then_inc(sem("norm_stats"), 1)
            arrived(U_PLE)
            pe.wait_ge(sem("act_lo"), before("lo", "p") + 1)
            for m in range(DT):
                for k in range(2):
                    last = mm3(ps[3 + m // 2][:, (m % 2) * T:(m % 2 + 1) * T], U_PLE % RING, (2 * m + k) * P, 6 + k, k == 0, k == 1)
                if m == 2:
                    norm_bc("n2")
            used(last)

            def last_down(slot, base, signal, after=None):
                for b in range(4):
                    for m in (2 * b, 2 * b + 1):
                        for kk in range(2):
                            last = mm3(ps[3 + b][:, (m % 2) * T:(m % 2 + 1) * T], slot, (8 * kk + m) * P, base + kk,
                                       False, kk == 1, skip=True)
                    if b < 3:
                        last.then_inc(sem(signal), 1)
                    else:
                        used(last)
                    if after and b:
                        after(b - 1)

            def down(slot, base, first):
                for kk in range(2):
                    for m in range(DT):
                        start = first and kk == 0 and m % 2 == 0
                        last = mm3(ps[3 + m // 2][:, (m % 2) * T:(m % 2 + 1) * T], slot, (8 * kk + m) * P, base + kk,
                                   start, False, skip=True)
                return last

            def pair_tiles(u, slot, base):
                for m in range(2):
                    for k in range(8):
                        last = mm3(ps[slot][:, m * T:(m + 1) * T], slot, (8 * m + k) * P, base + k, k == 0, k == 7)
                return last

            first_unit(U_F1, 8, "n3")
            norm_stats("n3", sq3, [("norm_sq", before("sq", "n3") + 4)])
            two_tiles(U_F1 + 1, 8)
            norm_bc("n3")
            s0 = (U_F1 + 2) % RING

            def ffn1_step(j, u, c, first):
                pe.wait_ge(sem("lo_ready"), u + 1)
                pe.wait_ge(sem("gate_r"), j)
                used(pair_tiles(u, s0, 8))
                pe.wait_ge(sem("lo_ready"), u + 2)
                pe.wait_ge(sem("hid_y"), j)
                used(pair_tiles(u + 1, (s0 + 1) % RING, 8))
                pe.wait_ge(sem("lo_ready"), u + 3)
                pe.wait_ge(sem("hid_lo"), j)
                if first:
                    pe.wait_ge(sem("ple_copy"), 4)
                used(down((s0 + 2) % RING, 2 * c, first))

            for c in range(2):
                ffn1_step(1 + c, U_F1 + 2 + 3 * c, c, c == 0)
            with pe.Fori(1, (PAIRS1 - 1) // 2) as i:
                for c in range(2):
                    ffn1_step(2 * i + (1 + c), 6 * i + (U_F1 + 2 + 3 * c), c, False)
            arrived(U_PG - 1)
            pe.wait_ge(sem("hid_lo"), PAIRS1)

            def ff_stats(b):
                pe.wait_ge(sem("norm_sq"), before("sq", "n4") + b + 1)
                for k in (2 * b, 2 * b + 1):
                    for s in range(2):
                        last = mm(ps[7][:, s:s + 1], sq2[:, k, s * P:(s + 1) * P], mean_col(MEAN_D), start=k == 0 and s == 0,
                                  stop=k == 7, skip_group_check=True)
                return last

            last_down((U_PG - 1) % RING, 2 * ((PAIRS1 - 1) % 2), "ff_bank", ff_stats)
            ff_stats(3).then_inc(sem("norm_stats"), 1)
            norm_bc("n4")
            for m in range(4):
                if m == 0:
                    first_unit(U_PG, 0, "ff")
                else:
                    two_tiles(U_PG + m, 0)
                if m == 2:
                    pe.wait_ge(sem("rel_in"), 16)
                    pe.wait_ge(sem("oneh_in"), 16)
                    mm(ps[3][0:HEADS, :], rel_s[0:33, 0, 0:HEADS], oneh_s[0:33, 0, :], start=True, stop=True)\
                        .then_inc(sem("bv_mm"), 1)

            def latent_stats(n):
                which, tiles, at = ((MEAN_CQ, 6, 0), (MEAN_CKV, 2, 6))[n]
                pe.wait_ge(sem("c_sq"), 4)
                if n:
                    pe.wait_ge(sem("norm_bcs"), before("bcs", "c") + n)
                for s in range(2):
                    for k in range(tiles):
                        last = mm(ps[7][:, s:s + 1], sqc[:, at + k, s * P:(s + 1) * P], mean_col(which), start=k == 0, stop=k == tiles - 1)
                last.then_inc(sem("norm_stats"), 1)

            def latent_bc(n):
                pe.wait_ge(sem("norm_factors"), before("rx", "c") + n + 1)
                for s in range(2):
                    last = mm(ps[7][:, T + s * P:T + (s + 1) * P], rx[:, s, :], ident, start=True, stop=True)
                last.then_inc(sem("norm_bc"), 1)

            first_unit(U_CQ, 8, "n5")
            norm_stats("n5", sq3, [("norm_sq", before("sq", "n5") + 4)])
            two_tiles(U_CQ + 1, 8)
            norm_bc("n5")
            two_tiles(U_CQ + 2, 8)
            two_tiles(U_CKV, 8)
            two_tiles(U_QA, 8)
            latent_stats(0)
            two_tiles(U_QA + 1, 8)
            latent_bc(0)
            latent_stats(1)
            two_tiles(U_KA, 8)
            latent_bc(1)
            two_tiles(U_KA + 1, 8)
            token_major(U_VA, 8)
            pe.wait_ge(sem("qk_sq"), 4)
            for s in range(2):
                for j in range(8):
                    c = 2 * j
                    last = mm(ps[7][:, 16 * s:16 * s + 16], sqA[:, j, s * P:(s + 1) * P],
                              cst_s[:, C_Z64 + 16 - c:C_Z64 + 32 - c], start=j == 0, stop=j == 7)
            last.then_inc(sem("norm_stats"), 1)
            u = U_KR
            arrived(u)
            for b in range(RING):
                bank_free(u, b)
            for k in range(8):
                mm3(ps[0][:, 0:T], u % RING, k * P, 8 + k, k == 0, k == 7)
            pe.wait_ge(sem("act_lo"), before("lo", "c") + 2)
            for s in range(2):
                for k in range(2):
                    xs = slice(s * P, (s + 1) * P)
                    wc = slice(1024 + 512 * k, 1536 + 512 * k)
                    mm(ps[1 + s][:, :], xh[:, 6 + k, xs], whi[:, u % RING, wc], start=k == 0, stop=False)
                    mm(ps[1 + s][:, :], xl[:, 6 + k, xs], whi[:, u % RING, wc], start=False, stop=False)
                    last = mm(ps[1 + s][:, :], xh[:, 6 + k, xs], wlo[:, u % RING, wc], start=False, stop=k == 1)
            used(last)
            pe.wait_ge(sem("norm_factors"), before("rx", "sa") + 1)
            for j in range(4):
                for s in range(2):
                    last = mm(ps[3 + j // 2][:, (j % 2) * T + s * P:(j % 2) * T + (s + 1) * P], kxA[:, s, j * P:(j + 1) * P],
                              ident, start=True, stop=True)
                if j % 2:
                    last.then_inc(sem("norm_bc"), 1)

            def qk(p):
                if p:
                    pe.wait_ge(sem("head_l"), 4 * p)
                else:
                    pe.wait_ge(sem("ka_n"), 2)
                if p == 4:
                    pe.wait_ge(sem("kb_n"), 8)
                    pe.wait_ge(sem("q_rot"), 4)
                for hh in range(2):
                    h = 2 * (p % 4) + hh
                    if p < 4:
                        a = 64 * hh
                        q_, k_ = qa[a:a + 64, h // 2, :], ka[a:a + 64, h // 2, :]
                    else:
                        q_, k_ = qb[0:96, h, :], kb[0:96, h, :]
                    mm(ps[3 + hh][:, 0:P], q_[:, 0:P], k_[:, 0:P], start=True, stop=True)
                    last = mm(ps[3 + hh][:, P:384], q_[:, P:T], k_, start=True, stop=True)
                last.then_inc(sem("head_qk"), 1)

            def turn(p):
                pe.wait_ge(sem("head_p"), 4 * p + 4)
                if p:
                    pe.wait_ge(sem("head_trc"), 2 * p)
                for hh in range(2):
                    for c in range(3):
                        last = nc.tensor.transpose(ps[5 + hh][:, c * P:(c + 1) * P],
                                                   probs[:, 2 * (p % 2) + hh, c * P:(c + 1) * P], ident)
                last.then_inc(sem("head_tr"), 1)

            def pv(p):
                v = va if p < 4 else vb
                pe.wait_ge(sem("head_trc"), 2 * p + 2)
                if p:
                    pe.wait_ge(sem("head_ml"), p)
                for hh in range(2):
                    h = 2 * (p % 4) + hh
                    o = ps[7][64 * hh:64 * hh + 64, :]
                    PT = probsT[:, 2 * (p % 2) + hh, :]
                    hv = slice(64 * h, 64 * h + 64)
                    mm(o[:, 0:P], v[:, 0, hv], PT[:, 0:P], start=True, stop=True)
                    mm(o[:, P:T], v[:, 0, hv], PT[:, P:T], start=True, stop=False)
                    last = mm(o[:, P:T], v[:, 1, hv], PT[:, T:384], start=False, stop=True)
                last.then_inc(sem("head_pv"), 1)

            qk(0)
            arrived(U_UK)
            for h in range(HEADS):
                b = (U_UK + h // 2) % RING
                if h % 2 == 0 and h // 2 < 3:
                    pe.wait_ge(sem(f"evac{b}"), FILLS[U_UK][b])
                if h == 6:
                    pe.wait_ge(sem("uk_ev"), 1)
                for k in range(2):
                    last = mm3(ps[b][:, (h % 2) * T:(h % 2 + 1) * T], U_UK % RING, (2 * h + k) * P, 6 + k, k == 0, k == 1)
                if h % 2 and h < 7:
                    last.then_inc(sem("uk_mm"), 1)
            used(last)
            turn(0)
            qk(1)
            pe.wait_ge(sem("uk_ev"), 4)
            for n in range(3):
                u = U_UQ + n
                arrived(u)
                for blk in range(16):
                    i = 16 * n + blk
                    h, k = divmod(i, 6)
                    b = (h // 2) % RING
                    if h == 6 and k == 0:
                        pe.wait_ge(sem("uq_ev"), 1)
                    last = mm3(ps[b][:, (h % 2) * T:(h % 2 + 1) * T], u % RING, blk * P, k, k == 0, k == 5)
                    if k == 5 and h % 2 and blk < 15:
                        last.then_inc(sem("uq_mm"), 1)
                used(last)
                pv(n)
                turn(n + 1)
                if n < 2:
                    qk(n + 2)
            pe.wait_ge(sem("uq_ev"), 4)
            pe.wait_ge(sem("uk_ev"), 4)
            pv(3)
            pe.wait_ge(sem("head_ml"), 4)
            for s in range(2):
                for h in range(16):
                    sq = (sqq if h < 8 else sqk)[0:96, h % 8, s * P:(s + 1) * P]
                    last = mm(ps[7][:, 16 * s:16 * s + 16], sq, cst_s[0:96, C_Z96 + 16 - h:C_Z96 + 32 - h], start=h == 0, stop=h == 15)
            last.then_inc(sem("norm_stats"), 1)
            pe.wait_ge(sem("norm_factors"), before("rx", "sb") + 1)
            for h in range(HEADS):
                b = (h // 2) % RING
                if h == 6:
                    pe.wait_ge(sem("kb_n"), 2)
                for s in range(2):
                    last = mm(ps[b][0:96, (h % 2) * T + s * P:(h % 2) * T + (s + 1) * P], kxB[:, 8 * s + h, :], ident, start=True, stop=True)
                if h % 2:
                    last.then_inc(sem("norm_bc"), 1)
            for p in range(6):
                if p < 4:
                    qk(4 + p)
                if p >= 2:
                    pv(4 + p - 2)
                if 1 <= p < 5:
                    turn(p + 3)
            pe.wait_ge(sem("head_ml"), 8)
            for m in range(4):
                u = U_WO + m
                arrived(u)
                if m == 3:
                    pe.wait_ge(sem("wo_x"), 1)
                last = pair_tiles(u, u % RING, 8)
                used(last)

            first_unit(U_F2, 0, "n6")
            def ffn2_step(j, u, s, base, first):
                pe.wait_ge(sem("lo_ready"), u + 1)
                used(pair_tiles(u, s, 0))
                pe.wait_ge(sem("lo_ready"), u + 2)
                pe.wait_ge(sem("hid2_lo"), j)
                used(down((s + 1) % RING, base, first))

            norm_stats("n6", sq3, [("norm_sq", before("sq", "n6") + 4)])
            for j in range(1, 4):
                ffn2_step(j, U_F2 + 2 * j - 1, (U_F2 + 2 * j - 1) % RING, 8 + 2 * ((j - 1) % 3), j == 1)
                if j == 1:
                    norm_bc("n6")
            with pe.Fori(1, (PAIRS2 - 1) // 3) as i:
                for c in range(3):
                    ffn2_step(3 * i + (1 + c), 6 * i + (U_F2 + 1 + 2 * c), (U_F2 + 1 + 2 * c) % RING, 8 + 2 * c, False)
            arrived(UNITS - 1)
            pe.wait_ge(sem("hid2_lo"), PAIRS2)
            last_down((UNITS - 1) % RING, 8 + 2 * ((PAIRS2 - 1) % 3), "out_bank")


def _tiles(v):
    return v.reshape(-1, P).T


def _channel_blocks(m):
    k, n = m.shape[0] // P, m.shape[1] // P
    return m.reshape(k, P, n, P).transpose(1, 2, 0, 3).reshape(P, n * k, P)


def _row_blocks(m):
    k, n = m.shape[0] // P, m.shape[1] // P
    return m.reshape(k, P, n, P).transpose(1, 0, 2, 3).reshape(P, n * k, P)


def _wide(m):
    k = m.shape[0] // P
    return m.reshape(k, P, 512).transpose(1, 0, 2).reshape(P, k * 4, P)


def _weights(a):
    f = lambda n: np.asarray(a[n], np.float32) if a[n].ndim == 2 else np.asarray(a[n][0], np.float32)
    w = f("w_in")
    q, ff, fb, zi, zg, zu, zv, ga, gb = np.split(w, np.cumsum([1024] * 5 + [512] * 2 + [1024]), axis=1)
    parts = [_wide(zv), _channel_blocks(zu)]
    for g in range(2):
        parts += [_channel_blocks(m[:, 512 * g:512 * g + 512]) for m in (q, ff, fb)]
    parts += [_wide(zi[:, 0:512]), _wide(zi[:, 512:])]
    parts += [_channel_blocks(m) for m in (ga, zg, gb, f("w_a"), f("w_b"), f("w_out"), f("w_ple"))]
    gate, up, down = f("w_gate"), f("w_up"), f("w_down")
    pair = lambda m, j: m[:, 256 * j:256 * j + 256]
    for j in range(PAIRS1):
        parts += [_channel_blocks(pair(gate, j)), _channel_blocks(pair(up, j))]
        if j:
            parts.append(_row_blocks(down[256 * (j - 1):256 * j]))
    parts += [_row_blocks(down[256 * (PAIRS1 - 1):]), _channel_blocks(f("w_ple_gate"))]
    w2, uq, ukv = f("w_in_2"), f("w_uq_2"), f("w_ukv_2")
    qa, ka, va, cq, ckv, kr = np.split(w2, np.cumsum([512, 512, 512, 768, 256]), axis=1)
    parts += [_channel_blocks(m) for m in (cq, ckv, qa, ka)] + [_wide(va)]
    swap = np.r_[16:32, 0:16]
    ukv = ukv.reshape(256, HEADS, 128)
    uq = uq.reshape(768, HEADS, 96)
    parts += [_channel_blocks(np.concatenate([kr, kr, kr, kr[:, swap]], axis=1)),
              _wide(ukv[:, :, 64:].reshape(256, 512)), _channel_blocks(ukv.reshape(256, 1024)),
              _channel_blocks(np.concatenate([uq, uq[:, :, 64 + swap]], axis=2).reshape(768, 1024)),
              _channel_blocks(f("w_o_2"))]
    ff1, ff2 = f("w_ff1_2"), f("w_ff2_2")
    for j in range(PAIRS2):
        parts.append(_channel_blocks(pair(ff1, j)))
        if j:
            parts.append(_row_blocks(ff2[256 * (j - 1):256 * j]))
    parts.append(_row_blocks(ff2[256 * (PAIRS2 - 1):]))
    full = np.concatenate(parts, axis=1).reshape(P, UNITS, UNIT)
    return np.ascontiguousarray(full.transpose(1, 0, 2))


def _params(a):
    v = lambda n: np.asarray(a[n], np.float32).reshape(-1)
    pad = lambda x, at=0: np.concatenate([np.zeros(at, np.float32), x, np.zeros(P - at - len(x), np.float32)])[:, None]
    swap = lambda g: pad(np.concatenate([g[80:96], g[64:80]]), 64)
    qb, kb = v("qnorm_b_g_2"), v("knorm_b_g_2")
    return np.concatenate([
        _tiles(v("norm_mix_pre")), _tiles(v("lb_gamma_fwd")), _tiles(v("lb_gamma_bwd")), _tiles(v("hg_norm")),
        _tiles(v("norm_mix_post")), _tiles(v("norm_ffn_pre")), _tiles(v("norm_ffn_post")), _tiles(v("norm_mix_g_2")),
        _tiles(v("cq_norm_g_2")), _tiles(v("ckv_norm_g_2")), _tiles(v("norm_ffn_g_2")),
        np.tile(v("qnorm_a_g_2"), 2)[:, None], np.tile(v("knorm_a_g_2"), 2)[:, None],
        pad(qb), pad(kb), swap(qb), swap(kb)], axis=1)


def _constants():
    c = np.zeros((P, NCST), np.float32)
    c[:, C_ID:C_ID + P] = np.eye(P)
    c[:64, C_Z64 + 16] = c[64:, C_Z64 + 17] = 1 / 64
    c[:, C_Z96 + 16] = 1 / 96
    for k, n in enumerate((1024, 768, 256, 128)):
        c[:, C_MEAN + k] = 1 / n
    freq = 1.0 / (np.float32(10000.0) ** (np.arange(0, 32, 2, dtype=np.float32) / np.float32(32)))
    c[64:96, C_INVF] = np.tile(freq, 2)
    c[64:80, C_SIGN], c[80:96, C_SIGN] = -1, 1
    return c


def _level_masks():
    i = np.arange(P)
    return np.stack([(i[:, None] >> lv == i[None] >> lv) & (i[:, None] >> lv - 1 != i[None] >> lv - 1)
                     for lv in range(1, 8)], axis=1).astype(np.int32)


def _distances():
    d = np.arange(512) - 127
    safe = np.maximum(d, 1).astype(np.float32)
    large = 16 + (np.log(safe / 16) / np.log(2048 / 16) * 16).astype(np.int64)
    bucket = np.where(d < 16, d, np.minimum(large, 31))
    n = (d <= 128).astype(int) + (d % 4 == 0) + (d % 16 == 0)
    seen = (d >= 0) & (n > 0)
    t = np.zeros((33, 512), np.float32)
    t[bucket[seen], np.flatnonzero(seen)] = 1
    t[32] = np.where(seen, np.log(np.maximum(n, 1)), NEG)
    return t


def kernel(**a):
    import concourse.bacc as bacc
    from concourse.bass_utils import run_bass_kernel_spmd

    f = lambda n: np.asarray(a[n], np.float32)
    causal = np.zeros((P, T), np.float32)
    causal[:, P:] = np.where(np.arange(P)[None] <= np.arange(P)[:, None], 0, NEG)
    arrays = {
        "w": _weights(a),
        "xT": f("x")[0].T.reshape(DT, P, T).transpose(1, 0, 2),
        "pT": f("p")[0, 0].T.reshape(2, P, T).transpose(1, 0, 2),
        "par": _params(a), "cst": _constants(), "lvl": _level_masks(),
        "sgw": f("sg_w")[0].transpose(2, 0, 1),
        "sgb": np.repeat(f("sg_b")[0].reshape(4, 2, P), 64, axis=1).transpose(1, 0, 2),
        "lnr": np.broadcast_to(np.stack([f("sg_ln_g")[0], f("sg_ln_b")[0]])[None], (P, 2, 512)),
        "rel": f("rel_bias_2"), "oneh": _distances(), "maskb": causal,
        "pos": np.asarray(a["positions_2"], np.int32).reshape(1, T),
    }
    arrays = {k: np.ascontiguousarray(v) for k, v in arrays.items()}
    nc = bacc.Bacc("TRN2", target_bir_lowering=False, num_devices=1)
    args = [nc.dram_tensor(k, v.shape, mybir.dt.from_np(v.dtype), kind="ExternalInput").ap() for k, v in arrays.items()]
    out = nc.dram_tensor("out", (P, DT, T), F32, kind="ExternalOutput").ap()
    build_blocks(nc, *args, out)
    r = run_bass_kernel_spmd(nc, [arrays], core_ids=[0]).results[0]["out"]
    return np.ascontiguousarray(r.transpose(2, 1, 0).reshape(1, T, D))
```

```python
from contextlib import ExitStack

import numpy as np

import concourse.bass as bass
from concourse import mybir

F32 = mybir.dt.float32
F32R = mybir.dt.float32r
I32 = mybir.dt.int32
ALU = mybir.AluOpType
ACT = mybir.ActivationFunctionType
AX = mybir.AxisListType.X

P = 128
T = 256
D = 1024
DT = D // P
UNIT = 2048
RING = 3
HEADS = 8
FFN = 2816
FFN2 = 4096
EPS = 1e-6
TINY = float(np.finfo(np.float32).tiny)
NEG = -1e30

U_ZV, U_ZU = 0, 2
U_Q = (4, 10)
U_ZI, U_GA, U_ZG, U_GB = 16, 20, 24, 28
U_WA, U_WB, U_WOUT, U_PLE = 32, 36, 38, 42
U_F1 = 43
PAIRS1 = FFN // 256
U_PG = U_F1 + 3 * PAIRS1
U_QA = U_PG + 4
U_KA, U_VA, U_CQ, U_CKV = U_QA + 2, U_QA + 4, U_QA + 6, U_QA + 9
U_KR, U_UK, U_UQ = U_QA + 10, U_QA + 11, U_QA + 12
U_WO = U_UQ + 3
U_F2 = U_WO + 4
PAIRS2 = FFN2 // 256
UNITS = U_F2 + 2 * PAIRS2

PAR = {}
_at = 0
for _name, _n in (("mix_pre", 8), ("gamma", 16), ("hg_norm", 8), ("mix_post", 8), ("ffn_pre", 8),
                  ("ffn_post", 8), ("mix2", 8), ("cq", 6), ("ckv", 2), ("ffn2", 8), ("qa", 1), ("ka", 1),
                  ("qb", 1), ("kb", 1), ("qb_swap", 1), ("kb_swap", 1)):
    PAR[_name] = _at
    _at += _n
NPAR = _at
C_ID, C_Z64, C_Z96, C_MEAN, C_INVF, C_SIGN = 0, 128, 160, 192, 196, 197
NCST = 198
MEAN_D, MEAN_CQ, MEAN_CKV, MEAN_HEAD = range(4)


def banks_of(u):
    if u in (U_WB, U_WB + 1, U_PLE) or U_UK <= u:
        return ()
    if U_F1 <= u < U_PG:
        return ()
    if u == U_KR:
        return (0, 1, 2)
    return (u % RING,)


def fill_counts():
    before, count = [], [0] * RING
    for u in range(UNITS):
        before.append(tuple(count))
        for b in banks_of(u):
            count[b] += 1
    return before


FILLS = fill_counts()

SIGNALS = {
    "sq": dict(n1=2, n3=4, n4=4, n5=4, n6=4),
    "st": dict(n1=1, o=1, n2=1, n3=1, n4=1, n5=1, sa=1, c=1, sb=1, n6=1),
    "rx": dict(n1=1, o=1, n2=1, n3=1, n4=1, n5=1, sa=1, c=1, sb=1, n6=1),
    "bc": dict(n1=1, o=4, n2=1, n3=1, n4=1, n5=1, sa=2, c=1, sb=4, n6=1),
    "bcs": dict(n1=1, n3=1, n4=1, n5=1, c=1, n6=1),
    "y": dict(a=2, m=4, n2=4, n4=4, c=4),
    "hi": dict(n1=4, a=2, b=2, m=4, p=1, n3=4, ff=4, n5=4, c=4, n6=4),
    "lo": dict(n1=4, a=2, b=2, m=4, p=1, n3=4, ff=4, n5=4, c=4, n6=4),
}


FOLDED = ("n1", "n2", "n3", "n4", "n5", "n6")
NORMS = ("n1", "n2", "n3", "n4", "n5", "c", "n6")


def z_index(u):
    return u - U_ZU if u < U_ZI else u - U_ZU - 4


def k_index(u):
    return (u - U_Q[0]) // 6 * 4 + (u - U_Q[0]) % 6 - 2


def before(kind, stage):
    stages = list(SIGNALS[kind])
    return sum(SIGNALS[kind][s] for s in stages[:stages.index(stage)])


def hgrn_schedule():
    steps = {}
    for g, first in enumerate((10, 18)):
        for lv in range(9):
            steps.setdefault(first + lv, []).append(("level", g, lv))
    for g, u in enumerate((19, 27)):
        steps.setdefault(u, []).insert(0, ("pv", g, 0))
    return steps


_C1 = np.float32(6.28125)
_C2 = np.float32(int((2 * np.pi - float(_C1)) * 2 ** 21) / 2 ** 21)
TWO_PI = (float(_C1), float(_C2), float(np.float32(2 * np.pi - float(_C1) - float(_C2))))


def build_blocks(nc, w, xT, pT, par, cst, lvl, sgw, sgb, lnr, rel, oneh, maskb, pos, out):
    scratch = nc.dram_tensor("bias_scratch", [HEADS, 512], F32, kind="Internal").ap()
    ctx = ExitStack()
    with ctx:
        def sb(name, shape, dt=F32):
            return ctx.enter_context(nc.sbuf_tensor(name, shape, dt))

        sems = {}

        def sem(name):
            if name not in sems:
                sems[name] = ctx.enter_context(nc.semaphore(name))
            return sems[name]

        raw = sb("raw", [P, RING, UNIT])
        whi = sb("whi", [P, RING, UNIT], F32R)
        wlo = sb("wlo", [P, RING, UNIT], F32R)
        xh = sb("xh", [P, 16, T], F32R)
        xl = sb("xl", [P, 16, T], F32R)
        x = sb("x", [P, DT, T])
        work = sb("work", [P, 88 * T])
        par_s = sb("par_s", [P, NPAR])
        cst_s = sb("cst_s", [P, NCST])
        lvl_s = sb("lvl_s", [P, 7, P], I32)
        lb = sb("lb", [P, 3, 16])
        rx = sb("rx", [P, 2, P])
        bcs = sb("bcs", [P, T])
        nt = sb("nt", [P, 4, 32])
        eps_s = sb("eps_s", [P, 4])
        rtok = sb("rtok", [P, len(NORMS), 4])
        gqk = sb("gqk", [P, 1])
        half_s = sb("half_s", [P, 4])
        nti = sb("nti", [P, 32], I32)
        rs = sb("rs", [P, 32])
        ps = [ctx.enter_context(nc.psum_tensor(f"ps{b}", [P, 512], F32)) for b in range(8)]

        def view(at, tiles, inner=T):
            return work[:, at * T:(at + tiles) * T].rearrange("p (n t) -> p n t", t=inner)

        def col(name, k=0, a=0, b=P):
            return par_s[a:b, PAR[name] + k:PAR[name] + k + 1]

        def two(ap):
            return ap.rearrange("p (a t) -> p a t", a=2)

        def alternating(pair, level, first, start=0, tokens=4 * T):
            w = 1 << (level - 1)
            h, t = divmod(start, T)
            a, b = (v[:, h, t:t + w] for v in (pair[first], pair[1 - first]))
            return bass.AP(a.tensor, a.offset, [list(a.ap[0]), [2 * w, tokens // (2 * w)], [b.offset - a.offset + w, 2], [1, w]])

        ident = cst_s[:, C_ID:C_ID + P]

        def mean_col(which):
            return cst_s[:, C_MEAN + which:C_MEAN + which + 1]

        sq1 = view(28, 8)
        zv, zu = view(52, 4, 512), view(48, 4)
        lnr_s = view(44, 4, 512)
        sgw_s, sgb_s = view(64, 4, P), view(68, 2, P)
        vn = view(28, 4, 512)
        bout = view(84, 4)
        G = []
        for g in range(2):
            a = 28 * g
            G.append(dict(q=view(a, 4), Q=(view(a + 4, 4), view(a + 8, 4)),
                          K=(view(a + 12, 4), view(a + 16, 4)), F=(view(a + 20, 4), view(a + 24, 4)),
                          ksum=view(56 + 8 * g, 4), Kc=view(68 - 8 * g, 4),
                          S=work[:, (56 + 8 * g) * T:(64 + 8 * g) * T].rearrange("p (s h t) -> p s h t", s=2, t=T)))
        zi = view(72, 8, D)
        t1 = view(80, 4, 512)
        ga, zg, gb = view(4, 8), view(12, 8), view(20, 8)
        sqo = [view(56, 4), view(52, 4)]
        rxo = view(32, 8, P)
        afull = view(40, 8)
        merged, mtmp = view(48, 8), view(56, 8)
        mix, sq2, tmp2 = view(0, 8), view(8, 8), view(16, 8)
        sq3 = view(24, 8)
        plx = view(56, 8)
        pT_s = view(80, 2)
        silu = work[:, 72 * T:74 * T]
        hid = [view(74, 2), view(76, 2), view(78, 2)]
        gated = work[:, 32 * T:34 * T]
        sgate = view(74, 4, 512)
        gtmp = work[:, 78 * T:80 * T]
        bias = view(0, 8)
        qa, ka = view(8, 4), view(12, 4)
        sqA, kxA = view(16, 8), view(16, 4, 512)
        va, vb = view(24, 4, 512), view(28, 4, 512)
        bcs2, rxc = view(56, 2), view(58, 2, P)
        c8, sqc, yc = view(32, 8), view(48, 8), view(64, 8)
        qb, kb, qsw, sqq, sqk = view(48, 8), view(56, 8), view(64, 8), view(72, 8), view(32, 8)
        kxB = view(72, 6, 96)
        probs = work[:, 16 * T:22 * T].rearrange("p (n t) -> p n t", t=384)
        out_a = view(76, 4)
        smx = work[:, 22 * T:22 * T + 24].rearrange("p (a b c) -> p a b c", a=2, b=3)
        probsT = work[:, 40 * T:46 * T].rearrange("p (n t) -> p n t", t=384)
        cosk, sink, cosq, sinq = (view(80 + i, 1) for i in range(4))
        kr, krs = view(84, 1), view(85, 1)
        ang, red = view(86, 1), view(87, 1)
        maskb_s = view(46, 1)
        oneh_s = view(86, 2, 512)
        bvec = view(80, 2, 512)
        rel_s = view(82, 1)

        block = ctx.enter_context(nc.Block())

        @block.sync
        def _(sp):
            sp.dma_start(x[:, 0:4, :], xT[:, 0:4, :]).then_inc(sem("x_in"), 16)
            sp.dma_start(x[:, 4:8, :], xT[:, 4:8, :]).then_inc(sem("x_in2"), 16)

            def load(u, slot):
                sp.dma_start(raw[:, slot, :], w[u]).then_inc(sem(f"raw_in{slot}"), 16)

            for u in range(RING):
                load(u, u)
            with sp.Fori(1, UNITS // RING) as i:
                for s in range(RING):
                    sp.wait_ge(sem("lo_ready"), i * RING + (s + 1 - RING))
                    sp.dma_start(raw[:, s, :], w[bass.ds(i * RING + s, 1)].rearrange("a p n -> (a p) n")).then_inc(sem(f"raw_in{s}"), 16)
            for u in range(UNITS // RING * RING, UNITS):
                sp.wait_ge(sem("lo_ready"), u + 1 - RING)
                load(u, u % RING)
            for b in range(4):
                sp.wait_ge(sem("out_ready"), b + 1)
                sp.dma_start(out[:, 2 * b:2 * b + 2, :], x[:, 2 * b:2 * b + 2, :]).then_inc(sem("out_sent"), 16)
            sp.wait_ge(sem("out_sent"), 64)

        @block.gpsimd
        def _(pool):
            pool.dma_start(par_s[:, :], par).then_inc(sem("par_in"), 16)
            pool.dma_start(cst_s[:, :], cst).then_inc(sem("cst_in"), 16)
            pool.dma_start(lnr_s, lnr).then_inc(sem("sg_in"), 16)
            pool.dma_start(sgw_s, sgw).then_inc(sem("sgw_in"), 16)
            pool.dma_start(sgb_s, sgb).then_inc(sem("sgb_in"), 16)
            pool.dma_start(lvl_s[:, :, :], lvl).then_inc(sem("lvl_in"), 16)
            nc.gpsimd.memset(half_s[:, :], -0.5).then_inc(sem("half"), 1)
            pool.wait_ge(sem("half"), 1)

            def token_factors(n):
                pool.wait_ge(sem("eps_added"), n + 1)
                w = 4 if NORMS[n] == "c" else 2
                nc.gpsimd.tensor_tensor(rtok[:, n, 0:w], eps_s[:, 0:w], half_s[:, 0:w], ALU.pow).then_inc(sem("rtok"), 1)

            token_factors(0)
            pool.wait_ge(sem("act_lo"), before("lo", "b") + 2)
            pool.wait_ge(sem("norm_stats"), before("st", "o") + 1)
            pool.dma_start(pT_s, pT).then_inc(sem("p_in"), 16)
            for n in range(1, 4):
                token_factors(n)
            pool.wait_ge(sem("act_lo"), before("lo", "p") + 1)
            pool.wait_ge(sem("ff_x"), 4)
            pool.dma_start(oneh_s[0:33, 0, :], oneh).then_inc(sem("oneh_in"), 16)
            pool.wait_ge(sem("rel_one"), 1)
            pool.dma_start(rel_s[0:32, 0, 0:HEADS], rel).then_inc(sem("rel_in"), 16)
            pool.wait_ge(sem("bvec"), 1)
            pool.dma_start(scratch, bvec[0:HEADS, 0, :]).then_inc(sem("scr_out"), 16)
            pool.wait_ge(sem("scr_out"), 16)
            pool.dma_start(bias[:, :, :], bass.AP(scratch.tensor, 0, [[1, P], [512, HEADS], [1, T]])).then_inc(sem("bias_in"), 16)
            pool.dma_start(ang[64:96, 0, :].bitcast(I32), pos[0:1, :].broadcast_to([32, T])).then_inc(sem("pos_in"), 16)
            token_factors(4)
            token_factors(5)
            pool.wait_ge(sem("act_lo"), before("lo", "c") + 4)
            pool.dma_start(maskb_s[:, 0, :], maskb).then_inc(sem("maskb_in"), 16)
            for s in ("bias_in", "pos_in", "maskb_in"):
                pool.wait_ge(sem(s), 16)
            token_factors(6)

        @block.scalar
        def _(act):
            A = nc.scalar.activation

            def split_hi(u, slot=None, rounds=None):
                if slot is None:
                    slot, rounds = u % RING, u // RING
                act.wait_ge(sem(f"raw_in{slot}"), rounds * 16 + 16)
                if not isinstance(u, int) or u >= RING:
                    act.wait_ge(sem("unit_used"), u + 1 - RING)
                A(whi[:, slot, :], raw[:, slot, :], ACT.Copy).then_inc(sem("hi_ready"), 1)

            def ahead(u):
                if u + RING < UNITS:
                    split_hi(u + RING)

            def filled(u):
                act.wait_ge(sem("unit_used"), u + 1)

            def evac(u, outs, func, b=None, **kw):
                b = u % RING if b is None else b
                src = two(ps[b][:, :]) if len(outs.shape) == 3 else ps[b][:, :]
                return A(outs, src, func, **kw).then_inc(sem(f"evac{b}"), 1)

            def split_x(name, y, dst, groups, n):
                for k in range(groups):
                    act.wait_ge(sem("act_y"), before("y", name) + n * (k + 1))
                    t = y.shape[1] // groups
                    A(xh[:, dst + k * t:dst + (k + 1) * t, :], y[:, k * t:(k + 1) * t, :], ACT.Copy)\
                        .then_inc(sem("act_hi"), 1)

            def gained_hi(name, gain, dst, k):
                for t in (2 * k, 2 * k + 1):
                    ins = A(xh[:, dst + t, :], x[:, t, :], ACT.Copy, scale=col(gain, t))
                ins.then_inc(sem("act_hi"), 1)

            def activated(u, dst, func, source=None, last=True, **kw):
                act.wait_ge(sem(f"evac{u % RING}"), FILLS[u][u % RING] + 1)
                ins = A(dst, dst if source is None else source, func, **kw)
                if last:
                    ins.then_inc(sem("z_act"), 1)

            def bc_copy(name):
                act.wait_ge(sem("norm_bc"), before("bc", name) + 1)
                A(bcs[:, :], ps[7][:, T:2 * T], ACT.Copy).then_inc(sem("norm_bcs"), 1)

            for k in range(2):
                act.wait_ge(sem(("x_in", "x_in2")[k]), 16)
                A(sq1[:, 4 * k:4 * k + 4, :], x[:, 4 * k:4 * k + 4, :], ACT.Square).then_inc(sem("norm_sq"), 1)
            act.wait_ge(sem("par_in"), 16)
            split_hi(0)
            for k in range(4):
                gained_hi("n1", "mix_pre", 0, k)
            split_hi(1)
            split_hi(2)
            act.wait_ge(sem("gam_sub"), 1)
            A(lb[:, 1, :], lb[:, 0, :], ACT.Exp).then_inc(sem("gam_exp"), 1)
            ahead(U_ZV)
            ahead(U_ZV + 1)

            filled(U_ZV + 1)
            act.wait_ge(sem("rtok"), 1)
            for s in range(2):
                evac(U_ZV + s, zv[:, s, :], ACT.Gelu, scale=rtok[:, 0, s:s + 1])
            bc_copy("n1")
            for m in range(2):
                u = U_ZU + m
                ahead(u)
                activated(u, zu[:, 2 * m:2 * m + 2, :], ACT.Gelu)
            steps = hgrn_schedule()

            def both_ways(g, lv):
                if lv > 1:
                    act.wait_ge(sem(f"tree{g}"), lv - 1)
                else:
                    act.wait_ge(sem("ksum"), g + 1)
                kc = G[g]["Kc"].rearrange("p h (n two w) -> p (h n) two w", two=2, w=1 << (lv - 1))
                A(kc, alternating(G[g]["K"], lv, 0), ACT.Copy).then_inc(sem("Kc"), 1)

            def hgrn_act(kind, g, lv):
                H = G[g]
                if kind == "level" and (g, lv) == (1, 1):
                    both_ways(g, lv)
                if kind == "level" and lv in (0, 8):
                    act.wait_ge(sem(f"lv_mm{g}"), lv + 1)
                    for s in range(2):
                        cols = (s if lv == 0 else 1 - s) * P
                        A(H["S"][:, s, :, cols:cols + P], ps[3 + 2 * g + s][:, :].rearrange("p (h t) -> p h t", h=4),
                          ACT.Copy).then_inc(sem(f"lv_copy{g}"), 1)
                if kind == "pv":
                    act.wait_ge(sem(f"pv_mm{g}"), 1)
                    for s in range(2):
                        src = ps[3 + 2 * g + s][:, :].rearrange("p (h t) -> p h t", h=2)
                        A(H["q"][:, 2 * s:2 * s + 2, :], src, ACT.Copy)
                        A(sqo[g][:, 2 * s:2 * s + 2, :], src, ACT.Square).then_inc(sem(f"o_sq{g}"), 1)

            for u in range(4, 32):
                for kind, g, lv in steps.get(u, ()):
                    if kind == "level" and 1 <= lv <= 7 and (g, lv) != (1, 1):
                        both_ways(g, lv)
                ahead(u)
                if u < U_ZI:
                    g, r = divmod(u - 4, 6)
                    part, m = divmod(r, 2)
                    H = G[g]
                    if part == 0:
                        activated(u, H["q"][:, 2 * m:2 * m + 2, :], ACT.Silu)
                    else:
                        F_, K_ = (H[n][part - 1][:, 2 * m:2 * m + 2, :] for n in ("F", "K"))
                        activated(u, F_, ACT.Sigmoid, source=K_)
                        act.wait_ge(sem("z_act"), z_index(u) + 1)
                        A(K_, K_, ACT.Sigmoid, scale=-1.0).then_inc(sem("z_k"), 1)
                        act.wait_ge(sem("lb"), 1)
                        act.wait_ge(sem("z_k"), k_index(u) + 1)
                        for h in (2 * m, 2 * m + 1):
                            c = 8 * (part - 1) + 4 * g + h
                            A(H["F"][part - 1][:, h, :], H["F"][part - 1][:, h, :], ACT.Identity, scale=lb[:, 2, c:c + 1],
                              bias=lb[:, 0, c:c + 1])
                            ins = A(H["K"][part - 1][:, h, :], H["K"][part - 1][:, h, :], ACT.Copy, scale=lb[:, 2, c:c + 1])
                        ins.then_inc(sem("gates"), 1)
                elif u < U_GA:
                    if (u - U_ZI) % 2 == 1:
                        filled(u)
                        half = (u - U_ZI) // 2
                        for s in range(2):
                            evac(u - 1 + s, zi[:, s, half * 512:half * 512 + 512], ACT.Copy, scale=rtok[:, 0, s:s + 1])
                else:
                    dst, func, m = ((ga, ACT.Sigmoid, u - U_GA) if u < U_ZG else
                                    (zg, ACT.Silu, u - U_ZG) if u < U_GB else (gb, ACT.Sigmoid, u - U_GB))
                    activated(u, dst[:, 2 * m:2 * m + 2, :], func)
                for step in steps.get(u, ()):
                    hgrn_act(*step)
                if u == U_GB + 1:
                    split_x("a", afull, 8, 2, 1)
            filled(U_GB + 3)
            for k in range(2):
                A(xh[:, 2 * k:2 * k + 2, :], bout[:, 2 * k:2 * k + 2, :], ACT.Copy).then_inc(sem("act_hi"), 1)
            for u in range(U_WA, U_WOUT):
                ahead(u)
            split_x("m", merged, 8, 4, 1)
            for m in range(4):
                u = U_WOUT + m
                ahead(u)
                filled(u)
                A(sq2[:, 2 * m:2 * m + 2, :], two(ps[u % RING][:, :]), ACT.Square)
                for t in range(2):
                    ins = A(mix[:, 2 * m + t, :], ps[u % RING][:, t * T:(t + 1) * T], ACT.Copy, scale=col("mix_post", 2 * m + t))
                ins.then_inc(sem(f"evac{u % RING}"), 1)
                if m == 1:
                    act.wait_ge(sem("p_in"), 16)
                    A(xh[:, 6:8, :], pT_s, ACT.Copy).then_inc(sem("act_hi"), 1)
            for k in range(4):
                act.wait_ge(sem("n2_x"), k + 1)
                gained_hi("n3", "ffn_pre", 8, k)
                A(sq3[:, 2 * k:2 * k + 2, :], x[:, 2 * k:2 * k + 2, :], ACT.Square).then_inc(sem("norm_sq"), 1)
            ahead(U_PLE)
            filled(U_PLE)
            for b in range(4):
                A(plx[:, 2 * b:2 * b + 2, :], two(ps[3 + b][:, :]), ACT.Copy).then_inc(sem("ple_copy"), 1)

            def silu_pair(j):
                act.wait_ge(sem("gate_r"), j + 1)
                A(silu, silu, ACT.Silu).then_inc(sem("silu"), 1)

            def hidden_hi(j, hidden_name, tile, slot_h):
                act.wait_ge(sem(hidden_name + "_y"), j + 1)
                A(xh[:, tile:tile + 2, :], hid[slot_h], ACT.Copy).then_inc(sem(hidden_name + "_hi"), 1)

            def split_at(i, k):
                split_hi(6 * i + k, k % RING, 2 * i + k // RING)

            split_hi(U_F1 + RING)
            bc_copy("n3")
            split_hi(U_F1 + 1 + RING)
            silu_pair(0)
            hidden_hi(0, "hid", 0, 0)
            with act.Fori(0, (PAIRS1 - 1) // 2) as i:
                for c in range(2):
                    k = U_F1 + 2 + 3 * c
                    split_at(i, k + RING)
                    silu_pair(2 * i + (1 + c))
                    split_at(i, k + 1 + RING)
                    hidden_hi(2 * i + (1 + c), "hid", 2 * ((1 + c) % 2), (1 + c) % 2)
                    split_at(i, k + 2 + RING)
            for b in range(4):
                if b < 3:
                    act.wait_ge(sem("ff_bank"), b + 1)
                else:
                    filled(U_PG - 1)
                A(sq2[:, 2 * b:2 * b + 2, :], two(ps[3 + b][:, :]), ACT.Square).then_inc(sem("norm_sq"), 1)
            ahead(U_PG - 1)
            bc_copy("n4")

            for k in range(4):
                act.wait_ge(sem("ff_x"), k + 1)
                A(xh[:, 2 * k:2 * k + 2, :], x[:, 2 * k:2 * k + 2, :], ACT.Copy).then_inc(sem("act_hi"), 1)
            for m in range(4):
                u = U_PG + m
                ahead(u)
                if m:
                    act.wait_ge(sem("pg_x"), m)
                    gained_hi("n5", "mix2", 8, m - 1)
                    A(sq3[:, 2 * m - 2:2 * m, :], x[:, 2 * m - 2:2 * m, :], ACT.Square).then_inc(sem("norm_sq"), 1)
                filled(u)
                evac(u, sgate[:, m % 2, :], ACT.Sigmoid)
            act.wait_ge(sem("pg_x"), 4)
            gained_hi("n5", "mix2", 8, 3)
            A(sq3[:, 6:8, :], x[:, 6:8, :], ACT.Square).then_inc(sem("norm_sq"), 1)

            for m in range(4):
                u = U_QA + m
                if m == 0:
                    ahead(u)
                    ahead(u + 1)
                    bc_copy("n5")
                elif m >= 2:
                    ahead(u)
                act.wait_ge(sem(f"evac{u % RING}"), FILLS[u][u % RING] + 1)
                A(sqA[:, 2 * m:2 * m + 2, :], (qa if m < 2 else ka)[:, 2 * (m % 2):2 * (m % 2) + 2, :], ACT.Square)\
                    .then_inc(sem("qk_sq"), 1)
            ahead(U_VA)
            act.wait_ge(sem("ang"), 1)
            A(sink[64:96, 0, :], red[64:96, 0, :], ACT.Sin).then_inc(sem("sin"), 1)
            act.wait_ge(sem("ang"), 2)
            A(cosk[64:96, 0, :], ang[64:96, 0, :], ACT.Sin).then_inc(sem("sin"), 1)
            ahead(U_VA + 1)
            filled(U_VA + 1)
            for s in range(2):
                evac(U_VA + s, va[:, s, :], ACT.Copy, scale=rtok[:, 4, s:s + 1])

            def head_pair_filled(name, half, u):
                if half == 3:
                    filled(u)
                else:
                    act.wait_ge(sem(name + "_mm"), half + 1)

            def softmax_exp(p):
                act.wait_ge(sem("head_max"), p + 1)
                for hh in range(2):
                    for s in range(2):
                        sl = slice(0, P) if s == 0 else slice(P, 384)
                        k = 2 * hh + s
                        A(probs[:, 2 * (p % 2) + hh, sl], probs[:, 2 * (p % 2) + hh, sl], ACT.Exp,
                          bias=smx[:, p % 2, 1, k:k + 1], accum_out=smx[:, p % 2, 2, k:k + 1]).then_inc(sem("head_exp"), 1)

            def probs_copy(p):
                act.wait_ge(sem("head_tr"), p + 1)
                for hh in range(2):
                    A(probsT[:, 2 * (p % 2) + hh, :], ps[5 + hh][:, 0:384], ACT.Copy).then_inc(sem("head_trc"), 1)

            def heads_hi(p):
                act.wait_ge(sem("head_pv"), p + 1)
                A(out_a[:, p, :] if p < 4 else xh[:, 8 + p, :], ps[7][:, 0:T], ACT.Copy).then_inc(sem("head_mh"), 1)

            for m in range(4):
                u = U_CQ + m
                ahead(u)
                act.wait_ge(sem(f"evac{u % RING}"), FILLS[u][u % RING] + 1)
                A(sqc[:, 2 * m:2 * m + 2, :], c8[:, 2 * m:2 * m + 2, :], ACT.Square).then_inc(sem("c_sq"), 1)
                softmax_exp(m)
                if m >= 1:
                    probs_copy(m - 1)
                if m == 2:
                    heads_hi(0)
            act.wait_ge(sem("norm_bc"), before("bc", "c") + 1)
            A(bcs2[:, :, :], two(ps[7][:, :]), ACT.Copy).then_inc(sem("norm_bcs"), 1)
            for k in range(4):
                act.wait_ge(sem("act_y"), before("y", "c") + k + 1)
                A(xh[:, 2 * k:2 * k + 2, :], yc[:, 2 * k:2 * k + 2, :], ACT.Copy).then_inc(sem("act_hi"), 1)
                if k == 0:
                    heads_hi(1)
                    probs_copy(3)
            u = U_KR
            ahead(u)
            act.wait_ge(sem("evac0"), FILLS[u][0] + 1)
            act.wait_ge(sem("act_lo"), before("lo", "c") + 4)
            A(sqk[64:96, :, :], kr[64:96, 0:1, :].broadcast_to([32, HEADS, T]), ACT.Square).then_inc(sem("kr_sq"), 1)
            filled(u)
            evac(u, vb[:, 0, :], ACT.Copy, b=1)
            evac(u, vb[:, 1, :], ACT.Copy, b=2)
            heads_hi(2)
            for half in range(4):
                if half == 3:
                    ahead(U_UK)
                head_pair_filled("uk", half, U_UK)
                b = (U_UK + half) % RING
                src = ps[b][0:64, :].rearrange("p (h t) -> p h t", h=2)
                hs = slice(2 * half, 2 * half + 2)
                A(sqk[0:64, hs, :], src, ACT.Square)
                A(kb[0:64, hs, :], src, ACT.Copy, scale=col("kb", 0, 0, 64)).then_inc(sem("uk_ev"), 1)
            heads_hi(3)
            act.wait_ge(sem("head_mh"), 4)
            A(xh[:, 8:12, :], out_a, ACT.Copy).then_inc(sem("out_a_hi"), 1)
            for n in range(3):
                ahead(U_UQ + n)
                for half in ((0,), (1,), (2, 3))[n]:
                    head_pair_filled("uq", half, U_UQ + 2)
                    b = half % RING
                    src = ps[b][0:96, :].rearrange("p (h t) -> p h t", h=2)
                    hs = slice(2 * half, 2 * half + 2)
                    if half == 2:
                        act.wait_ge(sem("out_a_lo"), 1)
                    A(sqq[0:96, hs, :], src, ACT.Square)
                    A(qsw[64:96, hs, :], ps[b][96:128, :].rearrange("p (h t) -> p h t", h=2), ACT.Copy)
                    A(qb[0:96, hs, :], src, ACT.Copy, scale=col("qb", 0, 0, 96)).then_inc(sem("uq_ev"), 1)
            ahead(U_WO)
            ahead(U_WO + 1)
            softmax_exp(4)
            for p in range(4):
                if p < 3:
                    softmax_exp(5 + p)
                probs_copy(4 + p)
                if p:
                    heads_hi(3 + p)
            heads_hi(7)
            for m in range(4):
                if m % 2 == 0:
                    ahead(U_WO + 2 + m // 2)
                act.wait_ge(sem("wo_x"), 4 + m + 1)
                gained_hi("n6", "ffn2", 0, m)
                A(sq3[:, 2 * m:2 * m + 2, :], x[:, 2 * m:2 * m + 2, :], ACT.Square).then_inc(sem("norm_sq"), 1)

            def relu_pair(j, u, bank):
                act.wait_ge(sem("unit_used"), u + 1)
                if not isinstance(j, int) or j >= 1:
                    act.wait_ge(sem("hid2_y"), j)
                A(silu, ps[bank][:, :], ACT.Relu).then_inc(sem("relu"), 1)

            split_hi(U_F2 + RING)
            relu_pair(0, U_F2, U_F2 % RING)
            hidden_hi(0, "hid2", 8, 0)
            with act.Fori(0, (PAIRS2 - 1) // 3 - 1) as i:
                for c in range(3):
                    k = U_F2 + 1 + 2 * c
                    split_at(i, k + RING)
                    relu_pair(3 * i + (1 + c), 6 * i + k, k % RING)
                    hidden_hi(3 * i + (1 + c), "hid2", 8 + 2 * ((1 + c) % 3), (1 + c) % 3)
                    split_at(i, k + 1 + RING)
            for j in range(PAIRS2 - 3, PAIRS2):
                u = U_F2 + 2 * j - 1
                ahead(u)
                relu_pair(j, u, u % RING)
                hidden_hi(j, "hid2", 8 + 2 * (j % 3), j % 3)
                ahead(u + 1)
            bc_copy("n6")

        @block.vector
        def _(dve):
            V = nc.vector
            chained = [0]

            def count(ins):
                chained[0] += 1
                ins.then_inc(sem("dve_chain"), 1)

            def link(ins):
                count(ins)
                dve.wait_ge(sem("dve_chain"), chained[0])

            def split_lo(u, slot=None):
                slot = u % RING if slot is None else slot
                dve.wait_ge(sem("hi_ready"), u + 1)
                V.tensor_tensor(wlo[:, slot, :], raw[:, slot, :], whi[:, slot, :].bitcast(F32), ALU.subtract)\
                    .then_inc(sem("lo_ready"), 1)

            def ahead(u):
                if u + RING < UNITS:
                    split_lo(u + RING)

            def evacuated(u):
                b = u % RING
                dve.wait_ge(sem(f"evac{b}"), FILLS[u][b] + 1)

            def rsqrt(src, dst, n):
                v, y, a, b2 = (nt[:, i, 0:n] for i in range(4))
                link(V.tensor_scalar(v, src, EPS, None, ALU.add))
                link(V.tensor_scalar(nti[:, 0:n], v.bitcast(I32), 1, None, ALU.logical_shift_right))
                link(V.tensor_scalar(y.bitcast(I32), nti[:, 0:n], -1.0, 1597463007.0, ALU.mult, ALU.add))
                for it in range(3):
                    link(V.tensor_tensor(a, y, y, ALU.mult))
                    link(V.scalar_tensor_tensor(b2, a, -0.5, v, ALU.mult, ALU.mult))
                    o = dst if it == 2 else y
                    link(V.scalar_tensor_tensor(o, b2, 1.5, y, ALU.add, ALU.mult))

            def norm_factors(name, n, w=2):
                dve.wait_ge(sem("norm_stats"), before("st", name) + 1)
                V.tensor_scalar(eps_s[:, 0:w], ps[7][:, 0:w], EPS, None, ALU.add).then_inc(sem("eps_added"), 1)
                dve.wait_ge(sem("rtok"), n + 1)
                V.tensor_copy((rx if w == 2 else rxc)[:, :, :], rtok[:, n, 0:w].unsqueeze(2).broadcast_to([P, w, P])).then_inc(sem("norm_factors"), 1)

            def fold(sq):
                for n in (4, 2, 1):
                    ins = V.tensor_tensor(sq[:, 0:n, :], sq[:, 0:n, :], sq[:, n:2 * n, :], ALU.add)
                    if n > 1:
                        link(ins)
                ins.then_inc(sem("folded"), 1)

            def fold_pair(sq, k):
                if k:
                    link(V.tensor_tensor(sq[:, 0:2, :], sq[:, 0:2, :], sq[:, 2 * k:2 * k + 2, :], ALU.add))
                if k == 3:
                    V.tensor_tensor(sq[:, 0, :], sq[:, 0, :], sq[:, 1, :], ALU.add).then_inc(sem("folded"), 1)

            def gained_lo(name, gain, dst, k):
                dve.wait_ge(sem("act_hi"), before("hi", name) + k + 1)
                for t in (2 * k, 2 * k + 1):
                    ins = V.scalar_tensor_tensor(xl[:, dst + t, :], x[:, t, :], col(gain, t), xh[:, dst + t, :].bitcast(F32),
                                                 ALU.mult, ALU.subtract)
                ins.then_inc(sem("act_lo"), 1)

            def factors_by_tile(n):
                return bcs[:, :].unsqueeze(1).broadcast_to([P, n, T])

            def scaled(u, dst):
                dve.wait_ge(sem("unit_used"), u + 1)
                V.tensor_tensor(dst, two(ps[u % RING][:, :]), factors_by_tile(2), ALU.mult).then_inc(sem(f"evac{u % RING}"), 1)

            def activated(u):
                dve.wait_ge(sem("z_act"), z_index(u) + 1)

            def split_x(name, y, dst, groups):
                for k in range(groups):
                    t = y.shape[1] // groups
                    dve.wait_ge(sem("act_hi"), before("hi", name) + k + 1)
                    V.tensor_tensor(xl[:, dst + k * t:dst + (k + 1) * t, :], y[:, k * t:(k + 1) * t, :],
                                    xh[:, dst + k * t:dst + (k + 1) * t, :].bitcast(F32), ALU.subtract)\
                        .then_inc(sem("act_lo"), 1)

            dve.wait_ge(sem("par_in"), 16)
            dve.wait_ge(sem("x_in"), 16)
            dve.wait_ge(sem("x_in2"), 16)
            split_lo(0)
            for k in range(4):
                gained_lo("n1", "mix_pre", 0, k)
            dve.wait_ge(sem("norm_sq"), 2)
            fold(sq1)
            split_lo(1)
            gam = par_s[:, PAR["gamma"]:PAR["gamma"] + 16]
            V.tensor_tensor(lb[:, 0, :], gam, gam, ALU.subtract).then_inc(sem("gam_sub"), 1)
            split_lo(2)
            dve.wait_ge(sem("gam_exp"), 1)
            link(V.reciprocal(lb[:, 0, :], lb[:, 1, :]))
            link(V.tensor_tensor(lb[:, 1, :], lb[:, 1, :], lb[:, 0, :], ALU.mult))
            link(V.tensor_tensor(lb[:, 0, :], lb[:, 1, :], lb[:, 1, :], ALU.subtract))
            V.tensor_scalar(lb[:, 2, :], lb[:, 0, :], -1.0, 1.0, ALU.mult, ALU.add).then_inc(sem("lb"), 1)

            norm_factors("n1", 0)
            ahead(0)
            ahead(1)
            dve.wait_ge(sem("sg_in"), 16)
            bn = nt[:, 0, 0:12].rearrange("p (s n) -> p s n", s=2)
            mv = rs[:, 0:4].rearrange("p (s n) -> p s n", s=2)
            for s in range(2):
                evacuated(U_ZV + s)
                link(V.bn_stats(bn[:, s, :], zv[:, s, :]))
            for s in range(2):
                link(V.bn_aggr(mv[:, s, :], bn[:, s, :]))
            rsqrt(mv[:, :, 1], rs[:, 8:10], 2)
            for s in range(2):
                link(V.tensor_scalar(zv[:, s, :], zv[:, s, :], mv[:, s, 0:1], rs[:, 8 + s:9 + s], ALU.subtract, ALU.mult))
                link(V.tensor_tensor(zv[:, s, :], zv[:, s, :], lnr_s[:, 0, :], ALU.mult))
                V.tensor_tensor(vn[:, s, :], zv[:, s, :], lnr_s[:, 1, :], ALU.add).then_inc(sem("vn"), 1)

            steps = hgrn_schedule()

            def gates(g, part, m):
                dve.wait_ge(sem("gates"), k_index(U_Q[g] + 2 + 2 * part + m) + 1)
                fm = G[g]["F"][part][:, 2 * m:2 * m + 2, :]
                link(V.tensor_scalar(fm, fm, TINY, 1.0, ALU.max, ALU.min))

            def decay(g, d, level):
                if level == 0:
                    return G[g]["F"][d].rearrange("p h t -> p (h t)")
                if level == 1:
                    return t1[:, d, :]
                at = sum(4 * T >> i for i in range(2, level))
                return G[g]["F"][d].rearrange("p h t -> p (h t)")[:, at:at + (4 * T >> level)]

            def tree_update(g, lv):
                H = G[g]
                half = 1 << (lv - 1)
                for d in range(2):
                    pair = decay(g, d, lv - 1).rearrange("p (n two) -> p n two", two=2)
                    if lv < 7:
                        count(V.tensor_tensor(decay(g, d, lv), pair[:, :, 0], pair[:, :, 1], ALU.mult))
                    n = 4 * T // (2 * half)
                    for X, side in ((H["Q"][d], 1 - d), (H["K"][d], d)):
                        v = X.rearrange("p h (n two w) -> p (h n) two w", two=2, w=half)[:, :, side, :]
                        dec = pair[:, :, 1 - side:2 - side].broadcast_to([P, n, half])
                        last = V.tensor_tensor(v, v, dec, ALU.mult)
                        if d == 0 or X is H["Q"][d]:
                            count(last)
                last.then_inc(sem(f"tree{g}"), 1)
                dve.wait_ge(sem(f"tree{g}"), lv)

            def hgrn_dve(kind, g, lv):
                H = G[g]
                if kind == "prep":
                    V.tensor_tensor(H["ksum"], H["K"][0], H["K"][1], ALU.add).then_inc(sem("ksum"), 1)
                    activated(U_Q[g] + 1)
                    for d in range(2):
                        V.tensor_tensor(H["Q"][d], H["q"], H["F"][d], ALU.mult).then_inc(sem(f"q_init{g}"), 1)
                if kind == "level" and 1 <= lv <= 7:
                    dve.wait_ge(sem(f"lv_mm{g}"), lv + 1)
                    dve.wait_ge(sem("lvl_in"), 16)
                    if lv == 1:
                        dve.wait_ge(sem(f"lv_copy{g}"), 2)
                        dve.wait_ge(sem(f"q_init{g}"), 2)
                    for s in range(2):
                        V.copy_predicated(H["S"][:, s, :, s * P:(s + 1) * P],
                                          lvl_s[:, lv - 1, :].unsqueeze(1).broadcast_to([P, 4, P]),
                                          ps[3 + 2 * g + s][:, :].rearrange("p (h t) -> p h t", h=4))\
                            .then_inc(sem(f"lv_pred{g}"), 1)
                    dve.wait_ge(sem(f"lv_pred{g}"), 2 * lv)
                    tree_update(g, lv)

            dve.wait_ge(sem("norm_bcs"), 1)
            for u in range(2, 32):
                if u < U_Q[0]:
                    scaled(u, zu[:, 2 * (u - U_ZU):2 * (u - U_ZU) + 2, :])
                elif u < U_ZI:
                    g, r = divmod(u - 4, 6)
                    part, m = divmod(r, 2)
                    area = G[g]["K"][part - 1] if part else G[g]["q"]
                    scaled(u, area[:, 2 * m:2 * m + 2, :])
                elif u >= U_GA:
                    if u == U_GA:
                        dve.wait_ge(sem("lv_mm0"), 9)
                    area, m = (ga, zg, gb)[(u - U_GA) // 4], (u - U_GA) % 4
                    scaled(u, area[:, 2 * m:2 * m + 2, :])
                if U_Q[0] <= u < U_ZI and (u - 4) % 6 == 5:
                    gates((u - 4) // 6, 1, 1)
                    if u < U_Q[1]:
                        hgrn_dve("prep", 0, 0)
                for step in steps.get(u, ()):
                    hgrn_dve(*step)
                ahead(u)
                if u == U_ZI:
                    hgrn_dve("prep", 1, 0)
                if u == U_ZU + 1:
                    dve.wait_ge(sem("sgb_in"), 16)
                if u == 5:
                    for b in range(2):
                        dve.wait_ge(sem("sg_mm"), b + 1)
                        s2 = sgb_s[:, 2 * b:2 * b + 2, :].unsqueeze(2).broadcast_to([P, 2, 2, P])
                        o4 = bout[:, 2 * b:2 * b + 2, :].rearrange("p j (s t) -> p j s t", s=2)
                        link(V.tensor_tensor(o4, ps[3 + b][:, :].rearrange("p (j s t) -> p j s t", j=2, s=2), s2, ALU.add))
                    activated(U_ZU + 1)
                    V.tensor_tensor(bout, bout, zu, ALU.mult).then_inc(sem("b_out"), 1)
                if 4 <= u < U_ZI:
                    g, r = divmod(u - 4, 6)
                    part, m = divmod(r, 2)
                    if part and r < 5:
                        gates(g, part - 1, m)
                if u == U_GB:
                    dve.wait_ge(sem("norm_stats"), before("st", "o") + 1)
                    rsqrt(ps[7][:, 0:16], rs[:, 0:16], 16)
                    V.tensor_copy(rxo, rs[:, 0:16].unsqueeze(2).broadcast_to([P, 16, P])).then_inc(sem("norm_factors"), 1)
                if u == U_GB + 1:
                    for h in range(HEADS):
                        if h % 2 == 0:
                            dve.wait_ge(sem("norm_bc"), before("bc", "o") + h // 2 + 1)
                        link(V.scalar_tensor_tensor(afull[:, h, :], G[h // 4]["q"][:, h % 4, :], col("hg_norm", h),
                                                    ps[3 + h // 2][:, (h % 2) * T:(h % 2 + 1) * T], ALU.mult, ALU.mult))
                    activated(U_ZG + 3)
                    for k in range(2):
                        V.tensor_tensor(afull[:, 4 * k:4 * k + 4, :], afull[:, 4 * k:4 * k + 4, :],
                                        zg[:, 4 * k:4 * k + 4, :], ALU.mult).then_inc(sem("act_y"), 1)
                    split_x("a", afull, 8, 2)
            for k in range(2):
                dve.wait_ge(sem("act_hi"), before("hi", "b") + k + 1)
                V.tensor_tensor(xl[:, 2 * k:2 * k + 2, :], bout[:, 2 * k:2 * k + 2, :],
                                xh[:, 2 * k:2 * k + 2, :].bitcast(F32), ALU.subtract).then_inc(sem("act_lo"), 1)
            def merged_lo(k):
                dve.wait_ge(sem("act_hi"), before("hi", "m") + k + 1)
                V.tensor_tensor(xl[:, 8 + 2 * k:10 + 2 * k, :], merged[:, 2 * k:2 * k + 2, :],
                                xh[:, 8 + 2 * k:10 + 2 * k, :].bitcast(F32), ALU.subtract).then_inc(sem("act_lo"), 1)

            activated(U_GB + 3)
            for m in range(4):
                u = U_WA + m
                ahead(u)
                dve.wait_ge(sem("unit_used"), u + 1)
                V.tensor_tensor(ga[:, 2 * m:2 * m + 2, :], ga[:, 2 * m:2 * m + 2, :], two(ps[u % RING][:, :]),
                                ALU.mult).then_inc(sem(f"evac{u % RING}"), 1)
            for n in range(2):
                u = U_WB + n
                ahead(u)
                dve.wait_ge(sem("unit_used"), u + 1)
                if n == 0:
                    for m in range(4):
                        evacuated(U_WA + m)
                for b in range(2):
                    t = slice(4 * n + 2 * b, 4 * n + 2 * b + 2)
                    link(V.tensor_tensor(mtmp[:, t, :], gb[:, t, :], two(ps[3 + 2 * n + b][:, :]), ALU.mult))
                    V.tensor_tensor(merged[:, t, :], mtmp[:, t, :], ga[:, t, :], ALU.add).then_inc(sem("act_y"), 1)
                    if 2 * n + b:
                        merged_lo(2 * n + b - 1)
            merged_lo(3)
            for m in range(4):
                ahead(U_WOUT + m)
                if m == 2:
                    dve.wait_ge(sem("act_hi"), before("hi", "p") + 1)
                    V.tensor_tensor(xl[:, 6:8, :], pT_s, xh[:, 6:8, :].bitcast(F32), ALU.subtract).then_inc(sem("act_lo"), 1)
            for k in range(4):
                evacuated(U_WOUT + k)
                fold_pair(sq2, k)
            norm_factors("n2", 1)
            dve.wait_ge(sem("norm_bc"), before("bc", "n2") + 1)
            fac = ps[7][:, T:2 * T].unsqueeze(1).broadcast_to([P, 2, T])
            for k in range(4):
                t = slice(2 * k, 2 * k + 2)
                V.tensor_tensor(tmp2[:, t, :], mix[:, t, :], fac, ALU.mult).then_inc(sem("act_y"), 1)
                dve.wait_ge(sem("act_y"), before("y", "n2") + k + 1)
                V.tensor_tensor(x[:, t, :], x[:, t, :], tmp2[:, t, :], ALU.add).then_inc(sem("n2_x"), 1)
                if k:
                    gained_lo("n3", "ffn_pre", 8, k - 1)
            gained_lo("n3", "ffn_pre", 8, 3)
            ahead(U_PLE)

            def gate_scaled(j, u, bank):
                dve.wait_ge(sem("unit_used"), u + 1)
                if not isinstance(j, int) or j >= 1:
                    dve.wait_ge(sem("gated"), j)
                V.tensor_tensor(two(silu), two(ps[bank][:, :]), factors_by_tile(2), ALU.mult).then_inc(sem("gate_r"), 1)

            def hidden(j, slot_h, u_up, bank):
                dve.wait_ge(sem("silu"), j + 1)
                if not isinstance(j, int) or j >= 1:
                    dve.wait_ge(sem("hid_y"), j)
                V.tensor_tensor(two(gated), two(silu), factors_by_tile(2), ALU.mult).then_inc(sem("gated"), 1)
                dve.wait_ge(sem("unit_used"), u_up + 1)
                dve.wait_ge(sem("gated"), j + 1)
                if not isinstance(j, int) or j >= 1:
                    dve.wait_ge(sem("hid_lo"), j)
                V.tensor_tensor(hid[slot_h], two(gated), two(ps[bank][:, :]), ALU.mult).then_inc(sem("hid_y"), 1)

            def hidden_lo(j, slot_h, hidden_name, base):
                dve.wait_ge(sem(hidden_name + "_hi"), j + 1)
                V.tensor_tensor(xl[:, base + 2 * slot_h:base + 2 * slot_h + 2, :], hid[slot_h],
                                xh[:, base + 2 * slot_h:base + 2 * slot_h + 2, :].bitcast(F32), ALU.subtract)\
                    .then_inc(sem(hidden_name + "_lo"), 1)

            split_lo(U_F1 + RING)
            dve.wait_ge(sem("norm_sq"), before("sq", "n3") + 4)
            fold(sq3)
            norm_factors("n3", 2)
            dve.wait_ge(sem("norm_bcs"), before("bcs", "n3") + 1)
            gate_scaled(0, U_F1, U_F1 % RING)
            split_lo(U_F1 + 1 + RING)
            hidden(0, 0, U_F1 + 1, (U_F1 + 1) % RING)
            hidden_lo(0, 0, "hid", 0)
            with dve.Fori(0, (PAIRS1 - 1) // 2) as i:
                for c in range(2):
                    j = 2 * i + (1 + c)
                    u = 6 * i + (U_F1 + 2 + 3 * c)
                    s0 = (U_F1 + 2) % RING
                    gate_scaled(j, u, s0)
                    split_lo(u + RING, s0)
                    split_lo(u + 1 + RING, (s0 + 1) % RING)
                    hidden(j, (1 + c) % 2, u + 1, (s0 + 1) % RING)
                    hidden_lo(j, (1 + c) % 2, "hid", 0)
                    split_lo(u + 2 + RING, (s0 + 2) % RING)
            def x_lo(k):
                dve.wait_ge(sem("act_hi"), before("hi", "ff") + k + 1)
                V.tensor_tensor(xl[:, 2 * k:2 * k + 2, :], x[:, 2 * k:2 * k + 2, :], xh[:, 2 * k:2 * k + 2, :].bitcast(F32),
                                ALU.subtract).then_inc(sem("act_lo"), 1)

            ahead(U_PG - 1)
            for k in range(4):
                dve.wait_ge(sem("norm_sq"), before("sq", "n4") + k + 1)
                fold_pair(sq2, k)
            norm_factors("n4", 3)
            dve.wait_ge(sem("norm_bcs"), before("bcs", "n4") + 1)
            for k in range(4):
                for t in range(2):
                    ins = V.scalar_tensor_tensor(tmp2[:, 2 * k + t, :], ps[3 + k][:, t * T:(t + 1) * T], col("ffn_post", 2 * k + t),
                                                 bcs[:, :], ALU.mult, ALU.mult)
                    if t == 0:
                        count(ins)
                ins.then_inc(sem("act_y"), 1)
                dve.wait_ge(sem("act_y"), before("y", "n4") + k + 1)
                V.tensor_tensor(x[:, 2 * k:2 * k + 2, :], x[:, 2 * k:2 * k + 2, :], tmp2[:, 2 * k:2 * k + 2, :], ALU.add)\
                    .then_inc(sem("ff_x"), 1)
                if k:
                    x_lo(k - 1)
            x_lo(3)
            dve.wait_ge(sem("ple_copy"), 4)
            for m in range(4):
                u = U_PG + m
                ahead(u)
                evacuated(u)
                if m == 0:
                    dve.wait_ge(sem("ff_x"), 4)
                    dve.wait_ge(sem("act_lo"), before("lo", "ff") + 4)
                else:
                    dve.wait_ge(sem("pg_x"), m)
                link(V.tensor_tensor(two(gtmp),
                                     two(sgate[:, m % 2, :]), plx[:, 2 * m:2 * m + 2, :], ALU.mult))
                V.tensor_tensor(x[:, 2 * m:2 * m + 2, :], x[:, 2 * m:2 * m + 2, :],
                                two(gtmp), ALU.add).then_inc(sem("pg_x"), 1)
                if m:
                    gained_lo("n5", "mix2", 8, m - 1)
                if m == 0:
                    dve.wait_ge(sem("oneh_in"), 16)
                    V.memset(rel_s[0:33, 0, 0:HEADS], 1.0).then_inc(sem("rel_one"), 1)
                if m == 3:
                    dve.wait_ge(sem("bv_mm"), 1)
                    V.tensor_copy(bvec[0:HEADS, 0, :], ps[3][0:HEADS, :]).then_inc(sem("bvec"), 1)
            gained_lo("n5", "mix2", 8, 3)
            ahead(U_QA)
            dve.wait_ge(sem("norm_sq"), before("sq", "n5") + 4)
            fold(sq3)
            norm_factors("n5", 4)
            ahead(U_QA + 1)
            def head_factors(name, width, kx):
                dve.wait_ge(sem("norm_stats"), before("st", name) + 1)
                rsqrt(ps[7][:, 0:32], rs[:, 0:32], 32)
                r3 = rs[:, 0:32].rearrange("p (s h) -> p s h", s=2)
                link(V.tensor_copy(kx, r3[:, :, 8:16].unsqueeze(3).broadcast_to([P, 2, HEADS, width])))
                V.tensor_scalar(r3[:, :, 0:8], r3[:, :, 0:8], float(np.float32(1.0 / np.sqrt(width))), None, ALU.mult)\
                    .then_inc(sem("norm_factors"), 1)

            def logits_row(p):
                dve.wait_ge(sem("head_qk"), p + 1)
                if p >= 2:
                    dve.wait_ge(sem("head_tr"), p - 1)
                for hh in range(2):
                    h = 2 * (p % 4) + hh
                    L = probs[:, 2 * (p % 2) + hh, :]
                    tab = bias_table(h) if p < 4 else mask_table()
                    V.scalar_tensor_tensor(L[:, 0:P], ps[3 + hh][:, 0:P], rs[:, h:h + 1], tab[0], ALU.mult, ALU.add)\
                        .then_inc(sem("head_l"), 1)
                    V.scalar_tensor_tensor(L[:, P:384], ps[3 + hh][:, P:384], rs[:, 16 + h:17 + h], tab[1], ALU.mult, ALU.add)\
                        .then_inc(sem("head_l"), 1)
                dve.wait_ge(sem("head_l"), 4 * p + 4)
                L2 = probs[:, 2 * (p % 2):2 * (p % 2) + 2, :]
                m4 = smx[:, p % 2, 0, :].rearrange("p (h s) -> p h s", s=2)
                V.reduce_max(m4[:, :, 0], L2[:, :, 0:P], AX).then_inc(sem("red"), 1)
                V.reduce_max(m4[:, :, 1], L2[:, :, P:384], AX).then_inc(sem("red"), 1)
                redn[0] += 2
                dve.wait_ge(sem("red"), redn[0])
                V.tensor_scalar(smx[:, p % 2, 1, :], smx[:, p % 2, 0, :], -1.0, None, ALU.mult).then_inc(sem("head_max"), 1)

            def normalise(p):
                dve.wait_ge(sem("head_exp"), 4 * p + 4)
                link(V.reciprocal(smx[:, p % 2, 0, :], smx[:, p % 2, 2, :]))
                for hh in range(2):
                    L = probs[:, 2 * (p % 2) + hh, :]
                    V.tensor_scalar(L[:, 0:P], L[:, 0:P], smx[:, p % 2, 0, 2 * hh:2 * hh + 1], None, ALU.mult).then_inc(sem("head_p"), 1)
                    V.tensor_scalar(L[:, P:384], L[:, P:384], smx[:, p % 2, 0, 2 * hh + 1:2 * hh + 2], None, ALU.mult).then_inc(sem("head_p"), 1)

            def heads_lo(p):
                dve.wait_ge(sem("head_mh"), p + 1)
                V.tensor_tensor(xl[:, 8 + p, :], ps[7][:, 0:T], xh[:, 8 + p, :].bitcast(F32), ALU.subtract)\
                    .then_inc(sem("head_ml"), 1)

            redn = [0]

            def bias_table(h):
                return bias[:, h, 127::-1], bias[:, h, ::-1]

            def mask_table():
                return maskb_s[:, 0, P:T], maskb_s[:, 0, :]

            dve.wait_ge(sem("norm_bcs"), before("bcs", "n5") + 1)
            for m in range(4):
                scaled(U_QA + m, (qa if m < 2 else ka)[:, 2 * (m % 2):2 * (m % 2) + 2, :])
                if m >= 2:
                    ahead(U_QA + m)
            V.tensor_tensor(gqk[:, :], col("qa"), col("ka"), ALU.mult).then_inc(sem("red"), 1)
            redn[0] += 1
            dve.wait_ge(sem("red"), redn[0])
            dve.wait_ge(sem("pos_in"), 16)
            a_, r_, c_ = ang[64:96, 0, :], red[64:96, 0, :], cosk[64:96, 0, :]
            link(V.tensor_copy(r_, a_.bitcast(I32)))
            link(V.tensor_scalar(a_, r_, cst_s[64:96, C_INVF:C_INVF + 1], None, ALU.mult))
            link(V.tensor_scalar(c_, a_, 1.0 / (2 * np.pi), 12582912.0, ALU.mult, ALU.add))
            link(V.tensor_scalar(c_, c_, 12582912.0, None, ALU.subtract))
            for part in TWO_PI:
                link(V.scalar_tensor_tensor(a_, c_, -part, a_, ALU.mult, ALU.add))
            lim = 3.1415925
            V.tensor_scalar(r_, a_, lim, -lim, ALU.min, ALU.max).then_inc(sem("ang"), 1)
            link(V.tensor_scalar(a_, a_, float(np.pi / 2), None, ALU.add))
            link(V.tensor_scalar(c_, a_, float(np.pi), -2 * float(np.pi), ALU.is_gt, ALU.mult))
            link(V.tensor_tensor(a_, a_, c_, ALU.add))
            V.tensor_scalar(a_, a_, lim, -lim, ALU.min, ALU.max).then_inc(sem("ang"), 1)
            head_factors("sa", 64, kxA.rearrange("p s (h w) -> p s h w", h=HEADS))
            ahead(U_VA)
            ahead(U_VA + 1)
            for b in range(2):
                dve.wait_ge(sem("norm_bc"), before("bc", "sa") + b + 1)
                V.scalar_tensor_tensor(ka[:, 2 * b:2 * b + 2, :], ka[:, 2 * b:2 * b + 2, :], gqk[:, 0:1],
                                       two(ps[3 + b][:, :]), ALU.mult, ALU.mult).then_inc(sem("ka_n"), 1)
            dve.wait_ge(sem("sin"), 2)
            sgn = cst_s[64:96, C_SIGN:C_SIGN + 1]
            link(V.tensor_copy(cosq[64:96, 0, :], cosk[64:96, 0, :]))
            link(V.tensor_scalar(sinq[64:96, 0, :], sink[64:96, 0, :], col("qb_swap", 0, 64, 96), sgn, ALU.mult, ALU.mult))
            link(V.tensor_scalar(sink[64:96, 0, :], sink[64:96, 0, :], col("kb_swap", 0, 64, 96), sgn, ALU.mult, ALU.mult))
            dve.wait_ge(sem("bias_in"), 16)
            for m in range(4):
                scaled(U_CQ + m, c8[:, 2 * m:2 * m + 2, :])
                if m == 3:
                    norm_factors("c", 5, 4)
                logits_row(m)
                if m:
                    normalise(m - 1)
                ahead(U_CQ + m)
            normalise(3)
            dve.wait_ge(sem("norm_bcs"), before("bcs", "c") + 1)
            for k in range(DT):
                gain = col("cq", k) if k < 6 else col("ckv", k - 6)
                ins = V.scalar_tensor_tensor(yc[:, k, :], c8[:, k, :], gain, bcs2[:, k // 6, :], ALU.mult, ALU.mult)
                if k % 2:
                    ins.then_inc(sem("act_y"), 1)
                else:
                    count(ins)
            split_x("c", yc, 0, 4)
            dve.wait_ge(sem("kr_mm"), 1)
            k_, s_ = kr[64:96, 0, :], krs[64:96, 0, :]
            link(V.tensor_tensor(s_, ps[0][96:128, 0:T], bcs[96:128, :], ALU.mult))
            V.tensor_tensor(k_, ps[0][64:96, 0:T], bcs[64:96, :], ALU.mult).then_inc(sem("evac0"), 1)
            ahead(U_KR)
            dve.wait_ge(sem("kr_sq"), 1)
            link(V.scalar_tensor_tensor(k_, k_, col("kb", 0, 64, 96), cosk[64:96, 0, :], ALU.mult, ALU.mult))
            link(V.tensor_tensor(s_, s_, sink[64:96, 0, :], ALU.mult))
            link(V.tensor_tensor(k_, k_, s_, ALU.add))
            ahead(U_UK)
            dve.wait_ge(sem("out_a_hi"), 1)
            V.tensor_tensor(xl[:, 8:12, :], out_a, xh[:, 8:12, :].bitcast(F32), ALU.subtract).then_inc(sem("out_a_lo"), 1)

            def rotate(half):
                dve.wait_ge(sem("uq_ev"), half + 1)
                hs = slice(2 * half, 2 * half + 2)
                q_, w_ = qb[64:96, hs, :], qsw[64:96, hs, :]
                V.tensor_tensor(q_, q_, cosq[64:96, 0:1, :].broadcast_to([32, 2, T]), ALU.mult).then_inc(sem("rot"), 1)
                V.tensor_tensor(w_, w_, sinq[64:96, 0:1, :].broadcast_to([32, 2, T]), ALU.mult).then_inc(sem("rot"), 1)
                dve.wait_ge(sem("rot"), 2 * half + 2)
                V.tensor_tensor(q_, q_, w_, ALU.add).then_inc(sem("q_rot"), 1)

            ahead(U_UQ)
            rotate(0)
            ahead(U_UQ + 1)
            rotate(1)
            ahead(U_UQ + 2)
            rotate(2)
            rotate(3)
            head_factors("sb", 96, kxB.rearrange("p (s h) w -> p s h w", s=2))
            dve.wait_ge(sem("uk_ev"), 4)
            for b in range(4):
                dve.wait_ge(sem("norm_bc"), before("bc", "sb") + b + 1)
                src = two(ps[b % RING][:, :])
                hs = slice(2 * b, 2 * b + 2)
                V.tensor_tensor(kb[0:64, hs, :], kb[0:64, hs, :], src[0:64], ALU.mult).then_inc(sem("kb_n"), 1)
                V.tensor_tensor(kb[64:96, hs, :], kr[64:96, 0:1, :].broadcast_to([32, 2, T]), src[64:96], ALU.mult)\
                    .then_inc(sem("kb_n"), 1)
            ahead(U_WO)

            def add_wo(m, bank):
                V.tensor_tensor(x[:, 2 * m:2 * m + 2, :], x[:, 2 * m:2 * m + 2, :], two(ps[bank][:, :]), ALU.add)\
                    .then_inc(sem("wo_x"), 1)

            dve.wait_ge(sem("unit_used"), U_WO + 2)
            for m, bank in enumerate((5, 6, 3, 4)):
                add_wo(m, bank)
            dve.wait_ge(sem("maskb_in"), 16)
            logits_row(4)
            ahead(U_WO + 1)
            for p in range(4):
                if p < 3:
                    logits_row(5 + p)
                normalise(4 + p)
                if p:
                    heads_lo(3 + p)
            heads_lo(7)
            for m, bank in enumerate((0, 1, 5, 6)):
                dve.wait_ge(sem("unit_used"), U_WO + 3 + m // 2)
                dve.wait_ge(sem("wo_x"), 4)
                add_wo(m, bank)
                if m:
                    gained_lo("n6", "ffn2", 0, m - 1)
                if m == 1:
                    ahead(U_WO + 2)
            gained_lo("n6", "ffn2", 0, 3)
            ahead(U_WO + 3)

            def relu_square(j, slot_h, slot):
                dve.wait_ge(sem("relu"), j + 1)
                if not isinstance(j, int) or j >= 1:
                    dve.wait_ge(sem("hid2_lo"), j)
                V.tensor_tensor(hid[slot_h], two(silu),
                                two(ps[slot][:, :]), ALU.mult).then_inc(sem("hid2_y"), 1)

            split_lo(U_F2 + RING)
            relu_square(0, 0, U_F2 % RING)
            hidden_lo(0, 0, "hid2", 8)
            dve.wait_ge(sem("norm_sq"), before("sq", "n6") + 4)
            fold(sq3)
            with dve.Fori(0, (PAIRS2 - 1) // 3 - 1) as i:
                for c in range(3):
                    u0 = 6 * i + (U_F2 + 1 + 2 * c)
                    s0 = (U_F2 + 1 + 2 * c) % RING
                    j = 3 * i + (1 + c)
                    split_lo(u0 + RING, s0)
                    relu_square(j, (1 + c) % 3, s0)
                    hidden_lo(j, (1 + c) % 3, "hid2", 8)
                    split_lo(u0 + 1 + RING, (s0 + 1) % RING)
            for j in range(PAIRS2 - 3, PAIRS2):
                u0 = U_F2 + 2 * j - 1
                ahead(u0)
                relu_square(j, j % 3, u0 % RING)
                hidden_lo(j, j % 3, "hid2", 8)
                ahead(u0 + 1)
                if j == PAIRS2 - 3:
                    norm_factors("n6", 6)
            dve.wait_ge(sem("norm_bcs"), before("bcs", "n6") + 1)
            link(V.tensor_tensor(bcs[:, :], bcs[:, :], bcs[:, :], ALU.mult))
            dve.wait_ge(sem("wo_x"), 8)
            for b in range(4):
                if b < 3:
                    dve.wait_ge(sem("out_bank"), b + 1)
                else:
                    dve.wait_ge(sem("unit_used"), UNITS)
                link(V.tensor_tensor(tmp2[:, 2 * b:2 * b + 2, :], two(ps[3 + b][:, :]), factors_by_tile(2), ALU.mult))
                V.tensor_tensor(x[:, 2 * b:2 * b + 2, :], x[:, 2 * b:2 * b + 2, :], tmp2[:, 2 * b:2 * b + 2, :],
                                ALU.add).then_inc(sem("out_ready"), 1)

        @block.tensor
        def _(pe):
            mm = nc.tensor.matmul

            def mm3(out, slot, at, tile, start, stop, width=P, skip=False):
                hi = whi[:, slot, at:at + width]
                mm(out, hi, xh[:, tile, :], start=start, stop=False, skip_group_check=skip)
                mm(out, hi, xl[:, tile, :], start=False, stop=False, skip_group_check=skip)
                return mm(out, wlo[:, slot, at:at + width], xh[:, tile, :], start=False, stop=stop, skip_group_check=skip)

            def arrived(u):
                pe.wait_ge(sem("lo_ready"), u + 1)

            def bank_free(u, b):
                if FILLS[u][b]:
                    pe.wait_ge(sem(f"evac{b}"), FILLS[u][b])

            def used(ins):
                ins.then_inc(sem("unit_used"), 1)

            def first_unit(u, base, x_name):
                arrived(u)
                bank_free(u, u % RING)
                for k in range(8):
                    if k % 2 == 0:
                        pe.wait_ge(sem("act_lo"), before("lo", x_name) + k // 2 + 1)
                    for m in range(2):
                        last = mm3(ps[u % RING][:, m * T:(m + 1) * T], u % RING, (8 * m + k) * P, base + k, k == 0 and m == 0,
                                   k == 7, skip=True)
                used(last)

            def two_tiles(u, base, x_name=None):
                arrived(u)
                bank_free(u, u % RING)
                for m in range(2):
                    for k in range(8):
                        if x_name and m == 0 and k % 4 == 0:
                            pe.wait_ge(sem("act_lo"), before("lo", x_name) + k // 4 + 1)
                        last = mm3(ps[u % RING][:, m * T:(m + 1) * T], u % RING, (8 * m + k) * P, base + k, k == 0, k == 7)
                used(last)

            def token_major(u0, base, x_name=None, between=None):
                for n in range(2):
                    u = u0 + n
                    arrived(u)
                    if n == 0:
                        for s in range(2):
                            bank_free(u0 + s, (u0 + s) % RING)
                    for s in range(2):
                        o = ps[(u0 + s) % RING][:, :]
                        for k in range(4):
                            t = base + 4 * n + k
                            if x_name and s == 0 and k % 2 == 0:
                                pe.wait_ge(sem("act_lo"), before("lo", x_name) + 2 * n + k // 2 + 1)
                            xs = slice(s * P, (s + 1) * P)
                            wc = slice(512 * k, 512 * k + 512)
                            first, end = n == 0 and k == 0, n == 1 and k == 3
                            mm(o, xh[:, t, xs], whi[:, u % RING, wc], start=first, stop=False)
                            mm(o, xl[:, t, xs], whi[:, u % RING, wc], start=False, stop=False)
                            last = mm(o, xh[:, t, xs], wlo[:, u % RING, wc], start=False, stop=end)
                    used(last)
                    if between and n == 0:
                        between()

            def norm_stats(name, sq):
                pe.wait_ge(sem("folded"), list(FOLDED).index(name) + 1)
                for s in range(2):
                    last = mm(ps[7][:, s:s + 1], sq[:, 0, s * P:(s + 1) * P], mean_col(MEAN_D), start=True, stop=True)
                last.then_inc(sem("norm_stats"), 1)

            def norm_bc(name):
                pe.wait_ge(sem("norm_factors"), before("rx", name) + 1)
                for s in range(2):
                    last = mm(ps[7][:, T + s * P:T + (s + 1) * P], rx[:, s, :], ident, start=True, stop=True)
                last.then_inc(sem("norm_bc"), 1)

            pe.wait_ge(sem("cst_in"), 16)
            token_major(U_ZV, 0, "n1")
            norm_stats("n1", sq1)
            steps = hgrn_schedule()

            def spatial_mix(b):
                pe.wait_ge(sem("sgw_in"), 16)
                pe.wait_ge(sem("vn"), 2)
                for j in (2 * b, 2 * b + 1):
                    for s in range(2):
                        for e in range(2):
                            g = 2 * j + e
                            c = (j % 2) * T + s * P
                            last = mm(ps[3 + b][64 * e:64 * e + 64, c:c + P], vn[:, s, g * 64:g * 64 + 64],
                                      sgw_s[:, g, :], start=True, stop=True)
                last.then_inc(sem("sg_mm"), 1)

            def hgrn_pe(kind, g, lv):
                H = G[g]
                if kind == "level":
                    banks = (ps[3 + 2 * g], ps[4 + 2 * g])
                    if lv == 0:
                        pe.wait_ge(sem("ksum"), g + 1)
                        pe.wait_ge(sem("b_out"), 1)
                        for s in range(2):
                            for h in range(4):
                                ts = slice(s * P, (s + 1) * P)
                                last = mm(banks[s][:, h * P:(h + 1) * P], H["ksum"][:, h, ts], H["q"][:, h, ts], start=True, stop=True)
                    elif lv <= 7:
                        pe.wait_ge(sem("Kc"), 7 * g + lv)
                        if lv == 1:
                            pe.wait_ge(sem(f"q_init{g}"), 2)
                            pe.wait_ge(sem(f"lv_copy{g}"), 2)
                        else:
                            pe.wait_ge(sem(f"tree{g}"), lv - 1)
                        for s in range(2):
                            for h in range(4):
                                last = mm(banks[s][:, h * P:(h + 1) * P], H["Kc"][:, h, s * P:(s + 1) * P],
                                          alternating(H["Q"], lv, 1, h * T + s * P, P), start=True, stop=True)
                    else:
                        pe.wait_ge(sem(f"tree{g}"), 7)
                        for s in range(2):
                            for h in range(4):
                                last = mm(banks[s][:, h * P:(h + 1) * P], H["K"][s][:, h, s * P:(s + 1) * P],
                                          H["Q"][s][:, h, (1 - s) * P:(2 - s) * P], start=True, stop=True)
                    last.then_inc(sem(f"lv_mm{g}"), 1)
                if kind == "pv":
                    pe.wait_ge(sem(f"lv_copy{g}"), 4)
                    for h in range(4):
                        for s in range(2):
                            hh = 4 * g + h
                            if h == 0 and s == 0:
                                for uu in (U_ZI + 1, U_ZI + 3):
                                    for v in (uu - 1, uu):
                                        pe.wait_ge(sem(f"evac{v % RING}"), FILLS[v][v % RING] + 1)
                            last = mm(ps[3 + 2 * g + h // 2][:, (h % 2) * T:(h % 2 + 1) * T],
                                      zi[:, s, hh * P:(hh + 1) * P], H["S"][:, s, h, :], start=s == 0, stop=s == 1)
                    last.then_inc(sem(f"pv_mm{g}"), 1)

            for u in range(U_ZU, U_WA):
                if U_ZI <= u < U_GA:
                    if (u - U_ZI) % 2 == 0:
                        token_major(u, 0, between=lambda u=u: [hgrn_pe(*step) for step in steps.get(u, ())])
                        continue
                else:
                    two_tiles(u, 0)
                if u == U_ZU:
                    norm_bc("n1")
                if u == U_Q[0]:
                    spatial_mix(0)
                    spatial_mix(1)
                for step in steps.get(u, ()):
                    hgrn_pe(*step)
                if u == U_GB:
                    for g in range(2):
                        pe.wait_ge(sem(f"o_sq{g}"), 2)
                    for h in range(HEADS):
                        for s in range(2):
                            last = mm(ps[7][:, 2 * h + s:2 * h + s + 1], sqo[h // 4][:, h % 4, s * P:(s + 1) * P],
                                      mean_col(MEAN_HEAD), start=True, stop=True)
                    last.then_inc(sem("norm_stats"), 1)
                if u == U_GB + 1:
                    pe.wait_ge(sem("norm_factors"), before("rx", "o") + 1)
                    for h in range(HEADS):
                        for s in range(2):
                            last = mm(ps[3 + h // 2][:, (h % 2) * T + s * P:(h % 2) * T + (s + 1) * P], rxo[:, 2 * h + s, :],
                                      ident, start=True, stop=True)
                        if h % 2:
                            last.then_inc(sem("norm_bc"), 1)
            for m in range(4):
                two_tiles(U_WA + m, 8, "a" if m == 0 else None)
            for n in range(2):
                u = U_WB + n
                arrived(u)
                if n == 0:
                    pe.wait_ge(sem("act_lo"), before("lo", "b") + 2)
                for m in range(4):
                    for k in range(4):
                        last = mm3(ps[3 + 2 * n + m // 2][:, (m % 2) * T:(m % 2 + 1) * T], u % RING, (4 * m + k) * P, k,
                                   k == 0, k == 3)
                used(last)
            first_unit(U_WOUT, 8, "m")
            for m in range(1, 4):
                two_tiles(U_WOUT + m, 8)
            arrived(U_PLE)
            pe.wait_ge(sem("act_lo"), before("lo", "p") + 1)
            for m in range(DT):
                for k in range(2):
                    last = mm3(ps[3 + m // 2][:, (m % 2) * T:(m % 2 + 1) * T], U_PLE % RING, (2 * m + k) * P, 6 + k, k == 0, k == 1)
                if m == 3:
                    norm_stats("n2", sq2)
            norm_bc("n2")
            used(last)

            def last_down(slot, base, signal):
                for b in range(4):
                    for m in (2 * b, 2 * b + 1):
                        for kk in range(2):
                            last = mm3(ps[3 + b][:, (m % 2) * T:(m % 2 + 1) * T], slot, (8 * kk + m) * P, base + kk,
                                       False, kk == 1, skip=True)
                    if b < 3:
                        last.then_inc(sem(signal), 1)
                    else:
                        used(last)

            def down(slot, base, first):
                for kk in range(2):
                    for m in range(DT):
                        start = first and kk == 0 and m % 2 == 0
                        last = mm3(ps[3 + m // 2][:, (m % 2) * T:(m % 2 + 1) * T], slot, (8 * kk + m) * P, base + kk,
                                   start, False, skip=True)
                return last

            def pair_tiles(u, slot, base):
                for m in range(2):
                    for k in range(8):
                        last = mm3(ps[slot][:, m * T:(m + 1) * T], slot, (8 * m + k) * P, base + k, k == 0, k == 7)
                return last

            first_unit(U_F1, 8, "n3")
            two_tiles(U_F1 + 1, 8)
            norm_stats("n3", sq3)
            s0 = (U_F1 + 2) % RING

            def ffn1_step(j, u, c, first):
                pe.wait_ge(sem("lo_ready"), u + 1)
                if not first:
                    pe.wait_ge(sem("gate_r"), j)
                used(pair_tiles(u, s0, 8))
                pe.wait_ge(sem("lo_ready"), u + 2)
                if first:
                    norm_bc("n3")
                    pe.wait_ge(sem("gate_r"), 1)
                else:
                    pe.wait_ge(sem("hid_y"), j)
                used(pair_tiles(u + 1, (s0 + 1) % RING, 8))
                pe.wait_ge(sem("lo_ready"), u + 3)
                pe.wait_ge(sem("hid_lo"), j)
                if first:
                    pe.wait_ge(sem("ple_copy"), 4)
                used(down((s0 + 2) % RING, 2 * c, first))

            for c in range(2):
                ffn1_step(1 + c, U_F1 + 2 + 3 * c, c, c == 0)
            with pe.Fori(1, (PAIRS1 - 1) // 2) as i:
                for c in range(2):
                    ffn1_step(2 * i + (1 + c), 6 * i + (U_F1 + 2 + 3 * c), c, False)
            arrived(U_PG - 1)
            pe.wait_ge(sem("hid_lo"), PAIRS1)

            last_down((U_PG - 1) % RING, 2 * ((PAIRS1 - 1) % 2), "ff_bank")
            norm_stats("n4", sq2)
            norm_bc("n4")
            for m in range(4):
                if m == 0:
                    first_unit(U_PG, 0, "ff")
                else:
                    two_tiles(U_PG + m, 0)
                if m == 2:
                    pe.wait_ge(sem("rel_in"), 16)
                    pe.wait_ge(sem("oneh_in"), 16)
                    mm(ps[3][0:HEADS, :], rel_s[0:33, 0, 0:HEADS], oneh_s[0:33, 0, :], start=True, stop=True)\
                        .then_inc(sem("bv_mm"), 1)

            def latent_stats():
                pe.wait_ge(sem("c_sq"), 4)
                pe.wait_ge(sem("head_mh"), 1)
                for which, tiles, at, c in ((MEAN_CQ, 6, 0, 0), (MEAN_CKV, 2, 6, 2)):
                    for s in range(2):
                        for k in range(tiles):
                            last = mm(ps[7][:, c + s:c + s + 1], sqc[:, at + k, s * P:(s + 1) * P], mean_col(which),
                                      start=k == 0, stop=k == tiles - 1)
                last.then_inc(sem("norm_stats"), 1)

            def latent_bc():
                pe.wait_ge(sem("norm_factors"), before("rx", "c") + 1)
                for c in range(4):
                    last = mm(ps[7][:, c * P:(c + 1) * P], rxc[:, c, :], ident, start=True, stop=True)
                last.then_inc(sem("norm_bc"), 1)

            def dilated_stats():
                pe.wait_ge(sem("qk_sq"), 4)
                for s in range(2):
                    for j in range(8):
                        c = 2 * j
                        last = mm(ps[7][:, 16 * s:16 * s + 16], sqA[:, j, s * P:(s + 1) * P],
                                  cst_s[:, C_Z64 + 16 - c:C_Z64 + 32 - c], start=j == 0, stop=j == 7)
                last.then_inc(sem("norm_stats"), 1)

            first_unit(U_QA, 8, "n5")
            two_tiles(U_QA + 1, 8)
            norm_stats("n5", sq3)
            two_tiles(U_KA, 8)
            norm_bc("n5")
            two_tiles(U_KA + 1, 8)
            token_major(U_VA, 8, between=dilated_stats)
            pe.wait_ge(sem("norm_factors"), before("rx", "sa") + 1)
            for j in range(4):
                for s in range(2):
                    last = mm(ps[3 + j // 2][:, (j % 2) * T + s * P:(j % 2) * T + (s + 1) * P], kxA[:, s, j * P:(j + 1) * P],
                              ident, start=True, stop=True)
                if j % 2:
                    last.then_inc(sem("norm_bc"), 1)

            def qk(p):
                if p:
                    pe.wait_ge(sem("head_l"), 4 * p)
                else:
                    pe.wait_ge(sem("ka_n"), 2)
                if p == 4:
                    pe.wait_ge(sem("kb_n"), 8)
                    pe.wait_ge(sem("q_rot"), 4)
                for hh in range(2):
                    h = 2 * (p % 4) + hh
                    if p < 4:
                        a = 64 * hh
                        q_, k_ = qa[a:a + 64, h // 2, :], ka[a:a + 64, h // 2, :]
                    else:
                        q_, k_ = qb[0:96, h, :], kb[0:96, h, :]
                    mm(ps[3 + hh][:, 0:P], q_[:, 0:P], k_[:, 0:P], start=True, stop=True)
                    last = mm(ps[3 + hh][:, P:384], q_[:, P:T], k_, start=True, stop=True)
                last.then_inc(sem("head_qk"), 1)

            def turn(p):
                pe.wait_ge(sem("head_p"), 4 * p + 4)
                if p:
                    pe.wait_ge(sem("head_trc"), 2 * p)
                for hh in range(2):
                    for c in range(3):
                        last = nc.tensor.transpose(ps[5 + hh][:, c * P:(c + 1) * P],
                                                   probs[:, 2 * (p % 2) + hh, c * P:(c + 1) * P], ident)
                last.then_inc(sem("head_tr"), 1)

            def pv(p):
                v = va if p < 4 else vb
                pe.wait_ge(sem("head_trc"), 2 * p + 2)
                if p > 4:
                    pe.wait_ge(sem("head_ml"), p - 4)
                elif p:
                    pe.wait_ge(sem("head_mh"), p)
                for hh in range(2):
                    h = 2 * (p % 4) + hh
                    o = ps[7][64 * hh:64 * hh + 64, :]
                    PT = probsT[:, 2 * (p % 2) + hh, :]
                    hv = slice(64 * h, 64 * h + 64)
                    mm(o[:, 0:P], v[:, 0, hv], PT[:, 0:P], start=True, stop=True)
                    mm(o[:, P:T], v[:, 0, hv], PT[:, P:T], start=True, stop=False)
                    last = mm(o[:, P:T], v[:, 1, hv], PT[:, T:384], start=False, stop=True)
                last.then_inc(sem("head_pv"), 1)

            for m in range(4):
                two_tiles(U_CQ + m, 8)
                qk(m)
                if m == 3:
                    latent_stats()
                if m:
                    turn(m - 1)
                if m == 2:
                    pv(0)
            u = U_KR
            arrived(u)
            for b in range(RING):
                bank_free(u, b)
            for k in range(8):
                last = mm3(ps[0][:, 0:T], u % RING, k * P, 8 + k, k == 0, k == 7)
            last.then_inc(sem("kr_mm"), 1)
            latent_bc()
            turn(3)
            pe.wait_ge(sem("norm_bcs"), before("bcs", "c") + 1)
            pv(1)
            pv(2)
            for s in range(2):
                for k in range(2):
                    if s == 0 and k == 0:
                        pe.wait_ge(sem("act_lo"), before("lo", "c") + 4)
                    xs = slice(s * P, (s + 1) * P)
                    wc = slice(1024 + 512 * k, 1536 + 512 * k)
                    mm(ps[1 + s][:, :], xh[:, 6 + k, xs], whi[:, u % RING, wc], start=k == 0, stop=False)
                    mm(ps[1 + s][:, :], xl[:, 6 + k, xs], whi[:, u % RING, wc], start=False, stop=False)
                    last = mm(ps[1 + s][:, :], xh[:, 6 + k, xs], wlo[:, u % RING, wc], start=False, stop=k == 1)
            used(last)
            arrived(U_UK)
            for h in range(HEADS):
                b = (U_UK + h // 2) % RING
                if h % 2 == 0 and h // 2 < 3:
                    pe.wait_ge(sem(f"evac{b}"), FILLS[U_UK][b])
                if h == 6:
                    pe.wait_ge(sem("uk_ev"), 1)
                for k in range(2):
                    last = mm3(ps[b][:, (h % 2) * T:(h % 2 + 1) * T], U_UK % RING, (2 * h + k) * P, 6 + k, k == 0, k == 1)
                if h % 2 and h < 7:
                    last.then_inc(sem("uk_mm"), 1)
            used(last)
            pv(3)
            pe.wait_ge(sem("uk_ev"), 4)
            for n in range(3):
                u = U_UQ + n
                arrived(u)
                for blk in range(16):
                    i = 16 * n + blk
                    h, k = divmod(i, 6)
                    b = (h // 2) % RING
                    if h == 6 and k == 0:
                        pe.wait_ge(sem("uq_ev"), 1)
                    last = mm3(ps[b][:, (h % 2) * T:(h % 2 + 1) * T], u % RING, blk * P, k, k == 0, k == 5)
                    if k == 5 and h % 2 and blk < 15:
                        last.then_inc(sem("uq_mm"), 1)
                used(last)
            pe.wait_ge(sem("uk_ev"), 4)
            pe.wait_ge(sem("head_mh"), 4)
            for s in range(2):
                for h in [*range(8, 16), *range(8)]:
                    if s == 0 and h < 8 and h % 2 == 0:
                        pe.wait_ge(sem("uq_ev"), h // 2 + 1)
                    sq = (sqq if h < 8 else sqk)[0:96, h % 8, s * P:(s + 1) * P]
                    last = mm(ps[7][:, 16 * s:16 * s + 16], sq, cst_s[0:96, C_Z96 + 16 - h:C_Z96 + 32 - h], start=h == 8, stop=h == 7)
            last.then_inc(sem("norm_stats"), 1)

            def wo_half(u, base, banks):
                arrived(u)
                for m in range(4):
                    for k in range(4):
                        last = mm3(ps[banks[m // 2]][:, (m % 2) * T:(m % 2 + 1) * T], u % RING, (4 * m + k) * P, base + k,
                                   k == 0, k == 3)
                used(last)

            pe.wait_ge(sem("out_a_lo"), 1)
            wo_half(U_WO, 8, (5, 6))
            pe.wait_ge(sem("norm_factors"), before("rx", "sb") + 1)
            for h in range(HEADS):
                b = (h // 2) % RING
                if h == 6:
                    pe.wait_ge(sem("kb_n"), 2)
                for s in range(2):
                    last = mm(ps[b][0:96, (h % 2) * T + s * P:(h % 2) * T + (s + 1) * P], kxB[:, 8 * s + h, :], ident, start=True, stop=True)
                if h % 2:
                    last.then_inc(sem("norm_bc"), 1)
            wo_half(U_WO + 1, 8, (3, 4))
            pe.wait_ge(sem("wo_x"), 4)
            qk(4)
            qk(5)

            def wo_part(k):
                if k == 0:
                    arrived(U_WO + 2)
                pe.wait_ge(sem("head_ml"), k + 1)
                for m in range(4):
                    last = mm3(ps[m // 2][:, (m % 2) * T:(m % 2 + 1) * T], (U_WO + 2) % RING, (4 * m + k) * P, 12 + k,
                               k == 0 and m % 2 == 0, k == 3, skip=True)
                return last

            for p in range(4):
                if p < 2:
                    qk(6 + p)
                turn(4 + p)
                if p:
                    pv(3 + p)
                if p >= 2:
                    wo_part(p - 2)
            pv(7)
            wo_part(2)
            used(wo_part(3))
            wo_half(U_WO + 3, 12, (5, 6))

            first_unit(U_F2, 0, "n6")
            def ffn2_step(j, u, s, base, first):
                pe.wait_ge(sem("lo_ready"), u + 1)
                used(pair_tiles(u, s, 0))
                pe.wait_ge(sem("lo_ready"), u + 2)
                pe.wait_ge(sem("hid2_lo"), j)
                used(down((s + 1) % RING, base, first))

            for j in range(1, 4):
                ffn2_step(j, U_F2 + 2 * j - 1, (U_F2 + 2 * j - 1) % RING, 8 + 2 * ((j - 1) % 3), j == 1)
            with pe.Fori(1, (PAIRS2 - 1) // 3 - 1) as i:
                for c in range(3):
                    ffn2_step(3 * i + (1 + c), 6 * i + (U_F2 + 1 + 2 * c), (U_F2 + 1 + 2 * c) % RING, 8 + 2 * c, False)
            for j in range(PAIRS2 - 3, PAIRS2):
                ffn2_step(j, U_F2 + 2 * j - 1, (U_F2 + 2 * j - 1) % RING, 8 + 2 * ((j - 1) % 3), False)
                if j == PAIRS2 - 3:
                    norm_stats("n6", sq3)
                if j == PAIRS2 - 2:
                    norm_bc("n6")
            arrived(UNITS - 1)
            pe.wait_ge(sem("hid2_lo"), PAIRS2)
            last_down((UNITS - 1) % RING, 8 + 2 * ((PAIRS2 - 1) % 3), "out_bank")


def _tiles(v):
    return v.reshape(-1, P).T


def _channel_blocks(m):
    k, n = m.shape[0] // P, m.shape[1] // P
    return m.reshape(k, P, n, P).transpose(1, 2, 0, 3).reshape(P, n * k, P)


def _row_blocks(m):
    k, n = m.shape[0] // P, m.shape[1] // P
    return m.reshape(k, P, n, P).transpose(1, 0, 2, 3).reshape(P, n * k, P)


def _wide(m):
    k = m.shape[0] // P
    return m.reshape(k, P, 512).transpose(1, 0, 2).reshape(P, k * 4, P)


def _weights(a):
    f = lambda n: np.asarray(a[n], np.float32) if a[n].ndim == 2 else np.asarray(a[n][0], np.float32)
    w = f("w_in")
    q, ff, fb, zi, zg, zu, zv, ga, gb = np.split(w, np.cumsum([1024] * 5 + [512] * 2 + [1024]), axis=1)
    parts = [_wide(zv), _channel_blocks(zu)]
    for g in range(2):
        parts += [_channel_blocks(m[:, 512 * g:512 * g + 512]) for m in (q, ff, fb)]
    parts += [_wide(zi[:, 0:512]), _wide(zi[:, 512:])]
    parts += [_channel_blocks(m) for m in (ga, zg, gb, f("w_a"), f("w_b"), f("w_out"), f("w_ple"))]
    gate, up, down = f("w_gate"), f("w_up"), f("w_down")
    pair = lambda m, j: m[:, 256 * j:256 * j + 256]
    for j in range(PAIRS1):
        parts += [_channel_blocks(pair(gate, j)), _channel_blocks(pair(up, j))]
        if j:
            parts.append(_row_blocks(down[256 * (j - 1):256 * j]))
    parts += [_row_blocks(down[256 * (PAIRS1 - 1):]), _channel_blocks(f("w_ple_gate"))]
    w2, uq, ukv = f("w_in_2"), f("w_uq_2"), f("w_ukv_2")
    qa, ka, va, cq, ckv, kr = np.split(w2, np.cumsum([512, 512, 512, 768, 256]), axis=1)
    parts += [_channel_blocks(qa), _channel_blocks(ka), _wide(va), _channel_blocks(cq), _channel_blocks(ckv)]
    swap = np.r_[16:32, 0:16]
    ukv = ukv.reshape(256, HEADS, 128)
    uq = uq.reshape(768, HEADS, 96)
    parts += [_channel_blocks(np.concatenate([kr, kr, kr, kr[:, swap]], axis=1)),
              _wide(ukv[:, :, 64:].reshape(256, 512)), _channel_blocks(ukv.reshape(256, 1024)),
              _channel_blocks(np.concatenate([uq, uq[:, :, 64 + swap]], axis=2).reshape(768, 1024)),
              _channel_blocks(f("w_o_2")[0:512]), _channel_blocks(f("w_o_2")[512:])]
    ff1, ff2 = f("w_ff1_2"), f("w_ff2_2")
    for j in range(PAIRS2):
        parts.append(_channel_blocks(pair(ff1, j)))
        if j:
            parts.append(_row_blocks(ff2[256 * (j - 1):256 * j]))
    parts.append(_row_blocks(ff2[256 * (PAIRS2 - 1):]))
    full = np.concatenate(parts, axis=1).reshape(P, UNITS, UNIT)
    return np.ascontiguousarray(full.transpose(1, 0, 2))


def _params(a):
    v = lambda n: np.asarray(a[n], np.float32).reshape(-1)
    pad = lambda x, at=0: np.concatenate([np.zeros(at, np.float32), x, np.zeros(P - at - len(x), np.float32)])[:, None]
    swap = lambda g: pad(np.concatenate([g[80:96], g[64:80]]), 64)
    qb, kb = v("qnorm_b_g_2"), v("knorm_b_g_2")
    return np.concatenate([
        _tiles(v("norm_mix_pre")), _tiles(v("lb_gamma_fwd")), _tiles(v("lb_gamma_bwd")), _tiles(v("hg_norm")),
        _tiles(v("norm_mix_post")), _tiles(v("norm_ffn_pre")), _tiles(v("norm_ffn_post")), _tiles(v("norm_mix_g_2")),
        _tiles(v("cq_norm_g_2")), _tiles(v("ckv_norm_g_2")), _tiles(v("norm_ffn_g_2")),
        np.tile(v("qnorm_a_g_2"), 2)[:, None], np.tile(v("knorm_a_g_2"), 2)[:, None],
        pad(qb), pad(kb), swap(qb), swap(kb)], axis=1)


def _constants():
    c = np.zeros((P, NCST), np.float32)
    c[:, C_ID:C_ID + P] = np.eye(P)
    c[:64, C_Z64 + 16] = c[64:, C_Z64 + 17] = 1 / 64
    c[:, C_Z96 + 16] = 1 / 96
    for k, n in enumerate((1024, 768, 256, 128)):
        c[:, C_MEAN + k] = 1 / n
    freq = 1.0 / (np.float32(10000.0) ** (np.arange(0, 32, 2, dtype=np.float32) / np.float32(32)))
    c[64:96, C_INVF] = np.tile(freq, 2)
    c[64:80, C_SIGN], c[80:96, C_SIGN] = -1, 1
    return c


def _level_masks():
    i = np.arange(P)
    return np.stack([(i[:, None] >> lv == i[None] >> lv) & (i[:, None] >> lv - 1 != i[None] >> lv - 1)
                     for lv in range(1, 8)], axis=1).astype(np.int32)


def _distances():
    d = np.arange(512) - 127
    safe = np.maximum(d, 1).astype(np.float32)
    large = 16 + (np.log(safe / 16) / np.log(2048 / 16) * 16).astype(np.int64)
    bucket = np.where(d < 16, d, np.minimum(large, 31))
    n = (d <= 128).astype(int) + (d % 4 == 0) + (d % 16 == 0)
    seen = (d >= 0) & (n > 0)
    t = np.zeros((33, 512), np.float32)
    t[bucket[seen], np.flatnonzero(seen)] = 1
    t[32] = np.where(seen, np.log(np.maximum(n, 1)), NEG)
    return t


def kernel(**a):
    import concourse.bacc as bacc
    from concourse.bass_utils import run_bass_kernel_spmd

    f = lambda n: np.asarray(a[n], np.float32)
    causal = np.zeros((P, T), np.float32)
    causal[:, P:] = np.where(np.arange(P)[None] <= np.arange(P)[:, None], 0, NEG)
    arrays = {
        "w": _weights(a),
        "xT": f("x")[0].T.reshape(DT, P, T).transpose(1, 0, 2),
        "pT": f("p")[0, 0].T.reshape(2, P, T).transpose(1, 0, 2),
        "par": _params(a), "cst": _constants(), "lvl": _level_masks(),
        "sgw": f("sg_w")[0].transpose(2, 0, 1),
        "sgb": np.repeat(f("sg_b")[0].reshape(4, 2, P), 64, axis=1).transpose(1, 0, 2),
        "lnr": np.broadcast_to(np.stack([f("sg_ln_g")[0], f("sg_ln_b")[0]])[None], (P, 2, 512)),
        "rel": f("rel_bias_2"), "oneh": _distances(), "maskb": causal,
        "pos": np.asarray(a["positions_2"], np.int32).reshape(1, T),
    }
    arrays = {k: np.ascontiguousarray(v) for k, v in arrays.items()}
    nc = bacc.Bacc("TRN2", target_bir_lowering=False, num_devices=1)
    args = [nc.dram_tensor(k, v.shape, mybir.dt.from_np(v.dtype), kind="ExternalInput").ap() for k, v in arrays.items()]
    out = nc.dram_tensor("out", (P, DT, T), F32, kind="ExternalOutput").ap()
    build_blocks(nc, *args, out)
    r = run_bass_kernel_spmd(nc, [arrays], core_ids=[0]).results[0]["out"]
    return np.ascontiguousarray(r.transpose(2, 1, 0).reshape(1, T, D))
```
